# Optimizing a Trainium2 kernel written in Bass

```python
import jax, jax.numpy as jnp
from jax import lax
import numpy as np

D_MODEL = 4096
BATCH = 1
SEQ = 256
DEPTH = 1

CHUNK = 64
Q_BLOCK = 128
RMS_EPS = 1e-6
L2_EPS = 1e-6

MLA_HEADS = 16
QK_NOPE = 128
QK_ROPE = 64
QK_HEAD = QK_NOPE + QK_ROPE
V_HEAD = 128
Q_LORA = 1024
KV_LORA = 512
ROPE_THETA = 10000.0
MLA_WIDTH = MLA_HEADS * V_HEAD

GDN_HEADS = 16
GDN_DK = 128
GDN_DV = 128
GDN_KEY_WIDTH = GDN_HEADS * GDN_DK
GDN_WIDTH = GDN_HEADS * GDN_DV
GDN_QKV = 2 * GDN_KEY_WIDTH + GDN_WIDTH
CONV_K = 4

N_BRANCH = 2

SPLITS = (Q_LORA, KV_LORA, QK_ROPE, MLA_WIDTH, GDN_QKV, GDN_HEADS, GDN_HEADS, GDN_WIDTH, D_MODEL, D_MODEL)
IN_WIDTH = Q_LORA + KV_LORA + QK_ROPE + MLA_WIDTH + GDN_QKV + 2 * GDN_HEADS + GDN_WIDTH + N_BRANCH * D_MODEL

kernel_name = 'hybrid_mla_gated_deltanet_parallel_block'

def _split_points(sizes):
    pts, acc = [], 0
    for s in sizes[:-1]:
        acc += s
        pts.append(acc)
    return pts

def rmsnorm(x, g):
    xf = x.astype(jnp.float32)
    y = xf * lax.rsqrt(jnp.mean(xf * xf, axis=-1, keepdims=True) + RMS_EPS)
    return (y * g.astype(jnp.float32)).astype(x.dtype)

def l2norm(x):
    xf = x.astype(jnp.float32)
    return xf * lax.rsqrt(jnp.sum(xf * xf, axis=-1, keepdims=True) + L2_EPS)

def rope(x, cos, sin):
    x1, x2 = jnp.split(x, 2, axis=-1)
    return jnp.concatenate([x1 * cos - x2 * sin, x2 * cos + x1 * sin], axis=-1)

def chunk_causal_attention(q, k, v):
    B, S, H, Dq = q.shape
    nb = S // Q_BLOCK
    qb = q.reshape(B, nb, Q_BLOCK, H, Dq).transpose(1, 0, 2, 3, 4)
    key_chunk = jnp.arange(S) // CHUNK
    scale = QK_HEAD ** -0.5

    def one_block(args):
        q_blk, blk = args
        q_chunk = (blk * Q_BLOCK + jnp.arange(Q_BLOCK)) // CHUNK
        s = jnp.einsum('bqhd,bkhd->bhqk', q_blk, k, preferred_element_type=jnp.float32) * scale
        s = jnp.where(key_chunk[None, :] <= q_chunk[:, None], s, -jnp.inf)
        p = jax.nn.softmax(s, axis=-1).astype(v.dtype)
        return jnp.einsum('bhqk,bkhd->bqhd', p, v)

    out = lax.map(one_block, (qb, jnp.arange(nb)))
    return out.transpose(1, 0, 2, 3, 4).reshape(B, S, H, v.shape[-1])

def causal_depthwise_conv(x, w):
    C = x.shape[-1]
    return lax.conv_general_dilated(x, w[:, None, :].astype(x.dtype), window_strides=(1,),
                                    padding=[(CONV_K - 1, 0)], dimension_numbers=('NWC', 'WIO', 'NWC'),
                                    feature_group_count=C)

def gated_delta_rule(q, k, v, g, beta):
    B, S, H, Dk = q.shape
    Dv = v.shape[-1]
    nc = S // CHUNK
    f32 = jnp.float32

    def to_chunks(t):
        t = t.astype(f32)
        return t.reshape(B, nc, CHUNK, H, *t.shape[3:]).swapaxes(2, 3)

    q = to_chunks(q) * (Dk ** -0.5)
    k, v, g, beta = to_chunks(k), to_chunks(v), to_chunks(g), to_chunks(beta)
    gc = jnp.cumsum(g, axis=-1)
    causal = jnp.tril(jnp.ones((CHUNK, CHUNK), dtype=bool))
    strict = jnp.tril(jnp.ones((CHUNK, CHUNK), dtype=bool), -1)
    diff = gc[..., :, None] - gc[..., None, :]
    decay = jnp.where(causal, jnp.exp(jnp.where(causal, diff, 0.0)), 0.0)
    k_beta = k * beta[..., None]
    v_beta = v * beta[..., None]
    low = jnp.where(strict, jnp.einsum('bnhid,bnhjd->bnhij', k_beta, k) * decay, 0.0)
    a = low + jnp.eye(CHUNK, dtype=f32)
    rhs = jnp.concatenate([v_beta, k_beta * jnp.exp(gc)[..., None]], axis=-1)
    sol = lax.linalg.triangular_solve(a, rhs, left_side=True, lower=True)
    u, w = sol[..., :Dv], sol[..., Dv:]
    attn_intra = jnp.einsum('bnhid,bnhjd->bnhij', q, k) * decay
    q_dec = q * jnp.exp(gc)[..., None]
    k_dec = k * jnp.exp(gc[..., -1:] - gc)[..., None]
    g_last = jnp.exp(gc[..., -1])

    def step(state, inp):
        u_c, w_c, a_c, qd_c, kd_c, gl_c = inp
        v_new = u_c - jnp.einsum('bhcd,bhde->bhce', w_c, state)
        o = jnp.einsum('bhcd,bhde->bhce', qd_c, state) + jnp.einsum('bhij,bhje->bhie', a_c, v_new)
        state = state * gl_c[..., None, None] + jnp.einsum('bhcd,bhce->bhde', kd_c, v_new)
        return state, o

    xs = tuple(jnp.moveaxis(t, 1, 0) for t in (u, w, attn_intra, q_dec, k_dec, g_last))
    s0 = jnp.zeros((B, H, Dk, Dv), f32)
    _, o = lax.scan(step, s0, xs)
    return o.transpose(1, 0, 3, 2, 4).reshape(B, S, H, Dv)

def setup_inputs(seed: int = 0) -> dict:
    key = jax.random.key(seed)
    ks = jax.random.split(key, 20)
    f32 = jnp.float32
    nrm = lambda k, shape, fan_in: jax.random.normal(k, shape, f32) * (fan_in ** -0.5)
    x = jax.random.normal(ks[0], (BATCH, SEQ, D_MODEL), f32)
    offset = jax.random.randint(ks[1], (BATCH, 1), 0, 16) * CHUNK
    positions = (offset + jnp.arange(SEQ, dtype=jnp.int32)[None, :]).astype(jnp.int32)
    gain = lambda k, n: 1.0 + 0.02 * jax.random.normal(k, (n,), f32)
    dt = jnp.exp(jax.random.uniform(ks[14], (GDN_HEADS,), f32, np.log(1e-3), np.log(1e-1)))
    return {
        'x': x,
        'positions': positions,
        'w_norm': gain(ks[2], D_MODEL),
        'w_in': nrm(ks[3], (D_MODEL, IN_WIDTH), D_MODEL),
        'b_gate': 0.02 * jax.random.normal(ks[4], (N_BRANCH, D_MODEL), f32),
        'w_q_up': nrm(ks[5], (Q_LORA, MLA_HEADS * QK_HEAD), Q_LORA),
        'w_kv_up': nrm(ks[6], (KV_LORA, MLA_HEADS * (QK_NOPE + V_HEAD)), KV_LORA),
        'g_q_latent': gain(ks[7], Q_LORA),
        'g_kv_latent': gain(ks[8], KV_LORA),
        'g_q_head': gain(ks[9], QK_HEAD),
        'g_k_head': gain(ks[10], QK_HEAD),
        'w_o_mla': nrm(ks[11], (MLA_WIDTH, D_MODEL), MLA_WIDTH),
        'conv_w': nrm(ks[12], (CONV_K, GDN_QKV), CONV_K),
        'a_log': jnp.log(jax.random.uniform(ks[13], (GDN_HEADS,), f32, 1.0, 16.0)),
        'dt_bias': dt + jnp.log(-jnp.expm1(-dt)),
        'g_gdn_out': gain(ks[15], GDN_DV),
        'w_o_gdn': nrm(ks[16], (GDN_WIDTH, D_MODEL), GDN_WIDTH),
        'w_out': nrm(ks[17], (D_MODEL, D_MODEL), D_MODEL),
    }

def reference(x, positions, w_norm, w_in, b_gate, w_q_up, w_kv_up, g_q_latent, g_kv_latent, g_q_head, g_k_head,
              w_o_mla, conv_w, a_log, dt_bias, g_gdn_out, w_o_gdn, w_out):
    B, S, _ = x.shape
    f32 = jnp.float32
    for _layer in range(DEPTH):
        xn = rmsnorm(x, w_norm)
        proj = jnp.einsum('bsd,de->bse', xn, w_in)
        (c_q, c_kv, k_rope, z_mla, qkv_g, b_logit, a_logit, z_gdn, gate_mla, gate_gdn) = jnp.split(
            proj, _split_points(SPLITS), axis=-1)

        q = jnp.einsum('bsr,re->bse', rmsnorm(c_q, g_q_latent), w_q_up).reshape(B, S, MLA_HEADS, QK_HEAD)
        kv = jnp.einsum('bsr,re->bse', rmsnorm(c_kv, g_kv_latent), w_kv_up).reshape(B, S, MLA_HEADS, QK_NOPE + V_HEAD)
        k_nope, v = kv[..., :QK_NOPE], kv[..., QK_NOPE:]
        k = jnp.concatenate([k_nope, jnp.broadcast_to(k_rope[:, :, None, :], (B, S, MLA_HEADS, QK_ROPE))], axis=-1)
        q = rmsnorm(q, g_q_head)
        k = rmsnorm(k, g_k_head)
        inv_freq = ROPE_THETA ** (-jnp.arange(0, QK_ROPE, 2, dtype=f32) / QK_ROPE)
        ang = positions.astype(f32)[..., None] * inv_freq
        cos = jnp.cos(ang)[:, :, None, :].astype(x.dtype)
        sin = jnp.sin(ang)[:, :, None, :].astype(x.dtype)
        q = jnp.concatenate([q[..., :QK_NOPE], rope(q[..., QK_NOPE:], cos, sin)], axis=-1)
        k = jnp.concatenate([k[..., :QK_NOPE], rope(k[..., QK_NOPE:], cos, sin)], axis=-1)
        o_mla = chunk_causal_attention(q, k, v).reshape(B, S, MLA_WIDTH)
        y_mla = jnp.einsum('bse,ed->bsd', o_mla * jax.nn.silu(z_mla), w_o_mla)

        qkv = jax.nn.silu(causal_depthwise_conv(qkv_g, conv_w))
        qg, kg, vg = jnp.split(qkv, [GDN_KEY_WIDTH, 2 * GDN_KEY_WIDTH], axis=-1)
        qg = l2norm(qg.reshape(B, S, GDN_HEADS, GDN_DK))
        kg = l2norm(kg.reshape(B, S, GDN_HEADS, GDN_DK))
        vg = vg.reshape(B, S, GDN_HEADS, GDN_DV)
        beta = jax.nn.sigmoid(b_logit.astype(f32))
        g_log = -jnp.exp(a_log.astype(f32)) * jax.nn.softplus(a_logit.astype(f32) + dt_bias.astype(f32))
        o_gdn = gated_delta_rule(qg, kg, vg, g_log, beta).astype(x.dtype)
        o_gdn = rmsnorm(o_gdn, g_gdn_out).reshape(B, S, GDN_WIDTH) * jax.nn.silu(z_gdn)
        y_gdn = jnp.einsum('bse,ed->bsd', o_gdn, w_o_gdn)

        h = jax.nn.sigmoid(gate_mla + b_gate[0]) * y_mla + jax.nn.sigmoid(gate_gdn + b_gate[1]) * y_gdn
        x = x + jnp.einsum('bsd,de->bse', h, w_out)
    return x


_drawn_inputs = setup_inputs


def setup_inputs(seed=0):
    import zlib

    import numpy as np

    out = dict(_drawn_inputs(seed))
    spreads = {}
    factors = {'w_norm': 5.386,
     'b_gate': 8.0,
     'g_q_latent': 8.0,
     'g_kv_latent': 8.0,
     'g_q_head': 8.0,
     'g_k_head': 8.0,
     'g_gdn_out': 8.0}
    for name, (base, spread) in spreads.items():
        noise = np.random.default_rng([zlib.crc32(name.encode()), seed]).standard_normal(out[name].shape)
        drawn = base * np.exp(spread * noise) if base else spread * noise
        out[name] = __import__('jax').numpy.asarray(drawn.astype(out[name].dtype))
    for name, factor in factors.items():
        out[name] = (out[name] * factor).astype(out[name].dtype)
    return out
```

```python
from contextlib import ExitStack

import numpy as np

import concourse.bass as bass
from concourse import mybir

F32 = mybir.dt.float32
F32R = mybir.dt.float32r
I32 = mybir.dt.int32
ALU = mybir.AluOpType
ACT = mybir.ActivationFunctionType
AX = mybir.AxisListType.X

P = 128
RING = 4
ROWS = 2
COLS = 512
DVE_LEAD = 2
ACT_LEAD = 3
NEG = -1.0e30
CHUNK = 64
LEVELS = (1, 2, 4, 8, 16, 32)

C_IDENT = 0
C_MASK = C_IDENT + P
C_CAUSAL = C_MASK + 3 * P
C_LEVEL = C_CAUSAL + P
C_SAME = C_LEVEL + len(LEVELS) * P
C_HALF = C_SAME + P
C_FREQ = C_HALF + 2 * P
C_EPS = C_FREQ + 32
C_ALL = C_EPS + 2


def shape_constants():
    c = np.zeros((P, C_ALL), np.float32)
    i = np.arange(P)
    c[:, C_IDENT:C_IDENT + P] = np.eye(P)
    for block, at in ((0, C_MASK), (1, C_MASK + P)):
        keys = np.arange((block + 1) * P)
        hidden = (keys[None, :] // CHUNK) > ((block * P + i)[:, None] // CHUNK)
        c[:, at:at + keys.size] = np.where(hidden, NEG, 0.0)
    same = (i[:, None] // CHUNK) == (i[None, :] // CHUNK)
    c[:, C_CAUSAL:C_CAUSAL + P] = same & (i[:, None] <= i[None, :])
    c[:, C_SAME:C_SAME + P] = same
    for n, s in enumerate(LEVELS):
        low = (i[:, None] // (2 * s) == i[None, :] // (2 * s)) & (i[:, None] % (2 * s) >= s) & (i[None, :] % (2 * s) < s)
        c[:, C_LEVEL + n * P:C_LEVEL + (n + 1) * P] = low.T if n == 0 else low
    c[:CHUNK, C_HALF:C_HALF + P] = 1.0
    c[CHUNK:, C_HALF + P:C_HALF + 2 * P] = 1.0
    c[:, C_FREQ:C_FREQ + 32] = (10000.0 ** (-np.arange(0, 64, 2, dtype=np.float32) / np.float32(64))).astype(np.float32)
    c[:, C_EPS] = 1e-6
    c[:, C_EPS + 1] = 1.0
    return c


class Count:

    def __init__(self, sem):
        self.sem, self.base = sem, 0

    def phase(self, names, repeats=1):
        p = Phase(self, names.split(), self.base)
        self.base += len(p.names) * repeats
        return p


class Phase:

    def __init__(self, count, names, base):
        self.names, self.base, self.at = names, base, 0
        assert len(set(names)) == len(names)

    def after(self, name, turn=0):
        return turn * len(self.names) + (self.base + self.names.index(name) + 1)

    def one(self, name):
        assert self.names[self.at] == name, (self.names[self.at], name)
        self.at = (self.at + 1) % len(self.names)
        return 1


class Arena:

    def __init__(self, nc, base, end):
        self.nc, self.at, self.end = nc, base, end

    def take(self, name, shape, dtype=F32):
        n = int(np.prod(shape[1:])) * 4
        t = self.nc.alloc_sbuf_tensor_at(name, shape, dtype, offset=self.at)
        self.at += (n + 31) // 32 * 32
        assert self.at <= self.end, (name, self.at, self.end)
        return t


def hybrid_block(nc, x, positions, w_norm, w_in, b_gate, w_q_up, w_kv_up, g_q_latent, g_kv_latent, g_q_head,
                 g_k_head, w_o_mla, conv_w, a_log, dt_bias, g_gdn_out, w_o_gdn, w_out, consts, out):
    _, S, D = x.shape
    TB = S // P
    RQ, RKV = w_q_up.shape[0], w_kv_up.shape[0]
    H = a_log.shape[0]
    QK = g_q_head.shape[0]
    NOPE, ROPE, DV = P, QK - P, P
    HALF = ROPE // 2
    W = w_o_mla.shape[0]
    TAPS = conv_w.shape[0]
    assert TB == 2 and D == 4096 and H == 16 and QK == 192 and W == H * DV
    O_C = 0
    O_ROPE = RQ + RKV
    O_Z = O_ROPE + ROPE
    O_QKV = O_Z + W
    O_BA = O_QKV + 3 * W
    O_ZG = O_BA + 2 * H
    O_GATE = O_ZG + W
    KD, KQ, KKV, KW = D // P, RQ // P, RKV // P, W // P

    xf = x.rearrange("a s d -> (a s) d")
    outf = out.rearrange("a s d -> (a s) d")
    tok = lambda a: a.rearrange("(t p) n -> p t n", p=P)
    rows = lambda a: a.rearrange("(k p) n -> p k n", p=P)

    z_d = nc.dram_tensor("z_scratch", (S, W), F32).ap()
    q_d = nc.dram_tensor("q_scratch", (S, H * QK), F32).ap()
    kv_d = nc.dram_tensor("kv_scratch", (S, H * 2 * P), F32).ap()
    g_d = nc.dram_tensor("g_scratch", (S + TAPS - 1, 3 * W), F32).ap()
    conv_d = nc.dram_tensor("conv_scratch", (S, H, 3, DV), F32).ap()
    zg_d = nc.dram_tensor("zg_scratch", (S, W), F32).ap()
    gate_d = nc.dram_tensor("gate_scratch", (S, 2 * D), F32).ap()
    row_d = nc.dram_tensor("row_scratch", (2, H, S), F32).ap()
    mix_d = [nc.dram_tensor(f"mix_scratch{i}", (P, H, S), F32).ap() for i in range(4)]

    with ExitStack() as ctx:
        sb = lambda name, shape, dt=F32: ctx.enter_context(nc.sbuf_tensor(name, shape, dt))
        sem = lambda name: ctx.enter_context(nc.semaphore(name))

        xT = [sb("xT_hi", [P, KD, S], F32R), sb("xT_lo", [P, KD, S], F32R)]
        raw = sb("raw_ring", [P, RING, ROWS * COLS])
        whi = sb("hi_ring", [P, RING, ROWS * COLS], F32R)
        wlo = sb("lo_ring", [P, RING, ROWS * COLS], F32R)
        stage = sb("stage", [P, 2, TB, COLS])
        cst = sb("cst", [P, C_ALL])
        misc = sb("misc", [P, TB, ROPE + 2 * H])
        gcol = sb("gcol", [P, KD + KQ + KKV])
        gqk = sb("gqk", [P, 2, QK])
        ggo = sb("ggo", [P, DV])
        trig = sb("trig", [P, 2, TB, HALF])
        ss = sb("ss", [P, 16])
        rs = sb("rs", [P, 16])
        beta = sb("beta", [P, H, TB])
        gc = sb("gc", [P, H, TB])
        egc = sb("egc", [P, H, TB])
        ekd = sb("ekd", [P, H, TB])
        glast = sb("glast", [P, H, 2 * TB])
        slab_base = nc.sbuf_base
        slab_end = nc.sbuf_usable_end
        area = lambda: Arena(nc, slab_base, slab_end)

        a0 = area()
        xin = a0.take("xin", [P, TB, D])
        junk = a0.take("junk", [P, D])
        graw = a0.take("graw", [KD + KQ + KKV, P])
        a1 = area()
        craw = a1.take("craw", [P, TB, RQ + RKV])
        cjunk = a1.take("cjunk", [P, RQ])
        cT = [a1.take("cT_hi", [P, KQ + KKV, S], F32R), a1.take("cT_lo", [P, KQ + KKV, S], F32R)]
        alg = a1.take("alg", [P, 2, H])
        pos_i = a1.take("pos_i", [P, TB], I32)
        pos_f = a1.take("pos_f", [P, TB])
        ang = a1.take("ang", [P, 2, TB, HALF])
        whole = a1.take("whole_turns", [P, 2, TB, HALF])
        av = a1.take("av", [P, 4, TB, H])
        gth = a1.take("gth", [P, 2, TB, H])
        gcT = a1.take("gcT", [H, 2, S])
        zrow = a1.take("zrow", [72, 256])

        ab = area()
        qk = ab.take("qk", [P, 2, TB, 2, QK])
        vt = ab.take("vt", [P, TB, 2, DV])
        zs = ab.take("zs", [P, TB, 2, DV])
        sq = ab.take("sq", [P, 2, TB, 2, QK])
        qkTa = ab.take("qkTa", [P, 2, 2, TB * P])
        qkTb = ab.take("qkTb", [ROPE, 2, 2, TB * P])
        sc = ab.take("sc", [P, 2, 3 * P])
        pT = ab.take("pT", [P, 2, 3 * P])
        og = ab.take("og", [P, TB, 2, DV])
        rt = ab.take("rt", [P, 4, 4 * TB, HALF])
        mx = ab.take("mx", [P, 3, TB, 2])
        xs = ab.take("xs", [P, TAPS, TB, COLS])
        cw = ab.take("cw", [P, TAPS, COLS])
        mT = [ab.take("mT_hi", [P, 2, S], F32R), ab.take("mT_lo", [P, 2, S], F32R)]

        ac = area()
        cv = ac.take("cv", [P, TB, 2, 3, DV])
        sl = ac.take("sl", [P, 2 * TB, 4, DV])
        tt = ac.take("tt", [P, 2 * TB, 2, P])
        wT = ac.take("wT", [P, 2 * TB, DV])
        kbe = ac.take("kbe", [P, 2 * TB, DV])
        kd = ac.take("kd", [P, 2 * TB, DV])
        rowb = ac.take("rowb", [P, 2, 2 * TB, P])
        erow = ac.take("erow", [P, 2 * TB, P])
        pq = ac.take("pq", [P, 2 * TB, 2, P])
        qeT = ac.take("qeT", [P, 2 * TB, 3, P])
        dec = ac.take("dec", [P, 2 * TB, P])
        lt = ac.take("lt", [P, 2 * TB, P])
        m1 = ac.take("m1", [P, 2 * TB, P])
        st = ac.take("st", [P, 2, 2, DV])
        bb = ac.take("bb", [P, 2, COLS])
        cf = ac.take("cf", [P, 8, 2 * TB])
        gT = [ac.take("gT_hi", [P, 2, S], F32R), ac.take("gT_lo", [P, 2, S], F32R)]

        ad = area()
        oT = [ad.take(f"oT{i}", [P, H, S], F32R) for i in range(3)]
        hb = ad.take("hb", [P, TB, COLS])
        ad.at = max(ad.at, ac.at)
        oT.insert(0, ad.take("oT3", [P, H, S], F32R))
        ae = area()
        xr = ae.take("xr", [P, 2, TB, COLS])

        acc = [ctx.enter_context(nc.psum_tensor(f"acc{i}", [P, TB, COLS], F32)) for i in range(2)]
        side = ctx.enter_context(nc.psum_tensor("side", [P, 4, COLS], F32))

        ident = cst[:, C_IDENT:C_IDENT + P]
        causal = cst[:, C_CAUSAL:C_CAUSAL + P]
        level = lambda n: cst[:, C_LEVEL + n * P:C_LEVEL + (n + 1) * P]
        eps = cst[:, C_EPS:C_EPS + 1]
        one = cst[:, C_EPS + 1:C_EPS + 2]

        landed = [sem(f"raw_landed{i}") for i in range(RING)]
        hi_done = sem("hi_done")
        lo_done = sem("lo_done")
        tile_used = sem("tile_used")
        emptied = [sem(f"acc_emptied{i}") for i in range(2)]
        gated = [sem(f"acc_gated{i}") for i in range(2)]
        summed = [sem(f"acc_summed{i}") for i in range(2)]
        stored = [sem(f"stage_stored{i}") for i in range(2)]
        s_const = sem("consts_landed")
        s_x = [sem(f"x_landed{i}") for i in range(TB)]
        s_gain = sem("gains_landed")
        s_bc = sem("rows_landed")
        s_row = sem("scalar_rows_landed")
        s_zero = sem("zero_rows_stored")
        s_gc = sem("gc_stored")
        s_mix = [sem(f"mix_stored{i}") for i in range(4)]
        s_qk = sem("qk_loaded")
        s_v = sem("v_loaded")
        s_zs = sem("zs_loaded")
        s_tap = sem("taps_loaded")
        s_conv = sem("conv_stored")
        s_cv = sem("conv_loaded")
        s_zg = sem("zg_loaded")
        s_gcb = sem("gc_rows_loaded")
        s_bb = sem("gate_bias_loaded")
        s_oT = [sem(f"mix_loaded{i}") for i in range(4)]
        s_gate = [sem(f"gate_loaded{i}") for i in range(2)]
        s_xr = [sem(f"residual_loaded{i}") for i in range(2)]
        s_out = [sem(f"out_stored{i}") for i in range(2)]
        pe_done, act_done, dve_done, pool_done = sem("pe_done"), sem("act_done"), sem("dve_done"), sem("pool_done")
        cp, ca, cd, cg = Count(pe_done), Count(act_done), Count(dve_done), Count(pool_done)

        NG = KD // 2
        NC = (KQ + KKV) // 2
        seq = lambda name, n: " ".join(f"{name}{i}" for i in range(n))
        P0 = cp.phase("gains " + seq("x", NG))
        A0 = ca.phase("sumsq0 sumsq1 ln rstd " + seq("hi", NG))
        D0 = cd.phase("norm0 norm1 gcol " + seq("lo", NG))
        P1 = cp.phase("cum gct " + seq("c", NC))
        A1 = ca.phase("sumsq0 sumsq1 sumsq2 sumsq3 lnq lnkv rstd beta expa expx lnx sin egc ekd glast " + seq("hi", NC))
        D1 = cd.phase("norm0 norm1 norm2 norm3 pos ang0 ang1 u0 u1 r0 r1 s1 s2 s3 s4 s5 adt nabs sp g "
                      "gc gth gth2 kdx gct " + seq("lo", NC))
        G1 = cg.phase("zero")
        TURNS = H // 2
        PB = cp.phase("heads scores probs values turn", TURNS)
        AB = ca.phase("rope sq ln rstd headsT expA expB expC expD probsT hi", TURNS)
        DB = cd.phase("sum unit gain r1 r2 r3 r4 r5 r6 ropeT mask max0 max1 neg rden div gate lo", TURNS)
        lv = range(1, len(LEVELS))
        PC = cp.phase("turns products t1 " + " ".join(f"ma{n} mb{n}" for n in lv) +
                      " solve kv0 ws1 kv1 ws2 kv2 ws3 out1 turn", TURNS)
        AC = ca.phase("silu square exp ln rstd erow kT " + " ".join(f"tT{n}" for n in lv if n > 1) +
                      " wT osq oln orstd hi", TURNS)
        DZ = cd.phase("zero")
        DC = cd.phase("sum cq kn qn cke kbe qeT qT lt attn l1 tt1 t1 " +
                      " ".join(f"ma{n} mb{n}" for n in lv) +
                      " u s1 v1 s2a s2b v2 s3a s3b v3 osum on ogate lo", TURNS)
        GB = cg.phase("m0 m1 m2 m3 a1 a2 a3", 12)
        GC = cg.phase("diff below mask decb vb kd gz", TURNS)
        PD = cp.phase("turn", TURNS)
        AD = ca.phase("hi", TURNS)
        DD = cd.phase("h3 lo", TURNS)

        T_MISC = 3 * KD // ROWS
        T_Z = T_MISC + RING
        T_Q = T_Z + (W // COLS) * KD // ROWS
        T_KV = T_Q + (H * QK // COLS) * KQ // ROWS
        T_B = T_KV + (H * 2 * P // COLS) * KKV // ROWS
        T_ZG = T_B + 12 * KD // ROWS
        T_C = T_ZG + (W // COLS) * KD // ROWS
        T_D = T_C + 16 * KD // ROWS
        T_E = T_D + 8 * 2 * KW // ROWS
        T_END = T_E + 8 * KD // ROWS
        MK = KD // RING
        MN = ROPE + 2 * H

        def landed_value(turn, t0, s):
            return turn * 16 + (16 * ((t0 + s) // RING + 1) + (16 if t0 >= T_MISC else 0))

        def width(t):
            return MK * MN if T_MISC <= t < T_Z else ROWS * COLS

        block = ctx.enter_context(nc.Block())

        @block.sync
        def _(sp):
            sp.dma_start(cst[:], consts).then_inc(s_const, 16)

            def load(t0, turn, per, s, src):
                if not (isinstance(turn, int) and t0 + turn * per + s < RING):
                    sp.wait_ge(lo_done, turn * per + (t0 + s - RING + 1))
                for dst, a in src:
                    sp.dma_start(dst, a).then_inc(landed[s % RING], 16)

            def tile(w, k0, col, s):
                return [(raw[:, s % RING, :].rearrange("p (k n) -> p k n", k=ROWS),
                         rows(w)[:, k0:k0 + ROWS, bass.ds(col, COLS)])]

            def chunks(t0, n, w, col0, kn, per_turn=2):
                per = per_turn * kn // ROWS
                with sp.Fori(0, n // per_turn) as i:
                    for c in range(per_turn):
                        for k in range(kn // ROWS):
                            s = c * (kn // ROWS) + k
                            load(t0, i, per, s, tile(w, k * ROWS, i * (per_turn * COLS) + (col0 + c * COLS), s))

            KT = KD // ROWS
            for s in range(KT):
                load(0, 0, KT, s, tile(w_in, s * ROWS, O_C, s))
            with sp.Fori(1, 3) as i:
                for s in range(KT):
                    load(0, i, KT, s, tile(w_in, s * ROWS, i * COLS + O_C, s))
            for s in range(RING):
                dst = raw[:, s, 0:MK * MN].rearrange("p (k n) -> p k n", k=MK)
                src = rows(w_in)[:, s * MK:(s + 1) * MK, :]
                load(T_MISC, 0, RING, s, [(dst[:, :, 0:ROPE], src[:, :, O_ROPE:O_ROPE + ROPE]),
                                          (dst[:, :, ROPE:MN], src[:, :, O_BA:O_BA + 2 * H])])
            chunks(T_Z, W // COLS, w_in, O_Z, KD)
            chunks(T_Q, H * QK // COLS, w_q_up, 0, KQ)
            chunks(T_KV, H * 2 * P // COLS, w_kv_up, 0, KKV)
            with sp.Fori(0, 4) as i:
                for s in range(3 * KT):
                    load(T_B, i, 3 * KT, s, tile(w_in, (s % KT) * ROWS, i * COLS + (O_QKV + (s // KT) * W), s))
                    if s % 24 == 6:
                        half = s // 24
                        for q in stored:
                            sp.wait_ge(q, 16 * 10)
                        sp.wait_ge(pe_done, PB.after("heads", i * 2 + (half - 1)))
                        sp.dma_start(qk[:, 0].rearrange("p t h n -> p t (h n)"),
                                     tok(q_d)[:, :, bass.ds(i * (4 * QK) + half * 2 * QK, 2 * QK)]).then_inc(s_qk, 16)
                        for h in range(2):
                            sp.dma_start(qk[:, 1, :, h, 0:NOPE],
                                         tok(kv_d)[:, :, bass.ds(i * (8 * P) + (half * 4 + h * 2) * P, P)]).then_inc(s_qk, 16)
                        sp.wait_ge(dve_done, DB.after("gate", i * 2 + (half - 1)))
                        for h in range(2):
                            sp.dma_start(vt[:, :, h, :],
                                         tok(kv_d)[:, :, bass.ds(i * (8 * P) + (half * 4 + h * 2 + 1) * P, P)]).then_inc(s_v, 16)
                        sp.dma_start(zs[:].rearrange("p t h n -> p t (h n)"),
                                     tok(z_d)[:, :, bass.ds(i * (4 * DV) + half * 2 * DV, 2 * DV)]).then_inc(s_zs, 16)
            chunks(T_ZG, W // COLS, w_in, O_ZG, KD)
            with sp.Fori(0, TURNS) as i:
                for s in range(2 * KT):
                    load(T_C, i, 2 * KT, s, tile(w_in, (s % KT) * ROWS, i * (2 * COLS) + (O_GATE + (s // KT) * COLS), s))
                    if s == 0:
                        sp.wait_ge(s_conv, 16 * 2 * 12)
                        for q in s_mix[0:2]:
                            sp.wait_ge(q, 16 * (TURNS + 1))
                        sp.wait_ge(act_done, AC.after("silu", i - 1))
                        sp.dma_start(cv[:].rearrange("p t h j n -> p t (h j n)"),
                                     conv_d.rearrange("(t p) h j n -> p t (h j n)", p=P)
                                     [:, :, bass.ds(i * (6 * DV), 6 * DV)]).then_inc(s_cv, 16)
                        sp.wait_ge(act_done, AC.after("erow", i - 1))
                        sp.wait_ge(pool_done, GC.after("decb", i - 1))
                        sp.dma_start(rowb[:].rearrange("p a b n -> p a (b n)"),
                                     row_d[:, bass.ds(i * 2, 2), :].rearrange("a h s -> a (h s)").partition_broadcast(P)).then_inc(s_gcb, 16)
                    if s == 8:
                        sp.wait_ge(stored[0], 16 * 20)
                        sp.wait_ge(stored[1], 16 * 16)
                        sp.wait_ge(pe_done, PC.after("turn", i - 1))
                        for h in range(2):
                            sp.dma_start(sl[:, h * TB:(h + 1) * TB, 3, :],
                                         tok(zg_d)[:, :, bass.ds(i * (2 * DV) + h * DV, DV)]).then_inc(s_zg, 16)
                        sp.dma_start(bb[:].rearrange("p a n -> p (a n)"),
                                     b_gate.rearrange("a n -> (a n)")[bass.ds(i * (2 * COLS), 2 * COLS)]
                                     .partition_broadcast(P)).then_inc(s_bb, 16)
            with sp.Fori(0, TURNS) as i:
                for s in range(2 * KW // ROWS):
                    w, k = (w_o_mla, s) if s < KW // ROWS else (w_o_gdn, s - KW // ROWS)
                    load(T_D, i, 2 * KW // ROWS, s, tile(w, k * ROWS, i * COLS, s))
            chunks(T_E, 8, w_out, 0, KD)

        @block.tensor
        def _(pe):
            def tiles(t0, turn, per, s0, s1, c, left, kn, n=COLS, kts=ROWS, k_at=0):
                for s in range(s0, s1):
                    pe.wait_ge(lo_done, turn * per + (t0 + s + 1))
                    for kk in range(kts):
                        k = (s * kts + kk) % kn
                        for tb in range(TB):
                            o = acc[c][:, tb, 0:n]
                            lh = left[0][:, k_at + k, tb * P:(tb + 1) * P]
                            ll = left[1][:, k_at + k, tb * P:(tb + 1) * P]
                            rh = whi[:, s % RING, kk * n:(kk + 1) * n]
                            rl = wlo[:, s % RING, kk * n:(kk + 1) * n]
                            nc.tensor.matmul(o, lh, rh, start=(k == 0), stop=False)
                            nc.tensor.matmul(o, lh, rl, start=False, stop=False)
                            last = nc.tensor.matmul(o, ll, rh, start=False, stop=(k == kn - 1))
                    last.then_inc(tile_used, 1)

            def turn_groups(src, kb0, n, names, phase, lo_phase, deps):
                for g in range(n):
                    if g >= 4:
                        pe.wait_ge(dve_done, lo_phase.after(f"lo{g - 4}"))
                    for kk in range(2):
                        for tb in range(TB):
                            k = kb0 + 2 * g + kk
                            mm = nc.tensor.transpose(side[:, g % 4, kk * S + tb * P:kk * S + (tb + 1) * P],
                                                     src[:, tb, k * P:(k + 1) * P], ident)
                    mm.then_inc(pe_done, phase.one(f"{names}{g}"))

            pe.sem_inc(tile_used, 1)
            pe.wait_ge(s_const, 16)
            pe.wait_ge(s_gain, 48)
            NR = KD + KQ + KKV
            nc.tensor.transpose(acc[0][:, 0, 0:NR], graw[:, :], cst[0:NR, C_IDENT:C_IDENT + NR]).then_inc(pe_done, P0.one("gains"))
            pe.wait_ge(dve_done, D0.after("norm1"))
            turn_groups(xin, 0, NG, "x", P0, D0, None)
            pe.wait_ge(dve_done, D0.after(f"lo{NG - 1}"))
            KT = KD // ROWS
            with pe.Fori(0, 3) as i:
                pe.wait_ge(emptied[0], i + 1)
                tiles(0, i, KT, 0, KT, 0, xT, KD)
            tiles(T_MISC, 0, RING, 0, RING, 1, xT, KD, MN, MK)

            def plain(t0, n, left, kn, seen0, seen1, k_at=0):
                per = 2 * kn // ROWS
                with pe.Fori(0, n // 2) as i:
                    pe.wait_ge(emptied[0], i + (seen0 + 1))
                    tiles(t0, i, per, 0, per // 2, 0, left, kn, k_at=k_at)
                    pe.wait_ge(emptied[1], i + (seen1 + 1))
                    tiles(t0, i, per, per // 2, per, 1, left, kn, k_at=k_at)

            plain(T_Z, 4, xT, KD, 3, 1)
            pe.wait_ge(dve_done, D1.after("g"))
            for tb in range(TB):
                g = av[:, 3, tb, :]
                nc.tensor.matmul(side[:, 0, tb * H:(tb + 1) * H], causal, g, start=True, stop=True)
                nc.tensor.matmul(side[:, 0, (2 + tb) * H:(3 + tb) * H], cst[:, C_SAME:C_SAME + P], g, start=True, stop=True)
                for c in range(2):
                    mm = nc.tensor.matmul(side[:, 0, (4 + 2 * tb + c) * H:(5 + 2 * tb + c) * H],
                                          cst[:, C_HALF + c * P:C_HALF + (c + 1) * P], g, start=True, stop=True)
            mm.then_inc(pe_done, P1.one("cum"))
            pe.wait_ge(dve_done, D1.after("gth2"))
            for a in range(2):
                for tb in range(TB):
                    mm = nc.tensor.transpose(side[0:H, 1, a * S + tb * P:a * S + (tb + 1) * P], gth[:, a, tb, :], ident)
            mm.then_inc(pe_done, P1.one("gct"))
            pe.wait_ge(dve_done, D1.after("gct"))
            pe.wait_ge(act_done, A1.after("glast"))
            turn_groups(craw, 0, NC, "c", P1, D1, None)
            pe.wait_ge(dve_done, D1.after(f"lo{NC - 1}"))
            plain(T_Q, 6, cT, KQ, 5, 3)
            plain(T_KV, 8, cT, KKV, 8, 6, k_at=KQ)

            def attend(i, half, B):
                turn = i * 2 + half
                B(0, 10)
                pe.wait_ge(dve_done, DB.after("r6", turn))
                for s in range(2):
                    for h in range(2):
                        for tb in range(TB):
                            n = ((s * 2 + h) * TB + tb) * P
                            nc.tensor.transpose(side[:, n // COLS, n % COLS:n % COLS + P], qk[:, s, tb, h, 0:NOPE], ident)
                            mm = nc.tensor.transpose(side[0:ROPE, 2 + n // COLS, n % COLS:n % COLS + P],
                                                     qk[:, s, tb, h, NOPE:QK], ident)
                mm.then_inc(pe_done, PB.one("heads"))
                B(10, 12)
                pe.wait_ge(act_done, AB.after("headsT", turn))
                pe.wait_ge(dve_done, DB.after("ropeT", turn))
                for h in range(2):
                    for tb in range(TB):
                        o = side[:, h, tb * P:tb * P + (tb + 1) * P]
                        nc.tensor.matmul(o, qkTa[:, 0, h, tb * P:(tb + 1) * P], qkTa[:, 1, h, 0:(tb + 1) * P], start=True, stop=False)
                        mm = nc.tensor.matmul(o, qkTb[:, 0, h, tb * P:(tb + 1) * P], qkTb[:, 1, h, 0:(tb + 1) * P], start=False, stop=True)
                mm.then_inc(pe_done, PB.one("scores"))
                B(12, 15)
                pe.wait_ge(act_done, AB.after("expD", turn))
                for h in range(2):
                    for b in range(3):
                        mm = nc.tensor.transpose(side[:, 2 + h, b * P:(b + 1) * P], sc[:, h, b * P:(b + 1) * P], ident)
                mm.then_inc(pe_done, PB.one("probs"))
                B(15, 17)
                pe.wait_ge(act_done, AB.after("probsT", turn))
                pe.wait_ge(s_v, i * 64 + (half * 32 + 32))
                for tb in range(TB):
                    for h in range(2):
                        for kb_ in range(tb + 1):
                            mm = nc.tensor.matmul(side[:, 0, (tb * 2 + h) * P:(tb * 2 + h + 1) * P],
                                                  pT[:, h, (tb + kb_) * P:(tb + kb_ + 1) * P], vt[:, kb_, h, :],
                                                  start=(kb_ == 0), stop=(kb_ == tb))
                mm.then_inc(pe_done, PB.one("values"))
                B(17, 19)
                pe.wait_ge(dve_done, DB.after("gate", turn))
                for h in range(2):
                    for tb in range(TB):
                        mm = nc.tensor.transpose(side[:, 1, h * S + tb * P:h * S + (tb + 1) * P], og[:, tb, h, :], ident)
                mm.then_inc(pe_done, PB.one("turn"))
                B(19, 24)

            with pe.Fori(0, 4) as i:
                def B(half, s0, s1):
                    for s in range(24 * half + s0, 24 * half + s1):
                        if s == 0:
                            pe.wait_ge(emptied[0], i * 2 + 13)
                        if s == KT:
                            pe.wait_ge(emptied[1], i + 11)
                        if s == 2 * KT:
                            pe.wait_ge(emptied[0], i * 2 + 14)
                        tiles(T_B, i, 3 * KT, s, s + 1, (s // KT) % 2, xT, KD)
                attend(i, 0, lambda a, b: B(0, a, b))
                attend(i, 1, lambda a, b: B(1, a, b))
            plain(T_ZG, W // COLS, xT, KD, 20, 14)


            pe.wait_ge(emptied[0], 23)
            pe.wait_ge(emptied[1], 17)
            pe.wait_ge(dve_done, DB.after("lo", TURNS - 1))
            with pe.Fori(0, TURNS) as i:
                C = lambda s: tiles(T_C, i, 2 * KT, s, s + 1, s // KT, xT, KD)
                col = lambda n: side[:, n // COLS, n % COLS:n % COLS + P]
                hb4 = range(2 * TB)
                pe.wait_ge(gated[0], i + 1)
                for s in range(4):
                    C(s)
                pe.wait_ge(dve_done, DC.after("qn", i))
                for n in range(2):
                    for b in hb4:
                        mm = nc.tensor.transpose(side[:, 2 + n, b * P:(b + 1) * P], sl[:, b, 1 - n, :], ident)
                mm.then_inc(pe_done, PC.one("turns"))
                C(4)
                C(5)
                pe.wait_ge(act_done, AC.after("kT", i))
                pe.wait_ge(dve_done, DC.after("qT", i))
                for b in hb4:
                    mm = nc.tensor.matmul(side[:, b // 2, (b % 2) * 2 * P:(b % 2 + 1) * 2 * P], pq[:, b, 0, :],
                                          pq[:, b].rearrange("p a n -> p (a n)"), start=True, stop=True)
                mm.then_inc(pe_done, PC.one("products"))
                C(6)
                C(7)
                pe.wait_ge(dve_done, DC.after("tt1", i))
                for b in hb4:
                    mm = nc.tensor.transpose(side[:, 2, b * P:(b + 1) * P], tt[:, b, 1, :], ident)
                mm.then_inc(pe_done, PC.one("t1"))
                s = 8
                before = "t1"
                for n in lv:
                    C(s)
                    pe.wait_ge(dve_done, DC.after(before, i))
                    for b in hb4:
                        mm = nc.tensor.matmul(side[:, 3, b * P:(b + 1) * P], lt[:, b, :], tt[:, b, 0, :], start=True, stop=True)
                    if n > 1:
                        for b in hb4:
                            mm = nc.tensor.transpose(side[:, 2, b * P:(b + 1) * P], tt[:, b, 0, :], ident)
                    mm.then_inc(pe_done, PC.one(f"ma{n}"))
                    C(s + 1)
                    pe.wait_ge(dve_done, DC.after(f"ma{n}", i))
                    if n > 1:
                        pe.wait_ge(act_done, AC.after(f"tT{n}", i))
                    for b in hb4:
                        if n < len(LEVELS) - 1:
                            left, right = tt[:, b, 1, :], m1[:, b, :]
                        else:
                            left, right = m1[:, b, :], tt[:, b, 1, :]
                        mm = nc.tensor.matmul(side[:, 0, b * P:(b + 1) * P], left, right, start=True, stop=True)
                    mm.then_inc(pe_done, PC.one(f"mb{n}"))
                    s += 2
                    before = f"mb{n}"
                    if s == KT:
                        pe.wait_ge(gated[1], i + 1)
                C(18)
                pe.wait_ge(dve_done, DC.after(before, i))
                pe.wait_ge(pool_done, GC.after("vb", i))
                for b in hb4:
                    nc.tensor.matmul(side[:, 2, b * P:(b + 1) * P], tt[:, b, 1, :], sl[:, b, 2, :], start=True, stop=True)
                    mm = nc.tensor.matmul(side[:, 3, b * P:(b + 1) * P], kbe[:, b, :], tt[:, b, 1, :], start=True, stop=True)
                mm.then_inc(pe_done, PC.one("solve"))

                def state_add(c, name):
                    r = slice((c % 2) * CHUNK, (c % 2 + 1) * CHUNK)
                    for h in range(2):
                        b = h * TB + c // 2
                        mm = nc.tensor.matmul(side[:, 1, h * P:(h + 1) * P], kd[r, b, :], sl[r, b, 2, :], start=True, stop=True)
                    return mm

                def from_state(c, name):
                    for h in range(2):
                        b = h * TB + c // 2
                        mm = nc.tensor.matmul(side[:, 0, h * P:(h + 1) * P], wT[:, b, :], st[:, c % 2, h, :], start=True, stop=True)
                    mm.then_inc(pe_done, PC.one(name))

                def block_out(tb):
                    for h in range(2):
                        b = h * TB + tb
                        o = side[:, 2, (tb * 2 + h) * P:(tb * 2 + h + 1) * P]
                        cs = [c for c in (2 * tb, 2 * tb + 1) if c > 0]
                        flat = qeT[:, b].rearrange("p a n -> p (a n)")
                        for c in cs:
                            nc.tensor.matmul(o, flat[:, (c % 2) * P:(c % 2) * P + P], st[:, c % 2, h, :], start=(c == cs[0]), stop=False)
                        mm = nc.tensor.matmul(o, dec[:, b, :], sl[:, b, 2, :], start=False, stop=True)
                    return mm

                C(19)
                pe.wait_ge(dve_done, DC.after("u", i))
                pe.wait_ge(pool_done, GC.after("kd", i))
                state_add(0, "kv0").then_inc(pe_done, PC.one("kv0"))
                C(20)
                pe.wait_ge(act_done, AC.after("wT", i))
                pe.wait_ge(dve_done, DC.after("s1", i))
                from_state(1, "ws1")
                C(21)
                pe.wait_ge(dve_done, DC.after("v1", i))
                block_out(0)
                state_add(1, "kv1").then_inc(pe_done, PC.one("kv1"))
                C(22)
                pe.wait_ge(dve_done, DC.after("s2b", i))
                from_state(2, "ws2")
                C(23)
                pe.wait_ge(dve_done, DC.after("v2", i))
                state_add(2, "kv2").then_inc(pe_done, PC.one("kv2"))
                C(24)
                pe.wait_ge(dve_done, DC.after("s3b", i))
                from_state(3, "ws3")
                C(25)
                pe.wait_ge(dve_done, DC.after("v3", i))
                block_out(1).then_inc(pe_done, PC.one("out1"))
                for s in range(26, 29):
                    C(s)
                pe.wait_ge(dve_done, DC.after("ogate", i))
                for h in range(2):
                    for tb in range(TB):
                        mm = nc.tensor.transpose(side[:, 3, h * S + tb * P:h * S + (tb + 1) * P], sl[:, h * TB + tb, 3, :], ident)
                mm.then_inc(pe_done, PC.one("turn"))
                for s in range(29, 32):
                    C(s)

            KO = KW // ROWS

            def turn_h(i_prev):
                pe.wait_ge(dve_done, DD.after("h3", i_prev))
                for k in range(4):
                    for tb in range(TB):
                        mm = nc.tensor.transpose(side[:, k // 2, (k % 2) * S + tb * P:(k % 2) * S + (tb + 1) * P],
                                                 hb[:, tb, k * P:(k + 1) * P], ident)
                mm.then_inc(pe_done, PD.one("turn"))

            for q in s_oT[0:2]:
                pe.wait_ge(q, 16)
            pe.wait_ge(gated[0], TURNS + 1)
            tiles(T_D, 0, 2 * KO, 0, KO, 0, oT[0:2], KW)
            for q in s_oT[2:4]:
                pe.wait_ge(q, 16)
            pe.wait_ge(gated[1], TURNS + 1)
            tiles(T_D, 0, 2 * KO, KO, 2 * KO, 1, oT[2:4], KW)
            with pe.Fori(1, TURNS) as i:
                pe.wait_ge(gated[0], i + (TURNS + 1))
                tiles(T_D, i, 2 * KO, 0, 3, 0, oT[0:2], KW)
                turn_h(i - 1)
                tiles(T_D, i, 2 * KO, 3, KO, 0, oT[0:2], KW)
                pe.wait_ge(gated[1], i + (TURNS + 1))
                tiles(T_D, i, 2 * KO, KO, 2 * KO, 1, oT[2:4], KW)
            turn_h(TURNS - 1)
            pe.wait_ge(dve_done, DD.after("lo", TURNS - 1))
            with pe.Fori(0, 4) as i:
                pe.wait_ge(summed[0], i + 1)
                tiles(T_E, i, 2 * KT, 0, KT, 0, xT, KD)
                pe.wait_ge(summed[1], i + 1)
                tiles(T_E, i, 2 * KT, KT, 2 * KT, 1, xT, KD)

        @block.scalar
        def _(act):
            def hi(t0, turn, per, s):
                act.wait_ge(landed[s % RING], landed_value(turn * (per // RING), t0, s))
                if not (isinstance(turn, int) and t0 + turn * per + s < RING):
                    act.wait_ge(tile_used, turn * per + (t0 + s - RING + 2))
                w = width(t0 + s)
                nc.scalar.copy(whi[:, s % RING, 0:w], raw[:, s % RING, 0:w]).then_inc(hi_done, 1)

            def rsqrt(dst, src, n, phase, ln, rstd, i=0):
                nc.scalar.activation(dst, src, ACT.Ln, bias=eps, scale=1.0 / n).then_inc(act_done, phase.one(ln))
                act.wait_ge(act_done, phase.after(ln, i))
                nc.scalar.activation(dst, dst, ACT.Exp, scale=-0.5).then_inc(act_done, phase.one(rstd))

            for q in emptied:
                act.sem_inc(q, 1)
            for q in (*stored, *s_mix, *s_out):
                act.sem_inc(q, 16)
            NR = KD + KQ + KKV
            act.dma_start(xin[:, 0, :], tok(xf)[:, 0, :]).then_inc(s_x[0], 16)
            act.dma_start(xin[:, 1, :], tok(xf)[:, 1, :]).then_inc(s_x[1], 16)
            act.dma_start(graw[0:KD, :], w_norm.rearrange("(k p) -> k p", p=P)).then_inc(s_gain, 16)
            act.dma_start(graw[KD:KD + KQ, :], g_q_latent.rearrange("(k p) -> k p", p=P)).then_inc(s_gain, 16)
            act.dma_start(graw[KD + KQ:NR, :], g_kv_latent.rearrange("(k p) -> k p", p=P)).then_inc(s_gain, 16)
            act.dma_start(gqk[:, 0, :], g_q_head.partition_broadcast(P)).then_inc(s_bc, 16)
            act.dma_start(gqk[:, 1, :], g_k_head.partition_broadcast(P)).then_inc(s_bc, 16)
            act.dma_start(ggo[:], g_gdn_out.partition_broadcast(P)).then_inc(s_bc, 16)

            for tb in range(TB):
                act.wait_ge(s_x[tb], 16)
                if tb:
                    act.wait_ge(act_done, A0.after("sumsq0"))
                nc.scalar.activation(junk[:], xin[:, tb, :], ACT.Square, accum_out=ss[:, tb:tb + 1]).then_inc(act_done, A0.one(f"sumsq{tb}"))
            act.wait_ge(s_const, 16)
            act.wait_ge(act_done, A0.after("sumsq1"))
            rsqrt(rs[:, 0:TB], ss[:, 0:TB], D, A0, "ln", "rstd")
            for s in range(ACT_LEAD):
                hi(0, 0, RING, s)

            def turn_hi(n, src_phase, names, dst, k0, g0, phase):
                for g in range(n):
                    act.wait_ge(pe_done, src_phase.after(f"{names}{g}"))
                    for kk in range(2):
                        k = 2 * g + kk
                        ins = nc.scalar.activation(dst[:, k, :], side[:, g % 4, kk * S:(kk + 1) * S], ACT.Copy,
                                                   scale=gcol[:, g0 + k:g0 + k + 1])
                    ins.then_inc(act_done, phase.one(f"hi{g}"))

            act.wait_ge(dve_done, D0.after("gcol"))
            turn_hi(NG, P0, "x", xT[0], 0, 0, A0)

            KT = KD // ROWS
            with act.Fori(0, 2) as i:
                for s in range(KT):
                    hi(0, i, KT, s + ACT_LEAD)
                act.wait_ge(tile_used, i * KT + (KT + 1))
                act.wait_ge(dve_done, D0.after(f"lo{NG - 1}"))
                nc.scalar.copy(craw[:, :, bass.ds(i * COLS, COLS)], acc[0][:]).then_inc(emptied[0], 1)
            for s in range(2 * KT, 3 * KT):
                hi(0, 0, RING, s + ACT_LEAD) if s + ACT_LEAD < T_MISC else hi(T_MISC, 0, RING, s + ACT_LEAD - T_MISC)
            act.wait_ge(tile_used, T_MISC + 1)
            nc.scalar.copy(craw[:, :, 2 * COLS:3 * COLS], acc[0][:]).then_inc(emptied[0], 1)
            hi(T_MISC, 0, RING, ACT_LEAD)
            for s in range(3):
                hi(T_Z, 0, RING, s)
            act.wait_ge(tile_used, T_Z + 1)
            nc.scalar.copy(misc[:], acc[1][:, :, 0:MN]).then_inc(emptied[1], 1)

            act.wait_ge(emptied[0], 4)
            for n, (tb, a, b) in enumerate(((0, 0, RQ), (1, 0, RQ), (0, RQ, RQ + RKV), (1, RQ, RQ + RKV))):
                if n:
                    act.wait_ge(act_done, A1.after(f"sumsq{n - 1}"))
                nc.scalar.activation(cjunk[:, 0:b - a], craw[:, tb, a:b], ACT.Square,
                                     accum_out=ss[:, n:n + 1]).then_inc(act_done, A1.one(f"sumsq{n}"))
            act.wait_ge(act_done, A1.after("sumsq3"))
            nc.scalar.activation(rs[:, 0:2], ss[:, 0:2], ACT.Ln, bias=eps, scale=1.0 / RQ).then_inc(act_done, A1.one("lnq"))
            nc.scalar.activation(rs[:, 2:4], ss[:, 2:4], ACT.Ln, bias=eps, scale=1.0 / RKV).then_inc(act_done, A1.one("lnkv"))
            act.wait_ge(act_done, A1.after("lnkv"))
            nc.scalar.activation(rs[:, 0:4], rs[:, 0:4], ACT.Exp, scale=-0.5).then_inc(act_done, A1.one("rstd"))
            act.wait_ge(emptied[1], 2)
            nc.scalar.activation(beta[:].rearrange("p h t -> p t h"), misc[:, :, ROPE:ROPE + H], ACT.Sigmoid).then_inc(act_done, A1.one("beta"))
            act.wait_ge(s_row, 48)
            nc.scalar.activation(alg[:, 0, :], alg[:, 0, :], ACT.Exp).then_inc(act_done, A1.one("expa"))
            act.wait_ge(dve_done, D1.after("nabs"))
            nc.scalar.activation(av[:, 1], av[:, 1], ACT.Exp).then_inc(act_done, A1.one("expx"))
            act.wait_ge(act_done, A1.after("expx"))
            nc.scalar.activation(av[:, 1], av[:, 1], ACT.Ln, bias=one).then_inc(act_done, A1.one("lnx"))
            nc.scalar.activation(trig[:], ang[:], ACT.Sin).then_inc(act_done, A1.one("sin"))

            def plain(t0, n, kn, dst, n_emptied, n_stored, func=ACT.Copy):
                per = 2 * kn // ROWS
                with act.Fori(0, n // 2) as i:
                    for s in range(per):
                        hi(t0, i, per, s + ACT_LEAD)
                        if (s + 1) % (per // 2) == 0:
                            c = s // (per // 2)
                            store(i * per + (t0 + s + 1), c, i + n_emptied[c], i * 16 + 16 * n_stored[c], dst,
                                  i * (2 * COLS) + c * COLS, func)

            def store(used, c, n_emptied, n_stored, dst, col, func=ACT.Copy):
                act.wait_ge(tile_used, used + 1)
                act.wait_ge(stored[c], n_stored + 16)
                if func == ACT.Copy:
                    nc.scalar.copy(stage[:, c], acc[c][:]).then_inc(emptied[c], 1)
                else:
                    nc.scalar.activation(stage[:, c], acc[c][:], func).then_inc(emptied[c], 1)
                act.wait_ge(emptied[c], n_emptied + 2)
                act.dma_start(tok(dst)[:, :, bass.ds(col, COLS)], stage[:, c]).then_inc(stored[c], 16)

            plain(T_Z, 4, KD, z_d, (3, 1), (0, 0), ACT.Silu)
            act.wait_ge(pe_done, P1.after("cum"))
            act.wait_ge(dve_done, D1.after("kdx"))
            nc.scalar.activation(egc[:], gc[:], ACT.Exp).then_inc(act_done, A1.one("egc"))
            nc.scalar.activation(ekd[:], ekd[:], ACT.Exp).then_inc(act_done, A1.one("ekd"))
            nc.scalar.activation(glast[:].rearrange("p h c -> p c h"),
                                 side[:, 0, 4 * H:8 * H].rearrange("p (c h) -> p c h", h=H), ACT.Exp).then_inc(act_done, A1.one("glast"))
            act.wait_ge(dve_done, D1.after("gct"))
            act.dma_start(row_d.rearrange("a h s -> h a s"), gcT[:]).then_inc(s_gc, 16)
            turn_hi(NC, P1, "c", cT[0], 0, KD, A1)
            plain(T_Q, 6, KQ, q_d, (5, 3), (2, 2))
            plain(T_KV, 8, KKV, kv_d, (8, 6), (5, 5))
            act.wait_ge(s_gc, 16)

            with act.Fori(0, 4) as i:
                for slot in range(3 * KT):
                    hi(T_B, i, 3 * KT, slot + ACT_LEAD)
                    half, s = slot // 24, slot % 24
                    turn = i * 2 + half
                    if s == 0:
                        act.wait_ge(pe_done, PB.after("heads", i * 2 + (half - 1)))
                        nc.scalar.copy(qk[:, 1, :, :, NOPE:QK],
                                       misc[:, :, 0:ROPE].unsqueeze(2).to_broadcast([P, TB, 2, ROPE])).then_inc(act_done, AB.one("rope"))
                    if s == 3:
                        act.wait_ge(s_qk, i * 96 + (48 * half + 48))
                        act.wait_ge(act_done, AB.after("rope", turn))
                        nc.scalar.activation(sq[:].rearrange("p a t h n -> p (a t h n)"), qk[:].rearrange("p a t h n -> p (a t h n)"),
                                             ACT.Square).then_inc(act_done, AB.one("sq"))
                    if s == 4:
                        act.wait_ge(dve_done, DB.after("sum", turn))
                        rsqrt(rs[:, 0:8], ss[:, 0:8], QK, AB, "ln", "rstd", turn)
                    if s == 9:
                        act.wait_ge(pe_done, PB.after("heads", turn))
                        nc.scalar.copy(qkTa[:].rearrange("p a h n -> p (a h n)"),
                                       side[:, 0:2, :].rearrange("p a n -> p (a n)")).then_inc(act_done, AB.one("headsT"))
                    if s == 12:
                        act.wait_ge(dve_done, DB.after("neg", turn))
                        for n, name in enumerate(("expA", "expB", "expC", "expD")):
                            tb, h = n // 2, n % 2
                            r = sc[:, h, tb * P:tb * P + (tb + 1) * P]
                            nc.scalar.activation(r, r, ACT.Exp, bias=mx[:, 1, tb, h:h + 1],
                                                 accum_out=mx[:, 2, tb, h:h + 1]).then_inc(act_done, AB.one(name))
                    if s == 14:
                        act.wait_ge(pe_done, PB.after("probs", turn))
                        nc.scalar.copy(pT[:], side[:, 2:4, 0:3 * P]).then_inc(act_done, AB.one("probsT"))
                    if (slot + 1) % KT == 0:
                        n = slot // KT
                        c = n % 2
                        store(i * (3 * KT) + (T_B + slot + 1), c, i * (2 - c) + ((12, 10)[c] + n // 2), i * (16 * (2 - c)) + 16 * (9 + n // 2),
                              g_d[TAPS - 1:TAPS - 1 + S, :], i * COLS + n * W)
                    if s == 18:
                        act.wait_ge(pe_done, PB.after("turn", turn))
                        for q in s_mix[0:2]:
                            act.wait_ge(q, i * 32 + (16 * half + 16))
                        nc.scalar.copy(mT[0][:].rearrange("p h n -> p (h n)"), side[:, 1, :]).then_inc(act_done, AB.one("hi"))
                    if s == 20:
                        act.wait_ge(dve_done, DB.after("lo", turn))
                        for n in range(2):
                            act.dma_start(mix_d[n][:, bass.ds(i * 4 + half * 2, 2), :], mT[n][:].bitcast(F32)).then_inc(s_mix[n], 16)

            plain(T_ZG, 4, KD, zg_d, (20, 14), (17, 13), ACT.Silu)

            with act.Fori(0, TURNS) as i:
                for s in range(2 * KT):
                    hi(T_C, i, 2 * KT, s + ACT_LEAD)
                    if s == 0:
                        act.wait_ge(s_cv, i * 16 + 16)
                        act.wait_ge(pe_done, PC.after("turn", i - 1))
                        nc.scalar.activation(sl[:, :, 0:3, :].rearrange("p (h t) j n -> p t h (j n)", h=2),
                                             cv[:].rearrange("p t h j n -> p t h (j n)"), ACT.Silu).then_inc(act_done, AC.one("silu"))
                        act.wait_ge(act_done, AC.after("silu", i))
                        nc.scalar.activation(tt[:], sl[:, :, 0:2, :], ACT.Square).then_inc(act_done, AC.one("square"))
                        act.wait_ge(pool_done, GC.after("below", i))
                        nc.scalar.activation(dec[:], dec[:], ACT.Exp).then_inc(act_done, AC.one("exp"))
                    if s == 1:
                        act.wait_ge(dve_done, DC.after("sum", i))
                        nc.scalar.activation(rs[:, 0:8], ss[:, 0:8], ACT.Ln, bias=eps).then_inc(act_done, AC.one("ln"))
                        act.wait_ge(act_done, AC.after("ln", i))
                        nc.scalar.activation(rs[:, 0:8], rs[:, 0:8], ACT.Exp, scale=-0.5).then_inc(act_done, AC.one("rstd"))
                    if s == 2:
                        act.wait_ge(s_gcb, i * 16 + 16)
                        nc.scalar.activation(erow[:], rowb[:, 0], ACT.Exp).then_inc(act_done, AC.one("erow"))
                    if s == 4:
                        act.wait_ge(pe_done, PC.after("turns", i))
                        nc.scalar.copy(pq[:, :, 0, :], side[:, 2, :].rearrange("p (b n) -> p b n", n=P)).then_inc(act_done, AC.one("kT"))
                    if 10 <= s < 18 and s % 2 == 0:
                        n = 1 + (s - 8) // 2
                        act.wait_ge(pe_done, PC.after(f"ma{n}", i))
                        nc.scalar.copy(tt[:, :, 1, :], side[:, 2, :].rearrange("p (b n) -> p b n", n=P)).then_inc(act_done, AC.one(f"tT{n}"))
                    if s == 19:
                        act.wait_ge(pe_done, PC.after("solve", i))
                        nc.scalar.copy(wT[:].rearrange("p b n -> p (b n)"), side[:, 3, :]).then_inc(act_done, AC.one("wT"))
                    if s == 15 or s == 31:
                        c = s // KT
                        act.wait_ge(gated[c], i + 2)
                        nc.scalar.activation(stage[:, c], stage[:, c], ACT.Sigmoid).then_inc(emptied[c], 1)
                        act.wait_ge(emptied[c], i + ((22, 16)[c] + 2))
                        act.dma_start(tok(gate_d)[:, :, bass.ds(i * (2 * COLS) + c * COLS, COLS)], stage[:, c]).then_inc(stored[c], 16)
                    if s == 26:
                        act.wait_ge(pe_done, PC.after("out1", i))
                        nc.scalar.activation(m1[:].rearrange("p b n -> p (b n)"), side[:, 2, :], ACT.Square).then_inc(act_done, AC.one("osq"))
                        act.wait_ge(dve_done, DC.after("osum", i))
                        rsqrt(rs[:, 0:4], ss[:, 0:4], DV, AC, "oln", "orstd", i)
                    if s == 28:
                        act.wait_ge(pe_done, PC.after("turn", i))
                        for q in s_mix[2:4]:
                            act.wait_ge(q, i * 16 + 16)
                        nc.scalar.copy(gT[0][:].rearrange("p h n -> p (h n)"), side[:, 3, :]).then_inc(act_done, AC.one("hi"))
                    if s == 30:
                        act.wait_ge(dve_done, DC.after("lo", i))
                        for n in range(2):
                            act.dma_start(mix_d[2 + n][:, bass.ds(i * 2, 2), :], gT[n][:].bitcast(F32)).then_inc(s_mix[2 + n], 16)

            def hT_hi(i_prev):
                act.wait_ge(pe_done, PD.after("turn", i_prev))
                nc.scalar.copy(xT[0][:, bass.ds(i_prev * 4, 4), :].rearrange("p k n -> p (k n)"),
                               side[:, 0:2, :].rearrange("p a n -> p (a n)")).then_inc(act_done, AD.one("hi"))

            KO = KW // ROWS
            for s in range(2 * KO):
                hi(T_D, 0, 2 * KO, s + ACT_LEAD)
            with act.Fori(1, TURNS) as i:
                for s in range(2 * KO):
                    hi(T_D, i, 2 * KO, s + ACT_LEAD)
                    if s == 3:
                        hT_hi(i - 1)
            hT_hi(TURNS - 1)

            def send(i, c):
                act.wait_ge(summed[c], i + 2)
                act.dma_start(tok(outf)[:, :, bass.ds(i * (2 * COLS) + c * COLS, COLS)], stage[:, c]).then_inc(s_out[c], 16)

            with act.Fori(0, 3) as i:
                for s in range(2 * KT):
                    hi(T_E, i, 2 * KT, s + ACT_LEAD)
                    if s == 15 or s == 31:
                        send(i, s // KT)
            for s in range(2 * KT):
                if s + ACT_LEAD < 2 * KT:
                    hi(T_E, 3, 2 * KT, s + ACT_LEAD)
                if s == 15 or s == 31:
                    send(3, s // KT)
            for q in s_out:
                act.wait_ge(q, 64 + 16)
            for q in s_mix:
                act.wait_ge(q, 16 * (TURNS + 1))
            act.wait_ge(stored[0], 16 * 28)
            act.wait_ge(stored[1], 16 * 24)

        @block.vector
        def _(dve):
            V = nc.vector

            def lo(t0, turn, per, s):
                dve.wait_ge(hi_done, turn * per + (t0 + s + 1))
                w = width(t0 + s)
                V.tensor_tensor(wlo[:, s % RING, 0:w], raw[:, s % RING, 0:w], whi[:, s % RING, 0:w].bitcast(F32),
                                ALU.subtract).then_inc(lo_done, 1)

            for q in (*gated, *summed):
                dve.sem_inc(q, 1)
            for tb in range(TB):
                if tb == 0:
                    dve.wait_ge(act_done, A0.after("rstd"))
                V.tensor_scalar(xin[:, tb, :], xin[:, tb, :], rs[:, tb:tb + 1], None, ALU.mult).then_inc(dve_done, D0.one(f"norm{tb}"))
            dve.wait_ge(pe_done, P0.after("gains"))
            NR = KD + KQ + KKV
            V.tensor_copy(gcol[:], acc[0][:, 0, 0:NR]).then_inc(dve_done, D0.one("gcol"))
            dve.wait_ge(dve_done, D0.after("gcol"))
            for s in range(DVE_LEAD):
                lo(0, 0, RING, s)

            def turn_lo(n, dst, g0, a_phase, phase):
                for g in range(n):
                    dve.wait_ge(act_done, a_phase.after(f"hi{g}"))
                    for kk in range(2):
                        k = 2 * g + kk
                        ins = V.scalar_tensor_tensor(out=dst[1][:, k, :], in0=side[:, g % 4, kk * S:(kk + 1) * S],
                                                     scalar=gcol[:, g0 + k:g0 + k + 1], in1=dst[0][:, k, :].bitcast(F32),
                                                     op0=ALU.mult, op1=ALU.subtract)
                    ins.then_inc(dve_done, phase.one(f"lo{g}"))

            turn_lo(NG, xT, 0, A0, D0)
            KT = KD // ROWS
            with dve.Fori(0, 2) as i:
                for s in range(KT):
                    lo(0, i, KT, s + DVE_LEAD)
            for s in range(2 * KT, 3 * KT + RING):
                t = s + DVE_LEAD
                lo(0, 0, RING, t) if t < T_MISC else lo(T_MISC, 0, RING, t - T_MISC) if t < T_Z else lo(T_Z, 0, RING, t - T_Z)
            dve.wait_ge(act_done, A1.after("rstd"))
            for n, (tb, a, b) in enumerate(((0, 0, RQ), (1, 0, RQ), (0, RQ, RQ + RKV), (1, RQ, RQ + RKV))):
                V.tensor_scalar(craw[:, tb, a:b], craw[:, tb, a:b], rs[:, n:n + 1], None, ALU.mult).then_inc(dve_done, D1.one(f"norm{n}"))
            dve.wait_ge(s_row, 48)
            V.tensor_copy(pos_f[:], pos_i[:]).then_inc(dve_done, D1.one("pos"))
            dve.wait_ge(dve_done, D1.after("pos"))
            for tb in range(TB):
                V.tensor_scalar(ang[:, :, tb, :], cst[:, C_FREQ:C_FREQ + HALF].unsqueeze(1).to_broadcast([P, 2, HALF]),
                                pos_f[:, tb:tb + 1], None, ALU.mult).then_inc(dve_done, D1.one(f"ang{tb}"))
            dve.wait_ge(dve_done, D1.after("ang1"))
            TWO_PI = 2.0 * np.pi
            MAGIC = 1.5 * 2.0 ** 23
            PART1 = 6.28125
            PART2 = float(np.float32(np.round((TWO_PI - PART1) * 2.0 ** 21) / 2.0 ** 21))
            PART3 = float(np.float32(TWO_PI - PART1 - PART2))
            V.tensor_scalar(whole[:, 0], ang[:, 0], 1.0 / TWO_PI, 0.25, ALU.mult, ALU.add).then_inc(dve_done, D1.one("u0"))
            V.tensor_scalar(whole[:, 1], ang[:, 1], 1.0 / TWO_PI, None, ALU.mult).then_inc(dve_done, D1.one("u1"))
            dve.wait_ge(dve_done, D1.after("u1"))
            V.tensor_scalar(whole[:], whole[:], MAGIC, None, ALU.add).then_inc(dve_done, D1.one("r0"))
            dve.wait_ge(dve_done, D1.after("r0"))
            V.tensor_scalar(whole[:], whole[:], MAGIC, None, ALU.subtract).then_inc(dve_done, D1.one("r1"))
            for part, name, before in ((PART1, "s1", "r1"), (PART2, "s2", "s1"), (PART3, "s3", "s2")):
                dve.wait_ge(dve_done, D1.after(before))
                V.scalar_tensor_tensor(out=ang[:], in0=whole[:], scalar=-part, in1=ang[:], op0=ALU.mult, op1=ALU.add).then_inc(dve_done, D1.one(name))
            dve.wait_ge(dve_done, D1.after("s3"))
            V.tensor_scalar(ang[:, 0], ang[:, 0], np.pi / 2, None, ALU.add).then_inc(dve_done, D1.one("s4"))
            dve.wait_ge(dve_done, D1.after("s4"))
            V.tensor_scalar(ang[:], ang[:], 3.1415925, -3.1415925, ALU.min, ALU.max).then_inc(dve_done, D1.one("s5"))
            dve.wait_ge(emptied[1], 2)
            V.tensor_tensor(av[:, 0], misc[:, :, ROPE + H:MN], alg[:, 1:2, :].to_broadcast([P, TB, H]), ALU.add).then_inc(dve_done, D1.one("adt"))
            dve.wait_ge(dve_done, D1.after("adt"))
            V.scalar_tensor_tensor(out=av[:, 1], in0=av[:, 0], scalar=-1.0, in1=av[:, 0], op0=ALU.mult, op1=ALU.min).then_inc(dve_done, D1.one("nabs"))
            dve.wait_ge(act_done, A1.after("lnx"))
            V.scalar_tensor_tensor(out=av[:, 2], in0=av[:, 0], scalar=0.0, in1=av[:, 1], op0=ALU.max, op1=ALU.add).then_inc(dve_done, D1.one("sp"))
            dve.wait_ge(dve_done, D1.after("sp"))
            V.scalar_tensor_tensor(out=av[:, 3], in0=av[:, 2], scalar=-1.0, in1=alg[:, 0:1, :].to_broadcast([P, TB, H]),
                                   op0=ALU.mult, op1=ALU.mult).then_inc(dve_done, D1.one("g"))

            def plain(t0, n, kn):
                per = 2 * kn // ROWS
                with dve.Fori(0, n // 2) as i:
                    for s in range(per):
                        lo(t0, i, per, s + DVE_LEAD)

            plain(T_Z, 4, KD)
            dve.wait_ge(pe_done, P1.after("cum"))
            V.tensor_copy(gc[:].rearrange("p h t -> p t h"), side[:, 0, 0:2 * H].rearrange("p (t h) -> p t h", h=H)).then_inc(dve_done, D1.one("gc"))
            V.tensor_copy(gth[:, 0], side[:, 0, 0:2 * H].rearrange("p (t h) -> p t h", h=H)).then_inc(dve_done, D1.one("gth"))
            V.tensor_copy(gth[:, 1], beta[:].rearrange("p h t -> p t h")).then_inc(dve_done, D1.one("gth2"))
            dve.wait_ge(dve_done, D1.after("gc"))
            V.tensor_tensor(ekd[:].rearrange("p h t -> p t h"), side[:, 0, 2 * H:4 * H].rearrange("p (t h) -> p t h", h=H),
                            gc[:].rearrange("p h t -> p t h"), ALU.subtract).then_inc(dve_done, D1.one("kdx"))
            dve.wait_ge(pe_done, P1.after("gct"))
            V.tensor_copy(gcT[:].rearrange("h a s -> h (a s)"), side[0:H, 1, :]).then_inc(dve_done, D1.one("gct"))
            turn_lo(NC, cT, KD, A1, D1)
            plain(T_Q, 6, KQ)
            plain(T_KV, 8, KKV)

            SCALE = float(QK) ** -0.5
            with dve.Fori(0, 4) as i:
                def after(name):
                    dve.wait_ge(dve_done, DB.after(name, turn))
                for slot in range(3 * KT):
                    lo(T_B, i, 3 * KT, slot + DVE_LEAD)
                    half, s = slot // 24, slot % 24
                    turn = i * 2 + half
                    flat = qk[:].rearrange("p a t h n -> p (a t h) n")
                    sqf = sq[:].rearrange("p a t h n -> p (a t h) n")
                    if s == 3:
                        dve.wait_ge(act_done, AB.after("sq", turn))
                        V.tensor_reduce(ss[:, 0:8], sqf, AX, ALU.add).then_inc(dve_done, DB.one("sum"))
                    if s == 4:
                        dve.wait_ge(act_done, AB.after("rstd", turn))
                        V.tensor_tensor(flat, flat, rs[:, 0:8].unsqueeze(2).to_broadcast([P, 8, QK]), ALU.mult).then_inc(dve_done, DB.one("unit"))
                        after("unit")
                        dve.wait_ge(s_bc, 48)
                        V.tensor_tensor(qk[:].rearrange("p a t h n -> p a (t h) n"), qk[:].rearrange("p a t h n -> p a (t h) n"),
                                        gqk[:].unsqueeze(2).to_broadcast([P, 2, 2 * TB, QK]), ALU.mult).then_inc(dve_done, DB.one("gain"))
                    if s == 5:
                        after("gain")
                        x1 = qk[:, :, :, :, NOPE:NOPE + HALF]
                        x2 = qk[:, :, :, :, NOPE + HALF:QK]
                        tg = lambda n, a: trig[:, n].unsqueeze(2).to_broadcast([P, TB, 2, HALF])
                        r = lambda n, a: rt[:, n, 4 * a:4 * a + 4, :].rearrange("p (t h) n -> p t h n", h=2)
                        for n, (xx, f, name) in enumerate(((x1, 0, "r1"), (x2, 1, "r2"), (x2, 0, "r3"), (x1, 1, "r4"))):
                            V.tensor_tensor(r(n, 0), xx[:, 0], tg(f, 0), ALU.mult)
                            V.tensor_tensor(r(n, 1), xx[:, 1], tg(f, 1), ALU.mult).then_inc(dve_done, DB.one(name))
                        after("r4")
                        rr = lambda n: rt[:, n].rearrange("p (a b) n -> p a b n", a=2)
                        v = lambda t: t.rearrange("p a t h n -> p a (t h) n")
                        V.tensor_tensor(v(x1), rr(0), rr(1), ALU.subtract).then_inc(dve_done, DB.one("r5"))
                        V.tensor_tensor(v(x2), rr(2), rr(3), ALU.add).then_inc(dve_done, DB.one("r6"))
                    if s == 9:
                        dve.wait_ge(pe_done, PB.after("heads", turn))
                        V.tensor_copy(qkTb[:].rearrange("p a h n -> p (a h n)"),
                                      side[0:ROPE, 2:4, :].rearrange("p a n -> p (a n)")).then_inc(dve_done, DB.one("ropeT"))
                    if s == 11:
                        dve.wait_ge(pe_done, PB.after("scores", turn))
                        V.scalar_tensor_tensor(out=sc[:], in0=side[:, 0:2, 0:3 * P], scalar=SCALE,
                                               in1=cst[:, C_MASK:C_MASK + 3 * P].unsqueeze(1).to_broadcast([P, 2, 3 * P]),
                                               op0=ALU.mult, op1=ALU.add).then_inc(dve_done, DB.one("mask"))
                        after("mask")
                        V.tensor_reduce(mx[:, 0, 0, :], sc[:, :, 0:P], AX, ALU.max).then_inc(dve_done, DB.one("max0"))
                        V.tensor_reduce(mx[:, 0, 1, :], sc[:, :, P:3 * P], AX, ALU.max).then_inc(dve_done, DB.one("max1"))
                        after("max1")
                        V.tensor_scalar(mx[:, 1], mx[:, 0], -1.0, None, ALU.mult).then_inc(dve_done, DB.one("neg"))
                    if s == 16:
                        dve.wait_ge(act_done, AB.after("expD", turn))
                        V.reciprocal(mx[:, 0], mx[:, 2]).then_inc(dve_done, DB.one("rden"))
                        after("rden")
                        dve.wait_ge(pe_done, PB.after("values", turn))
                        ogf = og[:].rearrange("p t h n -> p (t h) n")
                        V.tensor_tensor(ogf, side[:, 0, :].rearrange("p (b n) -> p b n", n=P),
                                        mx[:, 0].rearrange("p t h -> p (t h)").unsqueeze(2).to_broadcast([P, 2 * TB, DV]),
                                        ALU.mult).then_inc(dve_done, DB.one("div"))
                        after("div")
                        dve.wait_ge(s_zs, i * 32 + (16 * half + 16))
                        V.tensor_tensor(og[:], og[:], zs[:], ALU.mult).then_inc(dve_done, DB.one("gate"))
                    if s == 18:
                        dve.wait_ge(act_done, AB.after("hi", turn))
                        V.tensor_tensor(mT[1][:].rearrange("p h n -> p (h n)"), side[:, 1, :],
                                        mT[0][:].rearrange("p h n -> p (h n)").bitcast(F32), ALU.subtract).then_inc(dve_done, DB.one("lo"))

            plain(T_ZG, W // COLS, KD)

            for q in s_mix[0:2]:
                dve.wait_ge(q, 16 * (TURNS + 1))
            dve.wait_ge(s_conv, 16 * 2 * 12)
            V.memset(qeT[:], 0.0).then_inc(dve_done, DZ.one("zero"))
            bc = lambda a: a.unsqueeze(2).to_broadcast([P, 2 * TB, DV])
            with dve.Fori(0, TURNS) as i:
                def after(name):
                    dve.wait_ge(dve_done, DC.after(name, i))

                def of_pair(a):
                    return a[:, bass.ds(i * 2, 2), :].rearrange("p h t -> p (h t)")
                rk = rs[:, 0:8].rearrange("p (b j) -> p b j", j=2)
                for s in range(2 * KT):
                    lo(T_C, i, 2 * KT, s + DVE_LEAD)
                    if s == 0:
                        dve.wait_ge(act_done, AC.after("square", i))
                        V.tensor_reduce(ss[:, 0:8], tt[:].rearrange("p b j n -> p (b j) n"), AX, ALU.add).then_inc(dve_done, DC.one("sum"))
                    if s == 1:
                        dve.wait_ge(act_done, AC.after("rstd", i))
                        V.tensor_scalar(cf[:, 0], rk[:, :, 0], float(DV) ** -0.5, None, ALU.mult).then_inc(dve_done, DC.one("cq"))
                        V.tensor_tensor(sl[:, :, 1, :], sl[:, :, 1, :], bc(rk[:, :, 1]), ALU.mult).then_inc(dve_done, DC.one("kn"))
                        after("cq")
                        V.tensor_tensor(sl[:, :, 0, :], sl[:, :, 0, :], bc(cf[:, 0]), ALU.mult).then_inc(dve_done, DC.one("qn"))
                    if s == 2:
                        V.tensor_tensor(cf[:, 1], of_pair(beta), of_pair(egc), ALU.mult).then_inc(dve_done, DC.one("cke"))
                        after("cke")
                        V.tensor_tensor(kbe[:], sl[:, :, 1, :], bc(cf[:, 1]), ALU.mult).then_inc(dve_done, DC.one("kbe"))
                    if s == 4:
                        dve.wait_ge(pe_done, PC.after("turns", i))
                        dve.wait_ge(act_done, AC.after("erow", i))
                        dve.wait_ge(dve_done, DZ.after("zero"))
                        V.tensor_tensor(qeT[:].rearrange("p b a n -> p b (a n)").rearrange("p b (c n) -> p b c n", c=2)[:, :, :, 0:CHUNK],
                                        side[:, 3, :].rearrange("p (b c n) -> p b c n", c=2, n=CHUNK),
                                        erow[:].rearrange("p b (c n) -> p b c n", c=2), ALU.mult).then_inc(dve_done, DC.one("qeT"))
                        V.tensor_copy(pq[:, :, 1, :], side[:, 3, :].rearrange("p (b n) -> p b n", n=P)).then_inc(dve_done, DC.one("qT"))
                    if s == 6:
                        dve.wait_ge(pe_done, PC.after("products", i))
                        pr = side[:, 0:2, :].rearrange("p a (b j n) -> p (a b) j n", j=2, n=P)
                        dve.wait_ge(pool_done, GC.after("decb", i))
                        V.tensor_tensor(lt[:], pr[:, :, 0, :], lt[:], ALU.mult).then_inc(dve_done, DC.one("lt"))
                        V.tensor_tensor(dec[:], pr[:, :, 1, :], dec[:], ALU.mult).then_inc(dve_done, DC.one("attn"))
                        after("lt")
                        V.tensor_tensor(m1[:], lt[:], level(0).unsqueeze(1).to_broadcast([P, 2 * TB, P]), ALU.mult).then_inc(dve_done, DC.one("l1"))
                        after("l1")
                        V.tensor_tensor(tt[:, :, 1, :], ident.unsqueeze(1).to_broadcast([P, 2 * TB, P]), m1[:], ALU.subtract).then_inc(dve_done, DC.one("tt1"))
                    if s == 7:
                        dve.wait_ge(pe_done, PC.after("t1", i))
                        V.tensor_copy(tt[:, :, 0, :], side[:, 2, :].rearrange("p (b n) -> p b n", n=P)).then_inc(dve_done, DC.one("t1"))
                    if 8 <= s < 18:
                        n = 1 + (s - 8) // 2
                        if s % 2 == 0:
                            dve.wait_ge(pe_done, PC.after(f"ma{n}", i))
                            V.tensor_tensor(m1[:], side[:, 3, :].rearrange("p (b n) -> p b n", n=P),
                                            level(n).unsqueeze(1).to_broadcast([P, 2 * TB, P]), ALU.mult).then_inc(dve_done, DC.one(f"ma{n}"))
                        else:
                            dve.wait_ge(pe_done, PC.after(f"mb{n}", i))
                            j = 0 if n < len(LEVELS) - 1 else 1
                            V.tensor_tensor(tt[:, :, j, :], tt[:, :, j, :], side[:, 0, :].rearrange("p (b n) -> p b n", n=P),
                                            ALU.subtract).then_inc(dve_done, DC.one(f"mb{n}"))
                    if s == 18:
                        dve.wait_ge(pe_done, PC.after("solve", i))
                        V.tensor_copy(sl[:, :, 2, :], side[:, 2, :].rearrange("p (b n) -> p b n", n=P)).then_inc(dve_done, DC.one("u"))

                    def state(c, names):
                        for h in range(2):
                            V.scalar_tensor_tensor(out=st[:, c % 2, h, :], in0=st[:, (c - 1) % 2, h, :],
                                                   scalar=glast[:, bass.ds(i * 2 + h, 1), c - 1], in1=side[:, 1, h * P:(h + 1) * P],
                                                   op0=ALU.mult, op1=ALU.add).then_inc(dve_done, DC.one(names[h]))

                    def new_v(c, name):
                        r = slice((c % 2) * CHUNK, (c % 2 + 1) * CHUNK)
                        v = sl[:].rearrange("p (h t) j n -> p h t j n", t=TB)[r, :, c // 2, 2, :]
                        V.tensor_tensor(v, v, side[r, 0, 0:2 * P].rearrange("p (h n) -> p h n", n=P), ALU.subtract).then_inc(dve_done, DC.one(name))

                    if s == 19:
                        dve.wait_ge(pe_done, PC.after("kv0", i))
                        V.tensor_copy(st[:, 1].rearrange("p h n -> p (h n)"), side[:, 1, 0:2 * P]).then_inc(dve_done, DC.one("s1"))
                    if s == 20:
                        dve.wait_ge(pe_done, PC.after("ws1", i))
                        new_v(1, "v1")
                    if s == 21:
                        dve.wait_ge(pe_done, PC.after("kv1", i))
                        state(2, ("s2a", "s2b"))
                    if s == 22:
                        dve.wait_ge(pe_done, PC.after("ws2", i))
                        new_v(2, "v2")
                    if s == 23:
                        dve.wait_ge(pe_done, PC.after("kv2", i))
                        state(3, ("s3a", "s3b"))
                    if s == 24:
                        dve.wait_ge(pe_done, PC.after("ws3", i))
                        new_v(3, "v3")
                    if s == 26:
                        dve.wait_ge(act_done, AC.after("osq", i))
                        V.tensor_reduce(ss[:, 0:4], m1[:], AX, ALU.add).then_inc(dve_done, DC.one("osum"))
                    if s == 27:
                        dve.wait_ge(act_done, AC.after("orstd", i))
                        dve.wait_ge(pool_done, GC.after("gz", i))
                        V.tensor_tensor(m1[:], side[:, 2, :].rearrange("p (b n) -> p b n", n=P), bc(rs[:, 0:4]), ALU.mult).then_inc(dve_done, DC.one("on"))
                        after("on")
                        z = sl[:].rearrange("p (h t) j n -> p t h j n", t=TB)[:, :, :, 3, :]
                        V.tensor_tensor(z, z, m1[:].rearrange("p (t h) n -> p t h n", h=2), ALU.mult).then_inc(dve_done, DC.one("ogate"))
                    if s == 28:
                        dve.wait_ge(act_done, AC.after("hi", i))
                        V.tensor_tensor(gT[1][:].rearrange("p h n -> p (h n)"), side[:, 3, :],
                                        gT[0][:].rearrange("p h n -> p (h n)").bitcast(F32), ALU.subtract).then_inc(dve_done, DC.one("lo"))
                    if s == 15 or s == 31:
                        c = s // KT
                        dve.wait_ge(tile_used, i * (2 * KT) + (T_C + s + 2))
                        dve.wait_ge(s_bb, i * 16 + 16)
                        dve.wait_ge(stored[c], i * 16 + 16 * (20, 16)[c])
                        V.tensor_tensor(stage[:, c], acc[c][:], bb[:, c:c + 1, :].to_broadcast([P, TB, COLS]), ALU.add).then_inc(gated[c], 1)

            KO = KW // ROWS

            def turn_D(i, previous):
                for s in range(2 * KO):
                    lo(T_D, i, 2 * KO, s + DVE_LEAD)
                    if s == 3 and previous:
                        dve.wait_ge(act_done, AD.after("hi", i - 1))
                        hT_lo(i - 1)
                    if s == KO - 1:
                        dve.wait_ge(tile_used, i * (2 * KO) + (T_D + KO + 1))
                        dve.wait_ge(s_gate[0], i * 16 + 16)
                        V.tensor_tensor(stage[:, 0], acc[0][:], stage[:, 0], ALU.mult).then_inc(gated[0], 1)
                    if s == 2 * KO - 1:
                        dve.wait_ge(tile_used, i * (2 * KO) + (T_D + 2 * KO + 1))
                        dve.wait_ge(s_gate[1], i * 16 + 16)
                        V.tensor_tensor(stage[:, 1], acc[1][:], stage[:, 1], ALU.mult).then_inc(gated[1], 1)
                        dve.wait_ge(gated[1], i + (TURNS + 2))
                        V.tensor_tensor(hb[:], stage[:, 0], stage[:, 1], ALU.add).then_inc(dve_done, DD.one("h3"))

            def hT_lo(i_prev):
                V.tensor_tensor(xT[1][:, bass.ds(i_prev * 4, 4), :].rearrange("p k n -> p (k n)"),
                                side[:, 0:2, :].rearrange("p a n -> p (a n)"),
                                xT[0][:, bass.ds(i_prev * 4, 4), :].rearrange("p k n -> p (k n)").bitcast(F32),
                                ALU.subtract).then_inc(dve_done, DD.one("lo"))

            turn_D(0, False)
            with dve.Fori(1, TURNS) as i:
                turn_D(i, True)
            dve.wait_ge(act_done, AD.after("hi", TURNS - 1))
            hT_lo(TURNS - 1)

            def residual(i, c, s):
                dve.wait_ge(tile_used, i * (2 * KT) + (T_E + s + 2))
                dve.wait_ge(s_xr[c], i * 16 + 16)
                dve.wait_ge(s_out[c], i * 16 + 16)
                V.tensor_tensor(stage[:, c], acc[c][:], xr[:, c], ALU.add).then_inc(summed[c], 1)

            with dve.Fori(0, 3) as i:
                for s in range(2 * KT):
                    lo(T_E, i, 2 * KT, s + DVE_LEAD)
                    if s == 15 or s == 31:
                        residual(i, s // KT, s)
            for s in range(2 * KT):
                if s + DVE_LEAD < 2 * KT:
                    lo(T_E, 3, 2 * KT, s + DVE_LEAD)
                if s == 15 or s == 31:
                    residual(3, s // KT, s)

        @block.gpsimd
        def _(pool):
            G = nc.gpsimd
            pool.wait_ge(dve_done, D0.after(f"lo{NG - 1}"))
            pool.dma_start(alg[:, 0, :], a_log.partition_broadcast(P)).then_inc(s_row, 16)
            pool.dma_start(alg[:, 1, :], dt_bias.partition_broadcast(P)).then_inc(s_row, 16)
            with nc.allow_non_contiguous_dma(reason="256 positions"):
                pool.dma_start(pos_i[:], positions.rearrange("a (t p) -> p (a t)", p=P)).then_inc(s_row, 16)
            G.memset(zrow[:], 0.0).then_inc(pool_done, G1.one("zero"))
            pool.wait_ge(pool_done, G1.after("zero"))
            pool.dma_start(g_d[0:TAPS - 1, :].rearrange("a (b n) -> (a b) n", n=256), zrow[:]).then_inc(s_zero, 16)
            for q in stored:
                pool.wait_ge(q, 16 * 10)
            pool.wait_ge(s_zero, 16)
            with pool.Fori(0, 4) as i:
                for n in range(3):
                    def done(name):
                        return GB.after(name, i * 3 + n)
                    pool.wait_ge(stored[n % 2], i * (16 * (2 - n % 2)) + 16 * (11 + n // 2))
                    if n:
                        pool.wait_ge(s_conv, i * 96 + 32 * n)
                    for j in range(TAPS):
                        pool.dma_start(xs[:, j], tok(g_d[j:j + S, :])[:, :, bass.ds(i * COLS + n * W, COLS)]).then_inc(s_tap, 16)
                    pool.dma_start(cw[:], conv_w[:, bass.ds(i * COLS + n * W, COLS)].partition_broadcast(P)).then_inc(s_tap, 16)
                    pool.wait_ge(s_tap, i * (3 * 16 * (TAPS + 1)) + (n + 1) * 16 * (TAPS + 1))
                    for j in range(TAPS):
                        G.tensor_tensor(xs[:, j], xs[:, j], cw[:, j:j + 1, :].to_broadcast([P, TB, COLS]),
                                        ALU.mult).then_inc(pool_done, GB.one(f"m{j}"))
                    for j in range(1, TAPS):
                        pool.wait_ge(pool_done, done("m3" if j == 1 else f"a{j - 1}"))
                        G.tensor_tensor(xs[:, 0], xs[:, 0], xs[:, j], ALU.add).then_inc(pool_done, GB.one(f"a{j}"))
                    pool.wait_ge(pool_done, done("a3"))
                    for tb in range(TB):
                        pool.dma_start(conv_d[tb * P:(tb + 1) * P, bass.ds(i * 4, 4), n, :],
                                       xs[:, 0, tb, :].rearrange("p (h n) -> p h n", n=DV)).then_inc(s_conv, 16)
                pool.wait_ge(s_conv, i * 96 + 96)
            for q in s_mix[0:2]:
                pool.wait_ge(q, 16 * (TURNS + 1))
            pool.dma_start(oT[0][:].bitcast(F32), mix_d[0][:]).then_inc(s_oT[0], 16)
            with pool.Fori(0, TURNS) as i:
                def of_pair(a):
                    return a[:, bass.ds(i * 2, 2), :].rearrange("p h t -> p (h t)").unsqueeze(2).to_broadcast([P, 2 * TB, DV])
                pool.wait_ge(s_gcb, i * 16 + 16)
                pool.wait_ge(pe_done, PC.after("out1", i - 1))
                G.tensor_tensor(dec[:], rowb[:, 0], of_pair(gc), ALU.subtract).then_inc(pool_done, GC.one("diff"))
                pool.wait_ge(pool_done, GC.after("diff", i))
                G.tensor_tensor(dec[:], dec[:], causal.unsqueeze(1).to_broadcast([P, 2 * TB, P]), ALU.mult).then_inc(pool_done, GC.one("below"))
                pool.wait_ge(act_done, AC.after("exp", i))
                G.tensor_tensor(dec[:], dec[:], causal.unsqueeze(1).to_broadcast([P, 2 * TB, P]), ALU.mult).then_inc(pool_done, GC.one("mask"))
                pool.wait_ge(pool_done, GC.after("mask", i))
                G.tensor_tensor(lt[:], dec[:], rowb[:, 1], ALU.mult).then_inc(pool_done, GC.one("decb"))
                pool.wait_ge(act_done, AC.after("silu", i))
                G.tensor_tensor(sl[:, :, 2, :], sl[:, :, 2, :], of_pair(beta), ALU.mult).then_inc(pool_done, GC.one("vb"))
                pool.wait_ge(dve_done, DC.after("kn", i))
                G.tensor_tensor(kd[:], sl[:, :, 1, :], of_pair(ekd), ALU.mult).then_inc(pool_done, GC.one("kd"))
                pool.wait_ge(s_zg, i * 32 + 32)
                pool.wait_ge(s_bc, 48)
                G.tensor_tensor(sl[:, :, 3, :], sl[:, :, 3, :], ggo[:].unsqueeze(1).to_broadcast([P, 2 * TB, DV]),
                                ALU.mult).then_inc(pool_done, GC.one("gz"))
            for q in s_mix:
                pool.wait_ge(q, 16 * (TURNS + 1))
            pool.wait_ge(pe_done, PC.after("turn", TURNS - 1))
            pool.wait_ge(gated[1], TURNS + 1)
            for n in range(1, 4):
                pool.dma_start(oT[n][:].bitcast(F32), mix_d[n][:]).then_inc(s_oT[n], 16)
            pool.wait_ge(stored[0], 16 * 28)
            pool.wait_ge(stored[1], 16 * 24)
            with pool.Fori(0, TURNS) as i:
                for c in range(2):
                    pool.wait_ge(gated[c], i + (TURNS + 1))
                    pool.wait_ge(dve_done, DD.after("h3", i - 1))
                    pool.dma_start(stage[:, c], tok(gate_d)[:, :, bass.ds(i * COLS + c * D, COLS)]).then_inc(s_gate[c], 16)
            pool.wait_ge(tile_used, T_E + 1)
            with pool.Fori(0, 4) as i:
                for c in range(2):
                    pool.wait_ge(summed[c], i + 1)
                    pool.dma_start(xr[:, c], tok(xf)[:, :, bass.ds(i * (2 * COLS) + c * COLS, COLS)]).then_inc(s_xr[c], 16)


_INS = ["x", "positions", "w_norm", "w_in", "b_gate", "w_q_up", "w_kv_up", "g_q_latent", "g_kv_latent", "g_q_head",
        "g_k_head", "w_o_mla", "conv_w", "a_log", "dt_bias", "g_gdn_out", "w_o_gdn", "w_out"]


def kernel(**inputs):
    import numpy as _np
    import concourse.bacc as _bacc
    from concourse import mybir as _mybir
    from concourse.bass_utils import run_bass_kernel_spmd as _run

    nc = _bacc.Bacc("TRN2", target_bir_lowering=False, num_devices=1)
    arrays, args = {}, []
    for name in _INS + ["consts"]:
        a = shape_constants() if name == "consts" else _np.ascontiguousarray(inputs[name])
        arrays[f"in_{name}_dram"] = a
        args.append(nc.dram_tensor(f"in_{name}_dram", a.shape, _mybir.dt.from_np(a.dtype), kind="ExternalInput").ap())
    args.append(nc.dram_tensor("out_dram", inputs["x"].shape, _mybir.dt.float32, kind="ExternalOutput").ap())
    hybrid_block(nc, *args)
    r = _run(nc, [arrays], core_ids=[0])
    return r.results[0]["out_dram"]
```

```python
from contextlib import ExitStack

import numpy as np

import concourse.bass as bass
from concourse import mybir

F32 = mybir.dt.float32
F32R = mybir.dt.float32r
I32 = mybir.dt.int32
ALU = mybir.AluOpType
ACT = mybir.ActivationFunctionType
AX = mybir.AxisListType.X

P = 128
RING = 4
ROWS = 2
COLS = 512
DVE_LEAD = 2
ACT_LEAD = 3
NEG = -1.0e30
CHUNK = 64
LEVELS = (1, 2, 4, 8, 16, 32)

C_IDENT = 0
C_MASK = C_IDENT + P
C_CAUSAL = C_MASK + 3 * P
C_LEVEL = C_CAUSAL + P
C_SAME = C_LEVEL + len(LEVELS) * P
C_HALF = C_SAME + P
C_FREQ = C_HALF + 2 * P
C_EPS = C_FREQ + 32
C_ALL = C_EPS + 2


def shape_constants():
    c = np.zeros((P, C_ALL), np.float32)
    i = np.arange(P)
    c[:, C_IDENT:C_IDENT + P] = np.eye(P)
    for block, at in ((0, C_MASK), (1, C_MASK + P)):
        keys = np.arange((block + 1) * P)
        hidden = (keys[None, :] // CHUNK) > ((block * P + i)[:, None] // CHUNK)
        c[:, at:at + keys.size] = np.where(hidden, NEG, 0.0)
    same = (i[:, None] // CHUNK) == (i[None, :] // CHUNK)
    c[:, C_CAUSAL:C_CAUSAL + P] = same & (i[:, None] <= i[None, :])
    c[:, C_SAME:C_SAME + P] = same
    for n, s in enumerate(LEVELS):
        low = (i[:, None] // (2 * s) == i[None, :] // (2 * s)) & (i[:, None] % (2 * s) >= s) & (i[None, :] % (2 * s) < s)
        c[:, C_LEVEL + n * P:C_LEVEL + (n + 1) * P] = low.T if n == 0 else low
    c[:CHUNK, C_HALF:C_HALF + P] = 1.0
    c[CHUNK:, C_HALF + P:C_HALF + 2 * P] = 1.0
    c[:, C_FREQ:C_FREQ + 32] = (10000.0 ** (-np.arange(0, 64, 2, dtype=np.float32) / np.float32(64))).astype(np.float32)
    c[:, C_EPS] = 1e-6
    c[:, C_EPS + 1] = 1.0
    return c


class Count:

    def __init__(self, sem):
        self.sem, self.base = sem, 0

    def phase(self, names, repeats=1):
        p = Phase(self, names.split(), self.base)
        self.base += len(p.names) * repeats
        return p


class Phase:

    def __init__(self, count, names, base):
        self.names, self.base, self.at = names, base, 0
        assert len(set(names)) == len(names)

    def after(self, name, turn=0):
        return turn * len(self.names) + (self.base + self.names.index(name) + 1)

    def one(self, name):
        assert self.names[self.at] == name, (self.names[self.at], name)
        self.at = (self.at + 1) % len(self.names)
        return 1


class Arena:

    def __init__(self, nc, base, end):
        self.nc, self.at, self.end = nc, base, end

    def take(self, name, shape, dtype=F32):
        n = int(np.prod(shape[1:])) * 4
        t = self.nc.alloc_sbuf_tensor_at(name, shape, dtype, offset=self.at)
        self.at += (n + 31) // 32 * 32
        assert self.at <= self.end, (name, self.at, self.end)
        return t


def hybrid_block(nc, x, positions, w_norm, w_in, b_gate, w_q_up, w_kv_up, g_q_latent, g_kv_latent, g_q_head,
                 g_k_head, w_o_mla, conv_w, a_log, dt_bias, g_gdn_out, w_o_gdn, w_out, consts, out):
    _, S, D = x.shape
    TB = S // P
    RQ, RKV = w_q_up.shape[0], w_kv_up.shape[0]
    H = a_log.shape[0]
    QK = g_q_head.shape[0]
    NOPE, ROPE, DV = P, QK - P, P
    HALF = ROPE // 2
    W = w_o_mla.shape[0]
    TAPS = conv_w.shape[0]
    assert TB == 2 and D == 4096 and H == 16 and QK == 192 and W == H * DV
    O_C = 0
    O_ROPE = RQ + RKV
    O_Z = O_ROPE + ROPE
    O_QKV = O_Z + W
    O_BA = O_QKV + 3 * W
    O_ZG = O_BA + 2 * H
    O_GATE = O_ZG + W
    KD, KQ, KKV, KW = D // P, RQ // P, RKV // P, W // P

    xf = x.rearrange("a s d -> (a s) d")
    outf = out.rearrange("a s d -> (a s) d")
    tok = lambda a: a.rearrange("(t p) n -> p t n", p=P)
    rows = lambda a: a.rearrange("(k p) n -> p k n", p=P)

    z_d = nc.dram_tensor("z_scratch", (S, W), F32).ap()
    q_d = nc.dram_tensor("q_scratch", (S, H * QK), F32).ap()
    kv_d = nc.dram_tensor("kv_scratch", (S, H * 2 * P), F32).ap()
    g_d = nc.dram_tensor("g_scratch", (S + TAPS - 1, 3 * W), F32).ap()
    conv_d = nc.dram_tensor("conv_scratch", (S, H, 3, DV), F32).ap()
    zg_d = nc.dram_tensor("zg_scratch", (S, W), F32).ap()
    gate_d = nc.dram_tensor("gate_scratch", (S, 2 * D), F32).ap()
    row_d = nc.dram_tensor("row_scratch", (2, H, S), F32).ap()
    mix_d = [nc.dram_tensor(f"mix_scratch{i}", (P, H, S), F32).ap() for i in range(4)]

    with ExitStack() as ctx:
        sb = lambda name, shape, dt=F32: ctx.enter_context(nc.sbuf_tensor(name, shape, dt))
        sem = lambda name: ctx.enter_context(nc.semaphore(name))

        xT = [sb("xT_hi", [P, KD, S], F32R), sb("xT_lo", [P, KD, S], F32R)]
        raw = sb("raw_ring", [P, RING, ROWS * COLS])
        whi = sb("hi_ring", [P, RING, ROWS * COLS], F32R)
        wlo = sb("lo_ring", [P, RING, ROWS * COLS], F32R)
        stage = sb("stage", [P, 2, TB, COLS])
        cst = sb("cst", [P, C_ALL])
        misc = sb("misc", [P, TB, ROPE + 2 * H])
        gcol = sb("gcol", [P, KD + KQ + KKV])
        gqk = sb("gqk", [P, 2, QK])
        ggo = sb("ggo", [P, DV])
        trig = sb("trig", [P, 2, TB, HALF])
        ss = sb("ss", [P, 16])
        rx = sb("rx", [P, TB])
        rs = sb("rs", [P, 16])
        beta = sb("beta", [P, H, TB])
        gc = sb("gc", [P, H, TB])
        egc = sb("egc", [P, H, TB])
        ekd = sb("ekd", [P, H, TB])
        glast = sb("glast", [P, H, 2 * TB])
        slab_base = nc.sbuf_base
        slab_end = nc.sbuf_usable_end
        area = lambda: Arena(nc, slab_base, slab_end)

        a0 = area()
        xin = a0.take("xin", [P, TB, D])
        junk = a0.take("junk", [P, COLS])
        graw = a0.take("graw", [KD + KQ + KKV, P])
        a1 = area()
        craw = a1.take("craw", [P, TB, RQ + RKV])
        cjunk = a1.take("cjunk", [P, RQ])
        cT = [a1.take("cT_hi", [P, KQ + KKV, S], F32R), a1.take("cT_lo", [P, KQ + KKV, S], F32R)]
        alg = a1.take("alg", [P, 2, H])
        pos_i = a1.take("pos_i", [P, TB], I32)
        pos_f = a1.take("pos_f", [P, TB])
        ang = a1.take("ang", [P, 2, TB, HALF])
        whole = a1.take("whole_turns", [P, 2, TB, HALF])
        av = a1.take("av", [P, 4, TB, H])
        gth = a1.take("gth", [P, 2, TB, H])
        gcT = a1.take("gcT", [H, 2, S])
        zrow = a1.take("zrow", [72, 256])
        miscT = a1.take("miscT", [ROPE + 2 * H, S])

        ab = area()
        qk = ab.take("qk", [P, 2, TB, 2, QK])
        vt = ab.take("vt", [P, TB, 2, DV])
        zs = ab.take("zs", [P, TB, 2, DV])
        sq = ab.take("sq", [P, 2, TB, 2, QK])
        qkTa = ab.take("qkTa", [P, 2, 2, TB * P])
        qkTb = ab.take("qkTb", [ROPE, 2, 2, TB * P])
        sc = ab.take("sc", [P, 2, 3 * P])
        pT = ab.take("pT", [P, 2, 3 * P])
        og = ab.take("og", [P, TB, 2, DV])
        rt = ab.take("rt", [P, 4, 4 * TB, HALF])
        mx = ab.take("mx", [P, 3, TB, 2])
        xs = ab.take("xs", [P, TAPS, TB, COLS])
        cw = ab.take("cw", [P, TAPS, COLS])
        mT = [ab.take("mT_hi", [P, 2, S], F32R), ab.take("mT_lo", [P, 2, S], F32R)]

        ac = area()
        cv = ac.take("cv", [P, TB, 2, 3, DV])
        sl = ac.take("sl", [P, 2 * TB, 4, DV])
        tt = ac.take("tt", [P, 2 * TB, 2, P])
        wT = ac.take("wT", [P, 2 * TB, DV])
        kbe = ac.take("kbe", [P, 2 * TB, DV])
        kd = ac.take("kd", [P, 2 * TB, DV])
        rowb = ac.take("rowb", [P, 2, 2 * TB, P])
        erow = ac.take("erow", [P, 2 * TB, P])
        pq = ac.take("pq", [P, 2 * TB, 2, P])
        qeT = ac.take("qeT", [P, 2 * TB, 3, P])
        dec = ac.take("dec", [P, 2 * TB, P])
        lt = ac.take("lt", [P, 2 * TB, P])
        m1 = ac.take("m1", [P, 2 * TB, P])
        st = ac.take("st", [P, 2, 2, DV])
        bb = ac.take("bb", [P, 2, COLS])
        cf = ac.take("cf", [P, 8, 2 * TB])
        gT = [ac.take("gT_hi", [P, 2, S], F32R), ac.take("gT_lo", [P, 2, S], F32R)]

        ad = area()
        oT = [ad.take(f"oT{i}", [P, H, S], F32R) for i in range(3)]
        hb = ad.take("hb", [P, TB, COLS])
        ad.at = max(ad.at, ac.at)
        oT.insert(0, ad.take("oT3", [P, H, S], F32R))
        ae = area()
        xr = ae.take("xr", [P, 2, TB, COLS])

        acc = [ctx.enter_context(nc.psum_tensor(f"acc{i}", [P, TB, COLS], F32)) for i in range(2)]
        side = ctx.enter_context(nc.psum_tensor("side", [P, 4, COLS], F32))

        ident = cst[:, C_IDENT:C_IDENT + P]
        causal = cst[:, C_CAUSAL:C_CAUSAL + P]
        level = lambda n: cst[:, C_LEVEL + n * P:C_LEVEL + (n + 1) * P]
        eps = cst[:, C_EPS:C_EPS + 1]
        one = cst[:, C_EPS + 1:C_EPS + 2]

        landed = [sem(f"raw_landed{i}") for i in range(RING)]
        hi_done = sem("hi_done")
        lo_done = sem("lo_done")
        tile_used = sem("tile_used")
        emptied = [sem(f"acc_emptied{i}") for i in range(2)]
        gated = [sem(f"acc_gated{i}") for i in range(2)]
        summed = [sem(f"acc_summed{i}") for i in range(2)]
        stored = [sem(f"stage_stored{i}") for i in range(2)]
        s_ident = sem("ident_landed")
        s_const = sem("consts_landed")
        s_x = [sem(f"x_landed{i}") for i in range(D // COLS)]
        s_gain = sem("gains_landed")
        s_bc = sem("rows_landed")
        s_row = sem("scalar_rows_landed")
        s_zero = sem("zero_rows_stored")
        s_gc = sem("gc_stored")
        s_mix = [sem(f"mix_stored{i}") for i in range(4)]
        s_qk = sem("qk_loaded")
        s_v = sem("v_loaded")
        s_zs = sem("zs_loaded")
        s_tap = sem("taps_loaded")
        s_conv = sem("conv_stored")
        s_cv = sem("conv_loaded")
        s_zg = sem("zg_loaded")
        s_gcb = sem("gc_rows_loaded")
        s_bb = sem("gate_bias_loaded")
        s_oT = [sem(f"mix_loaded{i}") for i in range(4)]
        s_gate = [sem(f"gate_loaded{i}") for i in range(2)]
        s_xr = [sem(f"residual_loaded{i}") for i in range(2)]
        s_out = [sem(f"out_stored{i}") for i in range(2)]
        pe_done, act_done, dve_done, pool_done = sem("pe_done"), sem("act_done"), sem("dve_done"), sem("pool_done")
        cp, ca, cd, cg = Count(pe_done), Count(act_done), Count(dve_done), Count(pool_done)

        NG = KD // 2
        NC = (KQ + KKV) // 2
        seq = lambda name, n: " ".join(f"{name}{i}" for i in range(n))
        P0 = cp.phase("gains " + seq("x", NG))
        SQ_AT = 4
        X_LEAD = 3
        A0 = ca.phase(seq("hi", X_LEAD) + " " +
                      " ".join((f"hi{i + X_LEAD} " if i + X_LEAD < NG else "") + (f"sq{i - SQ_AT}" if i >= SQ_AT else "")
                               for i in range(SQ_AT + D // COLS * TB)) + " ln rstd")
        D0 = cd.phase("gcol " + seq("lo", NG) + " sumx")
        P1 = cp.phase("misc cum gct " + seq("c", NC))
        A1 = ca.phase("sumsq0 sumsq1 sumsq2 sumsq3 misc lnq lnkv rstd beta expa expx lnx sin egc ekd glast " + seq("hi", NC))
        D1 = cd.phase("pos ang0 ang1 u0 u1 r0 r1 s1 s2 s3 s4 s5 adt nabs norm0 norm1 norm2 norm3 sp g "
                      "gc gth gth2 kdx gct " + seq("lo", NC))
        G1 = cg.phase("zero")
        TURNS = H // 2
        PB = cp.phase("heads scores probs values turn", TURNS)
        AB = ca.phase("rope sq ln rstd headsT expA expB expC expD probsT hi", TURNS)
        DB = cd.phase("sum unit gain r1 r2 r3 r4 r5 r6 ropeT mask max0 max1 neg rden div gate lo", TURNS)
        lv = range(1, len(LEVELS))
        PC = cp.phase("turns products t1 " + " ".join(f"ma{n} mb{n}" for n in lv) +
                      " solve kv0 ws1 kv1 ws2 kv2 ws3 out1 turn", TURNS)
        AC = ca.phase("silu square exp ln rstd erow kT " + " ".join(f"tT{n}" for n in lv if n > 1) +
                      " wT osq oln orstd hi", TURNS)
        DZ = cd.phase("zero")
        DC = cd.phase("sum cq kn qn cke kbe qeT qT lt attn l1 tt1 t1 " +
                      " ".join(f"ma{n} mb{n}" for n in lv) +
                      " u s1 v1 s2a s2b v2 s3a s3b v3 osum on ogate lo", TURNS)
        GB = cg.phase("m0 m1 m2 m3 a1 a2 a3", 12)
        GC = cg.phase("diff below mask decb vb kd gz", TURNS)
        PD = cp.phase("turn", TURNS)
        AD = ca.phase("hi", TURNS)
        DD = cd.phase("h3 lo", TURNS)

        T_MISC = 3 * KD // ROWS
        T_Z = T_MISC + RING
        T_Q = T_Z + (W // COLS) * KD // ROWS
        T_KV = T_Q + (H * QK // COLS) * KQ // ROWS
        T_B = T_KV + (H * 2 * P // COLS) * KKV // ROWS
        T_ZG = T_B + 12 * KD // ROWS
        T_C = T_ZG + (W // COLS) * KD // ROWS
        T_D = T_C + 16 * KD // ROWS
        T_E = T_D + 8 * 2 * KW // ROWS
        T_END = T_E + 8 * KD // ROWS
        MK = KD // RING
        MN = ROPE + 2 * H
        BEFORE = dict(Z=(2, 2), Q=(4, 4), KV=(7, 7), B=(11, 11), ZG=(19, 15), C=(21, 17))

        def landed_value(turn, t0, s):
            return turn * 16 + (16 * ((t0 + s) // RING + 1) + (16 if t0 >= T_MISC else 0))

        def width(t):
            return MK * MN if T_MISC <= t < T_Z else ROWS * COLS

        block = ctx.enter_context(nc.Block())

        @block.sync
        def _(sp):
            sp.dma_start(cst[:, 0:P], consts[:, 0:P]).then_inc(s_ident, 16)

            def load(t0, turn, per, s, src):
                if not (isinstance(turn, int) and t0 + turn * per + s < RING):
                    sp.wait_ge(lo_done, turn * per + (t0 + s - RING + 1))
                for dst, a in src:
                    sp.dma_start(dst, a).then_inc(landed[s % RING], 16)

            def tile(w, k0, col, s):
                return [(raw[:, s % RING, :].rearrange("p (k n) -> p k n", k=ROWS),
                         rows(w)[:, k0:k0 + ROWS, bass.ds(col, COLS)])]

            def chunks(t0, n, w, col0, kn, per_turn=2):
                per = per_turn * kn // ROWS
                with sp.Fori(0, n // per_turn) as i:
                    for c in range(per_turn):
                        for k in range(kn // ROWS):
                            s = c * (kn // ROWS) + k
                            load(t0, i, per, s, tile(w, k * ROWS, i * (per_turn * COLS) + (col0 + c * COLS), s))

            KT = KD // ROWS
            for s in range(KT):
                load(0, 0, KT, s, tile(w_in, s * ROWS, O_C, s))
                if s == RING - 1:
                    sp.dma_start(cst[:, P:C_ALL], consts[:, P:C_ALL]).then_inc(s_const, 16)
            with sp.Fori(1, 3) as i:
                for s in range(KT):
                    load(0, i, KT, s, tile(w_in, s * ROWS, i * COLS + O_C, s))
            for s in range(RING):
                dst = raw[:, s, 0:MK * MN].rearrange("p (k n) -> p k n", k=MK)
                src = rows(w_in)[:, s * MK:(s + 1) * MK, :]
                load(T_MISC, 0, RING, s, [(dst[:, :, 0:ROPE], src[:, :, O_ROPE:O_ROPE + ROPE]),
                                          (dst[:, :, ROPE:MN], src[:, :, O_BA:O_BA + 2 * H])])
            chunks(T_Z, W // COLS, w_in, O_Z, KD)
            chunks(T_Q, H * QK // COLS, w_q_up, 0, KQ)
            chunks(T_KV, H * 2 * P // COLS, w_kv_up, 0, KKV)
            with sp.Fori(0, 4) as i:
                for s in range(3 * KT):
                    load(T_B, i, 3 * KT, s, tile(w_in, (s % KT) * ROWS, i * COLS + (O_QKV + (s // KT) * W), s))
                    if s % 24 == 6:
                        half = s // 24
                        for q in stored:
                            sp.wait_ge(q, 16 * 10)
                        sp.wait_ge(pe_done, PB.after("heads", i * 2 + (half - 1)))
                        sp.dma_start(qk[:, 0].rearrange("p t h n -> p t (h n)"),
                                     tok(q_d)[:, :, bass.ds(i * (4 * QK) + half * 2 * QK, 2 * QK)]).then_inc(s_qk, 16)
                        for h in range(2):
                            sp.dma_start(qk[:, 1, :, h, 0:NOPE],
                                         tok(kv_d)[:, :, bass.ds(i * (8 * P) + (half * 4 + h * 2) * P, P)]).then_inc(s_qk, 16)
                        sp.wait_ge(dve_done, DB.after("gate", i * 2 + (half - 1)))
                        for h in range(2):
                            sp.dma_start(vt[:, :, h, :],
                                         tok(kv_d)[:, :, bass.ds(i * (8 * P) + (half * 4 + h * 2 + 1) * P, P)]).then_inc(s_v, 16)
                        sp.dma_start(zs[:].rearrange("p t h n -> p t (h n)"),
                                     tok(z_d)[:, :, bass.ds(i * (4 * DV) + half * 2 * DV, 2 * DV)]).then_inc(s_zs, 16)
            chunks(T_ZG, W // COLS, w_in, O_ZG, KD)
            with sp.Fori(0, TURNS) as i:
                for s in range(2 * KT):
                    load(T_C, i, 2 * KT, s, tile(w_in, (s % KT) * ROWS, i * (2 * COLS) + (O_GATE + (s // KT) * COLS), s))
                    if s == 0:
                        sp.wait_ge(s_conv, 16 * 2 * 12)
                        for q in s_mix[0:2]:
                            sp.wait_ge(q, 16 * (TURNS + 1))
                        sp.wait_ge(act_done, AC.after("silu", i - 1))
                        sp.dma_start(cv[:].rearrange("p t h j n -> p t (h j n)"),
                                     conv_d.rearrange("(t p) h j n -> p t (h j n)", p=P)
                                     [:, :, bass.ds(i * (6 * DV), 6 * DV)]).then_inc(s_cv, 16)
                        sp.wait_ge(act_done, AC.after("erow", i - 1))
                        sp.wait_ge(pool_done, GC.after("decb", i - 1))
                        sp.dma_start(rowb[:].rearrange("p a b n -> p a (b n)"),
                                     row_d[:, bass.ds(i * 2, 2), :].rearrange("a h s -> a (h s)").partition_broadcast(P)).then_inc(s_gcb, 16)
                    if s == 8:
                        sp.wait_ge(stored[0], 16 * 20)
                        sp.wait_ge(stored[1], 16 * 16)
                        sp.wait_ge(pe_done, PC.after("turn", i - 1))
                        for h in range(2):
                            sp.dma_start(sl[:, h * TB:(h + 1) * TB, 3, :],
                                         tok(zg_d)[:, :, bass.ds(i * (2 * DV) + h * DV, DV)]).then_inc(s_zg, 16)
                        sp.dma_start(bb[:].rearrange("p a n -> p (a n)"),
                                     b_gate.rearrange("a n -> (a n)")[bass.ds(i * (2 * COLS), 2 * COLS)]
                                     .partition_broadcast(P)).then_inc(s_bb, 16)
            with sp.Fori(0, TURNS) as i:
                for s in range(2 * KW // ROWS):
                    w, k = (w_o_mla, s) if s < KW // ROWS else (w_o_gdn, s - KW // ROWS)
                    load(T_D, i, 2 * KW // ROWS, s, tile(w, k * ROWS, i * COLS, s))
            chunks(T_E, 8, w_out, 0, KD)

        @block.tensor
        def _(pe):
            def tiles(t0, turn, per, s0, s1, c, left, kn, k_at=0):
                for s in range(s0, s1):
                    pe.wait_ge(lo_done, turn * per + (t0 + s + 1))
                    for kk in range(ROWS):
                        k = (s * ROWS + kk) % kn
                        for tb in range(TB):
                            o = acc[c][:, tb, :]
                            lh = left[0][:, k_at + k, tb * P:(tb + 1) * P]
                            ll = left[1][:, k_at + k, tb * P:(tb + 1) * P]
                            rh = whi[:, s % RING, kk * COLS:(kk + 1) * COLS]
                            rl = wlo[:, s % RING, kk * COLS:(kk + 1) * COLS]
                            nc.tensor.matmul(o, lh, rh, start=(k == 0), stop=False)
                            nc.tensor.matmul(o, lh, rl, start=False, stop=False)
                            last = nc.tensor.matmul(o, ll, rh, start=False, stop=(k == kn - 1))
                    last.then_inc(tile_used, 1)

            def turn_group(src, g, name, phase, lo_phase):
                if g >= 4:
                    pe.wait_ge(dve_done, lo_phase.after(f"lo{g - 4}"))
                for kk in range(2):
                    for tb in range(TB):
                        k = 2 * g + kk
                        mm = nc.tensor.transpose(side[:, g % 4, kk * S + tb * P:kk * S + (tb + 1) * P],
                                                 src[:, tb, k * P:(k + 1) * P], ident)
                mm.then_inc(pe_done, phase.one(f"{name}{g}"))

            pe.sem_inc(tile_used, 1)
            pe.wait_ge(s_ident, 16)
            pe.wait_ge(s_gain, 48)
            NR = KD + KQ + KKV
            nc.tensor.transpose(acc[0][:, 0, 0:NR], graw[:, :], cst[0:NR, C_IDENT:C_IDENT + NR]).then_inc(pe_done, P0.one("gains"))
            KT = KD // ROWS

            def turn_x(g):
                pe.wait_ge(s_x[g // 2], 16)
                turn_group(xin, g, "x", P0, D0)

            for g in range(4):
                turn_x(g)
            for s in range(KT):
                pe.wait_ge(dve_done, D0.after(f"lo{s}"))
                tiles(0, 0, KT, s, s + 1, 0, xT, KD)
                if s + 4 < NG:
                    turn_x(s + 4)
            tiles(KT, 0, KT, 0, KT, 1, xT, KD)
            pe.wait_ge(emptied[0], 2)
            tiles(2 * KT, 0, KT, 0, KT, 0, xT, KD)
            pe.wait_ge(emptied[1], 2)
            for s in range(RING):
                pe.wait_ge(lo_done, T_MISC + s + 1)
                for kk in range(MK):
                    k = s * MK + kk
                    o = acc[1][0:MN, 0, 0:S]
                    wh, wl = (w[:, s % RING, kk * MN:(kk + 1) * MN] for w in (whi, wlo))
                    nc.tensor.matmul(o, wh, xT[0][:, k, :], start=(k == 0), stop=False)
                    nc.tensor.matmul(o, wh, xT[1][:, k, :], start=False, stop=False)
                    last = nc.tensor.matmul(o, wl, xT[0][:, k, :], start=False, stop=(k == KD - 1))
                last.then_inc(tile_used, 1)

            def plain(t0, n, left, kn, before, k_at=0):
                per = 2 * kn // ROWS
                with pe.Fori(0, n // 2) as i:
                    for c in range(2):
                        pe.wait_ge(emptied[c], i + (before[c] + 1))
                        tiles(t0, i, per, c * per // 2, (c + 1) * per // 2, c, left, kn, k_at=k_at)

            def turn_Z(i, first):
                for s in range(2 * KT):
                    if s % KT == 0:
                        pe.wait_ge(emptied[s // KT], i + (BEFORE["Z"][s // KT] + 1))
                    tiles(T_Z, i, 2 * KT, s, s + 1, s // KT, xT, KD)
                    if not first:
                        continue
                    if s == 1:
                        pe.wait_ge(emptied[1], 3)
                        for tb in range(TB):
                            mm = nc.tensor.transpose(side[:, 0, tb * MN:(tb + 1) * MN], miscT[:, tb * P:(tb + 1) * P], cst[0:MN, C_IDENT:C_IDENT + MN])
                        mm.then_inc(pe_done, P1.one("misc"))
                    if s == 9:
                        pe.wait_ge(dve_done, D1.after("g"))
                        pe.wait_ge(act_done, A1.after("misc"))
                        pe.wait_ge(s_const, 16)
                        for tb in range(TB):
                            g = av[:, 3, tb, :]
                            nc.tensor.matmul(side[:, 0, tb * H:(tb + 1) * H], causal, g, start=True, stop=True)
                            nc.tensor.matmul(side[:, 0, (2 + tb) * H:(3 + tb) * H], cst[:, C_SAME:C_SAME + P], g, start=True, stop=True)
                            for c in range(2):
                                mm = nc.tensor.matmul(side[:, 0, (4 + 2 * tb + c) * H:(5 + 2 * tb + c) * H],
                                                      cst[:, C_HALF + c * P:C_HALF + (c + 1) * P], g, start=True, stop=True)
                        mm.then_inc(pe_done, P1.one("cum"))
                    if s == 12:
                        pe.wait_ge(dve_done, D1.after("gth2"))
                        for a in range(2):
                            for tb in range(TB):
                                mm = nc.tensor.transpose(side[0:H, 1, a * S + tb * P:a * S + (tb + 1) * P], gth[:, a, tb, :], ident)
                        mm.then_inc(pe_done, P1.one("gct"))
                    if 15 <= s < 15 + NC:
                        pe.wait_ge(dve_done, D1.after("gct"))
                        pe.wait_ge(act_done, A1.after("glast"))
                        turn_group(craw, s - 15, "c", P1, D1)

            turn_Z(0, True)
            turn_Z(1, False)
            pe.wait_ge(dve_done, D1.after(f"lo{NC - 1}"))
            plain(T_Q, 6, cT, KQ, BEFORE["Q"])
            plain(T_KV, 8, cT, KKV, BEFORE["KV"], k_at=KQ)

            def attend(i, half, B):
                turn = i * 2 + half
                B(0, 10)
                pe.wait_ge(dve_done, DB.after("r6", turn))
                for s in range(2):
                    for h in range(2):
                        for tb in range(TB):
                            n = ((s * 2 + h) * TB + tb) * P
                            nc.tensor.transpose(side[:, n // COLS, n % COLS:n % COLS + P], qk[:, s, tb, h, 0:NOPE], ident)
                            mm = nc.tensor.transpose(side[0:ROPE, 2 + n // COLS, n % COLS:n % COLS + P],
                                                     qk[:, s, tb, h, NOPE:QK], ident)
                mm.then_inc(pe_done, PB.one("heads"))
                B(10, 12)
                pe.wait_ge(act_done, AB.after("headsT", turn))
                pe.wait_ge(dve_done, DB.after("ropeT", turn))
                for h in range(2):
                    for tb in range(TB):
                        o = side[:, h, tb * P:tb * P + (tb + 1) * P]
                        nc.tensor.matmul(o, qkTa[:, 0, h, tb * P:(tb + 1) * P], qkTa[:, 1, h, 0:(tb + 1) * P], start=True, stop=False)
                        mm = nc.tensor.matmul(o, qkTb[:, 0, h, tb * P:(tb + 1) * P], qkTb[:, 1, h, 0:(tb + 1) * P], start=False, stop=True)
                mm.then_inc(pe_done, PB.one("scores"))
                B(12, 15)
                pe.wait_ge(act_done, AB.after("expD", turn))
                for h in range(2):
                    for b in range(3):
                        mm = nc.tensor.transpose(side[:, 2 + h, b * P:(b + 1) * P], sc[:, h, b * P:(b + 1) * P], ident)
                mm.then_inc(pe_done, PB.one("probs"))
                B(15, 17)
                pe.wait_ge(act_done, AB.after("probsT", turn))
                pe.wait_ge(s_v, i * 64 + (half * 32 + 32))
                for tb in range(TB):
                    for h in range(2):
                        for kb_ in range(tb + 1):
                            mm = nc.tensor.matmul(side[:, 0, (tb * 2 + h) * P:(tb * 2 + h + 1) * P],
                                                  pT[:, h, (tb + kb_) * P:(tb + kb_ + 1) * P], vt[:, kb_, h, :],
                                                  start=(kb_ == 0), stop=(kb_ == tb))
                mm.then_inc(pe_done, PB.one("values"))
                B(17, 19)
                pe.wait_ge(dve_done, DB.after("gate", turn))
                for h in range(2):
                    for tb in range(TB):
                        mm = nc.tensor.transpose(side[:, 1, h * S + tb * P:h * S + (tb + 1) * P], og[:, tb, h, :], ident)
                mm.then_inc(pe_done, PB.one("turn"))
                B(19, 24)

            with pe.Fori(0, 4) as i:
                def B(half, s0, s1):
                    for s in range(24 * half + s0, 24 * half + s1):
                        if s == 0:
                            pe.wait_ge(emptied[0], i * 2 + (BEFORE["B"][0] + 1))
                        if s == KT:
                            pe.wait_ge(emptied[1], i + (BEFORE["B"][1] + 1))
                        if s == 2 * KT:
                            pe.wait_ge(emptied[0], i * 2 + (BEFORE["B"][0] + 2))
                        tiles(T_B, i, 3 * KT, s, s + 1, (s // KT) % 2, xT, KD)
                attend(i, 0, lambda a, b: B(0, a, b))
                attend(i, 1, lambda a, b: B(1, a, b))
            plain(T_ZG, W // COLS, xT, KD, BEFORE["ZG"])

            for c in range(2):
                pe.wait_ge(emptied[c], BEFORE["C"][c] + 1)
            pe.wait_ge(dve_done, DB.after("lo", TURNS - 1))
            with pe.Fori(0, TURNS) as i:
                C = lambda s: tiles(T_C, i, 2 * KT, s, s + 1, s // KT, xT, KD)
                col = lambda n: side[:, n // COLS, n % COLS:n % COLS + P]
                hb4 = range(2 * TB)
                pe.wait_ge(gated[0], i + 1)
                for s in range(4):
                    C(s)
                pe.wait_ge(dve_done, DC.after("qn", i))
                for n in range(2):
                    for b in hb4:
                        mm = nc.tensor.transpose(side[:, 2 + n, b * P:(b + 1) * P], sl[:, b, 1 - n, :], ident)
                mm.then_inc(pe_done, PC.one("turns"))
                C(4)
                C(5)
                pe.wait_ge(act_done, AC.after("kT", i))
                pe.wait_ge(dve_done, DC.after("qT", i))
                for b in hb4:
                    mm = nc.tensor.matmul(side[:, b // 2, (b % 2) * 2 * P:(b % 2 + 1) * 2 * P], pq[:, b, 0, :],
                                          pq[:, b].rearrange("p a n -> p (a n)"), start=True, stop=True)
                mm.then_inc(pe_done, PC.one("products"))
                C(6)
                C(7)
                pe.wait_ge(dve_done, DC.after("tt1", i))
                for b in hb4:
                    mm = nc.tensor.transpose(side[:, 2, b * P:(b + 1) * P], tt[:, b, 1, :], ident)
                mm.then_inc(pe_done, PC.one("t1"))
                s = 8
                before = "t1"
                for n in lv:
                    C(s)
                    pe.wait_ge(dve_done, DC.after(before, i))
                    for b in hb4:
                        mm = nc.tensor.matmul(side[:, 3, b * P:(b + 1) * P], lt[:, b, :], tt[:, b, 0, :], start=True, stop=True)
                    if n > 1:
                        for b in hb4:
                            mm = nc.tensor.transpose(side[:, 2, b * P:(b + 1) * P], tt[:, b, 0, :], ident)
                    mm.then_inc(pe_done, PC.one(f"ma{n}"))
                    C(s + 1)
                    pe.wait_ge(dve_done, DC.after(f"ma{n}", i))
                    if n > 1:
                        pe.wait_ge(act_done, AC.after(f"tT{n}", i))
                    for b in hb4:
                        if n < len(LEVELS) - 1:
                            left, right = tt[:, b, 1, :], m1[:, b, :]
                        else:
                            left, right = m1[:, b, :], tt[:, b, 1, :]
                        mm = nc.tensor.matmul(side[:, 0, b * P:(b + 1) * P], left, right, start=True, stop=True)
                    mm.then_inc(pe_done, PC.one(f"mb{n}"))
                    s += 2
                    before = f"mb{n}"
                    if s == KT:
                        pe.wait_ge(gated[1], i + 1)
                C(18)
                pe.wait_ge(dve_done, DC.after(before, i))
                pe.wait_ge(pool_done, GC.after("vb", i))
                for b in hb4:
                    nc.tensor.matmul(side[:, 2, b * P:(b + 1) * P], tt[:, b, 1, :], sl[:, b, 2, :], start=True, stop=True)
                    mm = nc.tensor.matmul(side[:, 3, b * P:(b + 1) * P], kbe[:, b, :], tt[:, b, 1, :], start=True, stop=True)
                mm.then_inc(pe_done, PC.one("solve"))

                def state_add(c, name):
                    r = slice((c % 2) * CHUNK, (c % 2 + 1) * CHUNK)
                    for h in range(2):
                        b = h * TB + c // 2
                        mm = nc.tensor.matmul(side[:, 1, h * P:(h + 1) * P], kd[r, b, :], sl[r, b, 2, :], start=True, stop=True)
                    return mm

                def from_state(c, name):
                    for h in range(2):
                        b = h * TB + c // 2
                        mm = nc.tensor.matmul(side[:, 0, h * P:(h + 1) * P], wT[:, b, :], st[:, c % 2, h, :], start=True, stop=True)
                    mm.then_inc(pe_done, PC.one(name))

                def block_out(tb):
                    for h in range(2):
                        b = h * TB + tb
                        o = side[:, 2, (tb * 2 + h) * P:(tb * 2 + h + 1) * P]
                        cs = [c for c in (2 * tb, 2 * tb + 1) if c > 0]
                        flat = qeT[:, b].rearrange("p a n -> p (a n)")
                        for c in cs:
                            nc.tensor.matmul(o, flat[:, (c % 2) * P:(c % 2) * P + P], st[:, c % 2, h, :], start=(c == cs[0]), stop=False)
                        mm = nc.tensor.matmul(o, dec[:, b, :], sl[:, b, 2, :], start=False, stop=True)
                    return mm

                C(19)
                pe.wait_ge(dve_done, DC.after("u", i))
                pe.wait_ge(pool_done, GC.after("kd", i))
                state_add(0, "kv0").then_inc(pe_done, PC.one("kv0"))
                C(20)
                pe.wait_ge(act_done, AC.after("wT", i))
                pe.wait_ge(dve_done, DC.after("s1", i))
                from_state(1, "ws1")
                C(21)
                pe.wait_ge(dve_done, DC.after("v1", i))
                block_out(0)
                state_add(1, "kv1").then_inc(pe_done, PC.one("kv1"))
                C(22)
                pe.wait_ge(dve_done, DC.after("s2b", i))
                from_state(2, "ws2")
                C(23)
                pe.wait_ge(dve_done, DC.after("v2", i))
                state_add(2, "kv2").then_inc(pe_done, PC.one("kv2"))
                C(24)
                pe.wait_ge(dve_done, DC.after("s3b", i))
                from_state(3, "ws3")
                C(25)
                pe.wait_ge(dve_done, DC.after("v3", i))
                block_out(1).then_inc(pe_done, PC.one("out1"))
                for s in range(26, 29):
                    C(s)
                pe.wait_ge(dve_done, DC.after("ogate", i))
                for h in range(2):
                    for tb in range(TB):
                        mm = nc.tensor.transpose(side[:, 3, h * S + tb * P:h * S + (tb + 1) * P], sl[:, h * TB + tb, 3, :], ident)
                mm.then_inc(pe_done, PC.one("turn"))
                for s in range(29, 32):
                    C(s)

            KO = KW // ROWS

            def turn_h(i_prev):
                pe.wait_ge(dve_done, DD.after("h3", i_prev))
                for k in range(4):
                    for tb in range(TB):
                        mm = nc.tensor.transpose(side[:, k // 2, (k % 2) * S + tb * P:(k % 2) * S + (tb + 1) * P],
                                                 hb[:, tb, k * P:(k + 1) * P], ident)
                mm.then_inc(pe_done, PD.one("turn"))

            for q in s_oT[0:2]:
                pe.wait_ge(q, 16)
            pe.wait_ge(gated[0], TURNS + 1)
            tiles(T_D, 0, 2 * KO, 0, KO, 0, oT[0:2], KW)
            for q in s_oT[2:4]:
                pe.wait_ge(q, 16)
            pe.wait_ge(gated[1], TURNS + 1)
            tiles(T_D, 0, 2 * KO, KO, 2 * KO, 1, oT[2:4], KW)
            with pe.Fori(1, TURNS) as i:
                pe.wait_ge(gated[0], i + (TURNS + 1))
                tiles(T_D, i, 2 * KO, 0, 3, 0, oT[0:2], KW)
                turn_h(i - 1)
                tiles(T_D, i, 2 * KO, 3, KO, 0, oT[0:2], KW)
                pe.wait_ge(gated[1], i + (TURNS + 1))
                tiles(T_D, i, 2 * KO, KO, 2 * KO, 1, oT[2:4], KW)
            turn_h(TURNS - 1)
            pe.wait_ge(dve_done, DD.after("lo", TURNS - 1))
            with pe.Fori(0, 4) as i:
                pe.wait_ge(summed[0], i + 1)
                tiles(T_E, i, 2 * KT, 0, KT, 0, xT, KD)
                pe.wait_ge(summed[1], i + 1)
                tiles(T_E, i, 2 * KT, KT, 2 * KT, 1, xT, KD)

        @block.scalar
        def _(act):
            def hi(t0, turn, per, s):
                act.wait_ge(landed[s % RING], landed_value(turn * (per // RING), t0, s))
                if not (isinstance(turn, int) and t0 + turn * per + s < RING):
                    act.wait_ge(tile_used, turn * per + (t0 + s - RING + 2))
                w = width(t0 + s)
                nc.scalar.copy(whi[:, s % RING, 0:w], raw[:, s % RING, 0:w]).then_inc(hi_done, 1)

            def rsqrt(dst, src, n, phase, ln, rstd, i=0):
                nc.scalar.activation(dst, src, ACT.Ln, bias=eps, scale=1.0 / n).then_inc(act_done, phase.one(ln))
                act.wait_ge(act_done, phase.after(ln, i))
                nc.scalar.activation(dst, dst, ACT.Exp, scale=-0.5).then_inc(act_done, phase.one(rstd))

            for q in emptied:
                act.sem_inc(q, 1)
            for q in (*stored, *s_mix, *s_out):
                act.sem_inc(q, 16)
            NR = KD + KQ + KKV
            act.dma_start(graw[0:KD, :], w_norm.rearrange("(k p) -> k p", p=P)).then_inc(s_gain, 16)
            act.dma_start(graw[KD:KD + KQ, :], g_q_latent.rearrange("(k p) -> k p", p=P)).then_inc(s_gain, 16)
            act.dma_start(graw[KD + KQ:NR, :], g_kv_latent.rearrange("(k p) -> k p", p=P)).then_inc(s_gain, 16)
            for n in range(D // COLS):
                act.dma_start(xin[:, :, n * COLS:(n + 1) * COLS], tok(xf)[:, :, n * COLS:(n + 1) * COLS]).then_inc(s_x[n], 16)
            act.dma_start(gqk[:, 0, :], g_q_head.partition_broadcast(P)).then_inc(s_bc, 16)
            act.dma_start(gqk[:, 1, :], g_k_head.partition_broadcast(P)).then_inc(s_bc, 16)
            act.dma_start(ggo[:], g_gdn_out.partition_broadcast(P)).then_inc(s_bc, 16)

            def turn_hi(g, src_phase, name, dst, g0, phase):
                act.wait_ge(pe_done, src_phase.after(f"{name}{g}"))
                for kk in range(2):
                    k = 2 * g + kk
                    ins = nc.scalar.activation(dst[:, k, :], side[:, g % 4, kk * S:(kk + 1) * S], ACT.Copy,
                                               scale=gcol[:, g0 + k:g0 + k + 1])
                ins.then_inc(act_done, phase.one(f"hi{g}"))

            def scaled(dst, src, func=ACT.Copy):
                for tb in range(TB):
                    ins = nc.scalar.activation(dst[:, tb, :], src[:, tb, :], func, scale=rx[:, tb:tb + 1])
                return ins

            KT = KD // ROWS
            act.wait_ge(dve_done, D0.after("gcol"))
            for s in range(ACT_LEAD):
                turn_hi(s, P0, "x", xT[0], 0, A0)
                hi(0, 0, RING, s)
            for s in range(2 * KT):
                hi(0, 0, RING, s + ACT_LEAD)
                if s + X_LEAD < NG:
                    turn_hi(s + X_LEAD, P0, "x", xT[0], 0, A0)
                q = s - SQ_AT
                if 0 <= q < D // COLS * TB:
                    n, tb = q // TB, q % TB
                    act.wait_ge(s_x[n], 16)
                    if q:
                        act.wait_ge(act_done, A0.after(f"sq{q - 1}"))
                    nc.scalar.activation(junk[:], xin[:, tb, n * COLS:(n + 1) * COLS], ACT.Square,
                                         accum_out=ss[:, tb * (D // COLS) + n:tb * (D // COLS) + n + 1]).then_inc(act_done, A0.one(f"sq{q}"))
                if s == SQ_AT + D // COLS * TB:
                    act.wait_ge(dve_done, D0.after("sumx"))
                    act.wait_ge(s_const, 16)
                    rsqrt(rx[:], rx[:], D, A0, "ln", "rstd")
                    act.wait_ge(tile_used, KT + 1)
                    act.wait_ge(dve_done, D0.after(f"lo{NG - 1}"))
                    act.wait_ge(act_done, A0.after("rstd"))
                    scaled(craw[:, :, 0:COLS], acc[0]).then_inc(emptied[0], 1)
            act.wait_ge(tile_used, 2 * KT + 1)
            scaled(craw[:, :, COLS:2 * COLS], acc[1]).then_inc(emptied[1], 1)
            for s in range(2 * KT, 3 * KT):
                hi(0, 0, RING, s + ACT_LEAD) if s + ACT_LEAD < T_MISC else hi(T_MISC, 0, RING, s + ACT_LEAD - T_MISC)
            act.wait_ge(tile_used, T_MISC + 1)
            scaled(craw[:, :, 2 * COLS:3 * COLS], acc[0]).then_inc(emptied[0], 1)
            hi(T_MISC, 0, RING, ACT_LEAD)
            for s in range(3):
                hi(T_Z, 0, RING, s)
            act.wait_ge(tile_used, T_Z + 1)
            nc.scalar.copy(miscT[:], acc[1][0:MN, 0, 0:S]).then_inc(emptied[1], 1)

            def plain(t0, n, kn, dst, n_emptied, n_stored, func):
                per = 2 * kn // ROWS
                with act.Fori(0, n // 2) as i:
                    for s in range(per):
                        hi(t0, i, per, s + ACT_LEAD)
                        if (s + 1) % (per // 2) == 0:
                            c = s // (per // 2)
                            store(i * per + (t0 + s + 1), c, i + n_emptied[c], i * 16 + 16 * n_stored[c], dst,
                                  i * (2 * COLS) + c * COLS, func)

            def store(used, c, n_emptied, n_stored, dst, col, func):
                act.wait_ge(tile_used, used + 1)
                act.wait_ge(stored[c], n_stored + 16)
                if func is None:
                    nc.scalar.copy(stage[:, c], acc[c][:]).then_inc(emptied[c], 1)
                else:
                    scaled(stage[:, c], acc[c], func).then_inc(emptied[c], 1)
                act.wait_ge(emptied[c], n_emptied + 2)
                act.dma_start(tok(dst)[:, :, bass.ds(col, COLS)], stage[:, c]).then_inc(stored[c], 16)

            def turn_Z(i, first):
                for s in range(2 * KT):
                    hi(T_Z, i, 2 * KT, s + ACT_LEAD)
                    if (s + 1) % KT == 0:
                        c = s // KT
                        store(i * (2 * KT) + (T_Z + s + 1), c, i + BEFORE["Z"][c], i * 16, z_d, i * (2 * COLS) + c * COLS, ACT.Silu)
                    if not first:
                        continue
                    if s < 2:
                        act.wait_ge(emptied[0], 3)
                        act.wait_ge(emptied[1], 3)
                        for tb in range(TB):
                            n = 2 * s + tb
                            a, b = ((0, RQ), (RQ, RQ + RKV))[s]
                            if n:
                                act.wait_ge(act_done, A1.after(f"sumsq{n - 1}"))
                            nc.scalar.activation(cjunk[:, 0:b - a], craw[:, tb, a:b], ACT.Square,
                                                 accum_out=ss[:, n:n + 1]).then_inc(act_done, A1.one(f"sumsq{n}"))
                    if s == 2:
                        act.wait_ge(pe_done, P1.after("misc"))
                        scaled(misc, side[:, 0, 0:TB * MN].rearrange("p (t n) -> p t n", n=MN)).then_inc(act_done, A1.one("misc"))
                    if s == 3:
                        act.wait_ge(act_done, A1.after("sumsq3"))
                        nc.scalar.activation(rs[:, 0:2], ss[:, 0:2], ACT.Ln, bias=eps, scale=1.0 / RQ).then_inc(act_done, A1.one("lnq"))
                        nc.scalar.activation(rs[:, 2:4], ss[:, 2:4], ACT.Ln, bias=eps, scale=1.0 / RKV).then_inc(act_done, A1.one("lnkv"))
                        act.wait_ge(act_done, A1.after("lnkv"))
                        nc.scalar.activation(rs[:, 0:4], rs[:, 0:4], ACT.Exp, scale=-0.5).then_inc(act_done, A1.one("rstd"))
                    if s == 4:
                        act.wait_ge(act_done, A1.after("misc"))
                        nc.scalar.activation(beta[:].rearrange("p h t -> p t h"), misc[:, :, ROPE:ROPE + H], ACT.Sigmoid).then_inc(act_done, A1.one("beta"))
                        act.wait_ge(s_row, 48)
                        nc.scalar.activation(alg[:, 0, :], alg[:, 0, :], ACT.Exp).then_inc(act_done, A1.one("expa"))
                    if s == 6:
                        act.wait_ge(dve_done, D1.after("nabs"))
                        nc.scalar.activation(av[:, 1], av[:, 1], ACT.Exp).then_inc(act_done, A1.one("expx"))
                        act.wait_ge(act_done, A1.after("expx"))
                        nc.scalar.activation(av[:, 1], av[:, 1], ACT.Ln, bias=one).then_inc(act_done, A1.one("lnx"))
                    if s == 8:
                        nc.scalar.activation(trig[:], ang[:], ACT.Sin).then_inc(act_done, A1.one("sin"))
                    if s == 11:
                        act.wait_ge(pe_done, P1.after("cum"))
                        act.wait_ge(dve_done, D1.after("kdx"))
                        nc.scalar.activation(egc[:], gc[:], ACT.Exp).then_inc(act_done, A1.one("egc"))
                        nc.scalar.activation(ekd[:], ekd[:], ACT.Exp).then_inc(act_done, A1.one("ekd"))
                        nc.scalar.activation(glast[:].rearrange("p h c -> p c h"),
                                             side[:, 0, 4 * H:8 * H].rearrange("p (c h) -> p c h", h=H), ACT.Exp).then_inc(act_done, A1.one("glast"))
                    if s == 14:
                        act.wait_ge(dve_done, D1.after("gct"))
                        act.dma_start(row_d.rearrange("a h s -> h a s"), gcT[:]).then_inc(s_gc, 16)
                    if 16 <= s < 16 + NC:
                        turn_hi(s - 16, P1, "c", cT[0], KD, A1)

            turn_Z(0, True)
            turn_Z(1, False)
            plain(T_Q, 6, KQ, q_d, BEFORE["Q"], (2, 2), None)
            plain(T_KV, 8, KKV, kv_d, BEFORE["KV"], (5, 5), None)
            act.wait_ge(s_gc, 16)

            with act.Fori(0, 4) as i:
                for slot in range(3 * KT):
                    hi(T_B, i, 3 * KT, slot + ACT_LEAD)
                    half, s = slot // 24, slot % 24
                    turn = i * 2 + half
                    if s == 0:
                        act.wait_ge(pe_done, PB.after("heads", i * 2 + (half - 1)))
                        nc.scalar.copy(qk[:, 1, :, :, NOPE:QK],
                                       misc[:, :, 0:ROPE].unsqueeze(2).to_broadcast([P, TB, 2, ROPE])).then_inc(act_done, AB.one("rope"))
                    if s == 3:
                        act.wait_ge(s_qk, i * 96 + (48 * half + 48))
                        act.wait_ge(act_done, AB.after("rope", turn))
                        nc.scalar.activation(sq[:].rearrange("p a t h n -> p (a t h n)"), qk[:].rearrange("p a t h n -> p (a t h n)"),
                                             ACT.Square).then_inc(act_done, AB.one("sq"))
                    if s == 4:
                        act.wait_ge(dve_done, DB.after("sum", turn))
                        rsqrt(rs[:, 0:8], ss[:, 0:8], QK, AB, "ln", "rstd", turn)
                    if s == 9:
                        act.wait_ge(pe_done, PB.after("heads", turn))
                        nc.scalar.copy(qkTa[:].rearrange("p a h n -> p (a h n)"),
                                       side[:, 0:2, :].rearrange("p a n -> p (a n)")).then_inc(act_done, AB.one("headsT"))
                    if s == 12:
                        act.wait_ge(dve_done, DB.after("neg", turn))
                        for n, name in enumerate(("expA", "expB", "expC", "expD")):
                            tb, h = n // 2, n % 2
                            r = sc[:, h, tb * P:tb * P + (tb + 1) * P]
                            nc.scalar.activation(r, r, ACT.Exp, bias=mx[:, 1, tb, h:h + 1],
                                                 accum_out=mx[:, 2, tb, h:h + 1]).then_inc(act_done, AB.one(name))
                    if s == 14:
                        act.wait_ge(pe_done, PB.after("probs", turn))
                        nc.scalar.copy(pT[:], side[:, 2:4, 0:3 * P]).then_inc(act_done, AB.one("probsT"))
                    if (slot + 1) % KT == 0:
                        n = slot // KT
                        c = n % 2
                        store(i * (3 * KT) + (T_B + slot + 1), c, i * (2 - c) + (BEFORE["B"][c] + n // 2),
                              i * (16 * (2 - c)) + 16 * (9 + n // 2), g_d[TAPS - 1:TAPS - 1 + S, :], i * COLS + n * W, ACT.Copy)
                    if s == 18:
                        act.wait_ge(pe_done, PB.after("turn", turn))
                        for q in s_mix[0:2]:
                            act.wait_ge(q, i * 32 + (16 * half + 16))
                        nc.scalar.copy(mT[0][:].rearrange("p h n -> p (h n)"), side[:, 1, :]).then_inc(act_done, AB.one("hi"))
                    if s == 20:
                        act.wait_ge(dve_done, DB.after("lo", turn))
                        for n in range(2):
                            act.dma_start(mix_d[n][:, bass.ds(i * 4 + half * 2, 2), :], mT[n][:].bitcast(F32)).then_inc(s_mix[n], 16)

            plain(T_ZG, 4, KD, zg_d, BEFORE["ZG"], (17, 13), ACT.Silu)

            with act.Fori(0, TURNS) as i:
                for s in range(2 * KT):
                    hi(T_C, i, 2 * KT, s + ACT_LEAD)
                    if s == 0:
                        act.wait_ge(s_cv, i * 16 + 16)
                        act.wait_ge(pe_done, PC.after("turn", i - 1))
                        nc.scalar.activation(sl[:, :, 0:3, :].rearrange("p (h t) j n -> p t h (j n)", h=2),
                                             cv[:].rearrange("p t h j n -> p t h (j n)"), ACT.Silu).then_inc(act_done, AC.one("silu"))
                        act.wait_ge(act_done, AC.after("silu", i))
                        nc.scalar.activation(tt[:], sl[:, :, 0:2, :], ACT.Square).then_inc(act_done, AC.one("square"))
                        act.wait_ge(pool_done, GC.after("below", i))
                        nc.scalar.activation(dec[:], dec[:], ACT.Exp).then_inc(act_done, AC.one("exp"))
                    if s == 1:
                        act.wait_ge(dve_done, DC.after("sum", i))
                        nc.scalar.activation(rs[:, 0:8], ss[:, 0:8], ACT.Ln, bias=eps).then_inc(act_done, AC.one("ln"))
                        act.wait_ge(act_done, AC.after("ln", i))
                        nc.scalar.activation(rs[:, 0:8], rs[:, 0:8], ACT.Exp, scale=-0.5).then_inc(act_done, AC.one("rstd"))
                    if s == 2:
                        act.wait_ge(s_gcb, i * 16 + 16)
                        nc.scalar.activation(erow[:], rowb[:, 0], ACT.Exp).then_inc(act_done, AC.one("erow"))
                    if s == 4:
                        act.wait_ge(pe_done, PC.after("turns", i))
                        nc.scalar.copy(pq[:, :, 0, :], side[:, 2, :].rearrange("p (b n) -> p b n", n=P)).then_inc(act_done, AC.one("kT"))
                    if 10 <= s < 18 and s % 2 == 0:
                        n = 1 + (s - 8) // 2
                        act.wait_ge(pe_done, PC.after(f"ma{n}", i))
                        nc.scalar.copy(tt[:, :, 1, :], side[:, 2, :].rearrange("p (b n) -> p b n", n=P)).then_inc(act_done, AC.one(f"tT{n}"))
                    if s == 19:
                        act.wait_ge(pe_done, PC.after("solve", i))
                        nc.scalar.copy(wT[:].rearrange("p b n -> p (b n)"), side[:, 3, :]).then_inc(act_done, AC.one("wT"))
                    if s == 15 or s == 31:
                        c = s // KT
                        act.wait_ge(gated[c], i + 2)
                        nc.scalar.activation(stage[:, c], stage[:, c], ACT.Sigmoid).then_inc(emptied[c], 1)
                        act.wait_ge(emptied[c], i + (BEFORE["C"][c] + 2))
                        act.dma_start(tok(gate_d)[:, :, bass.ds(i * (2 * COLS) + c * COLS, COLS)], stage[:, c]).then_inc(stored[c], 16)
                    if s == 26:
                        act.wait_ge(pe_done, PC.after("out1", i))
                        nc.scalar.activation(m1[:].rearrange("p b n -> p (b n)"), side[:, 2, :], ACT.Square).then_inc(act_done, AC.one("osq"))
                        act.wait_ge(dve_done, DC.after("osum", i))
                        rsqrt(rs[:, 0:4], ss[:, 0:4], DV, AC, "oln", "orstd", i)
                    if s == 28:
                        act.wait_ge(pe_done, PC.after("turn", i))
                        for q in s_mix[2:4]:
                            act.wait_ge(q, i * 16 + 16)
                        nc.scalar.copy(gT[0][:].rearrange("p h n -> p (h n)"), side[:, 3, :]).then_inc(act_done, AC.one("hi"))
                    if s == 30:
                        act.wait_ge(dve_done, DC.after("lo", i))
                        for n in range(2):
                            act.dma_start(mix_d[2 + n][:, bass.ds(i * 2, 2), :], gT[n][:].bitcast(F32)).then_inc(s_mix[2 + n], 16)

            def hT_hi(i_prev):
                act.wait_ge(pe_done, PD.after("turn", i_prev))
                nc.scalar.copy(xT[0][:, bass.ds(i_prev * 4, 4), :].rearrange("p k n -> p (k n)"),
                               side[:, 0:2, :].rearrange("p a n -> p (a n)")).then_inc(act_done, AD.one("hi"))

            KO = KW // ROWS
            for s in range(2 * KO):
                hi(T_D, 0, 2 * KO, s + ACT_LEAD)
            with act.Fori(1, TURNS) as i:
                for s in range(2 * KO):
                    hi(T_D, i, 2 * KO, s + ACT_LEAD)
                    if s == 3:
                        hT_hi(i - 1)
            hT_hi(TURNS - 1)

            def send(i, c):
                act.wait_ge(summed[c], i + 2)
                act.dma_start(tok(outf)[:, :, bass.ds(i * (2 * COLS) + c * COLS, COLS)], stage[:, c]).then_inc(s_out[c], 16)

            with act.Fori(0, 3) as i:
                for s in range(2 * KT):
                    hi(T_E, i, 2 * KT, s + ACT_LEAD)
                    if s == 15 or s == 31:
                        send(i, s // KT)
            for s in range(2 * KT):
                if s + ACT_LEAD < 2 * KT:
                    hi(T_E, 3, 2 * KT, s + ACT_LEAD)
                if s == 15 or s == 31:
                    send(3, s // KT)
            for q in s_out:
                act.wait_ge(q, 64 + 16)
            for q in s_mix:
                act.wait_ge(q, 16 * (TURNS + 1))
            act.wait_ge(stored[0], 16 * 28)
            act.wait_ge(stored[1], 16 * 24)

        @block.vector
        def _(dve):
            V = nc.vector

            def lo(t0, turn, per, s):
                dve.wait_ge(hi_done, turn * per + (t0 + s + 1))
                w = width(t0 + s)
                V.tensor_tensor(wlo[:, s % RING, 0:w], raw[:, s % RING, 0:w], whi[:, s % RING, 0:w].bitcast(F32),
                                ALU.subtract).then_inc(lo_done, 1)

            for q in (*gated, *summed):
                dve.sem_inc(q, 1)
            dve.wait_ge(pe_done, P0.after("gains"))
            NR = KD + KQ + KKV
            V.tensor_copy(gcol[:], acc[0][:, 0, 0:NR]).then_inc(dve_done, D0.one("gcol"))
            dve.wait_ge(dve_done, D0.after("gcol"))

            def turn_lo(g, dst, g0, a_phase, phase):
                dve.wait_ge(act_done, a_phase.after(f"hi{g}"))
                for kk in range(2):
                    k = 2 * g + kk
                    ins = V.scalar_tensor_tensor(out=dst[1][:, k, :], in0=side[:, g % 4, kk * S:(kk + 1) * S],
                                                 scalar=gcol[:, g0 + k:g0 + k + 1], in1=dst[0][:, k, :].bitcast(F32),
                                                 op0=ALU.mult, op1=ALU.subtract)
                ins.then_inc(dve_done, phase.one(f"lo{g}"))

            KT = KD // ROWS
            for s in range(DVE_LEAD):
                turn_lo(s, xT, 0, A0, D0)
                lo(0, 0, RING, s)
            for s in range(3 * KT + RING):
                t = s + DVE_LEAD
                if t < NG:
                    turn_lo(t, xT, 0, A0, D0)
                lo(0, 0, RING, t) if t < T_MISC else lo(T_MISC, 0, RING, t - T_MISC) if t < T_Z else lo(T_Z, 0, RING, t - T_Z)
                if s == SQ_AT + D // COLS * TB - 1:
                    dve.wait_ge(act_done, A0.after(f"sq{D // COLS * TB - 1}"))
                    V.tensor_reduce(rx[:], ss[:].rearrange("p (t n) -> p t n", t=TB), AX, ALU.add).then_inc(dve_done, D0.one("sumx"))

            TWO_PI = 2.0 * np.pi
            MAGIC = 1.5 * 2.0 ** 23
            PART1 = 6.28125
            PART2 = float(np.float32(np.round((TWO_PI - PART1) * 2.0 ** 21) / 2.0 ** 21))
            PART3 = float(np.float32(TWO_PI - PART1 - PART2))

            def norm(n):
                a, b = ((0, RQ), (RQ, RQ + RKV))[n // TB]
                V.tensor_scalar(craw[:, n % TB, a:b], craw[:, n % TB, a:b], rs[:, n:n + 1], None, ALU.mult).then_inc(dve_done, D1.one(f"norm{n}"))

            def turn_Z(i, first):
                for s in range(2 * KT):
                    lo(T_Z, i, 2 * KT, s + DVE_LEAD)
                    if not first:
                        continue
                    if s == 1:
                        dve.wait_ge(s_row, 48)
                        dve.wait_ge(s_const, 16)
                        V.tensor_copy(pos_f[:], pos_i[:]).then_inc(dve_done, D1.one("pos"))
                        dve.wait_ge(dve_done, D1.after("pos"))
                        for tb in range(TB):
                            V.tensor_scalar(ang[:, :, tb, :], cst[:, C_FREQ:C_FREQ + HALF].unsqueeze(1).to_broadcast([P, 2, HALF]),
                                            pos_f[:, tb:tb + 1], None, ALU.mult).then_inc(dve_done, D1.one(f"ang{tb}"))
                    if s == 2:
                        dve.wait_ge(dve_done, D1.after("ang1"))
                        V.tensor_scalar(whole[:, 0], ang[:, 0], 1.0 / TWO_PI, 0.25, ALU.mult, ALU.add).then_inc(dve_done, D1.one("u0"))
                        V.tensor_scalar(whole[:, 1], ang[:, 1], 1.0 / TWO_PI, None, ALU.mult).then_inc(dve_done, D1.one("u1"))
                        dve.wait_ge(dve_done, D1.after("u1"))
                        V.tensor_scalar(whole[:], whole[:], MAGIC, None, ALU.add).then_inc(dve_done, D1.one("r0"))
                        dve.wait_ge(dve_done, D1.after("r0"))
                        V.tensor_scalar(whole[:], whole[:], MAGIC, None, ALU.subtract).then_inc(dve_done, D1.one("r1"))
                    if s == 3:
                        for part, name, before in ((PART1, "s1", "r1"), (PART2, "s2", "s1"), (PART3, "s3", "s2")):
                            dve.wait_ge(dve_done, D1.after(before))
                            V.scalar_tensor_tensor(out=ang[:], in0=whole[:], scalar=-part, in1=ang[:], op0=ALU.mult, op1=ALU.add).then_inc(dve_done, D1.one(name))
                        dve.wait_ge(dve_done, D1.after("s3"))
                        V.tensor_scalar(ang[:, 0], ang[:, 0], np.pi / 2, None, ALU.add).then_inc(dve_done, D1.one("s4"))
                        dve.wait_ge(dve_done, D1.after("s4"))
                        V.tensor_scalar(ang[:], ang[:], 3.1415925, -3.1415925, ALU.min, ALU.max).then_inc(dve_done, D1.one("s5"))
                    if s == 4:
                        dve.wait_ge(act_done, A1.after("misc"))
                        V.tensor_tensor(av[:, 0], misc[:, :, ROPE + H:MN], alg[:, 1:2, :].to_broadcast([P, TB, H]), ALU.add).then_inc(dve_done, D1.one("adt"))
                        dve.wait_ge(dve_done, D1.after("adt"))
                        V.scalar_tensor_tensor(out=av[:, 1], in0=av[:, 0], scalar=-1.0, in1=av[:, 0], op0=ALU.mult, op1=ALU.min).then_inc(dve_done, D1.one("nabs"))
                        dve.wait_ge(act_done, A1.after("rstd"))
                        norm(0)
                    if s == 5:
                        norm(1)
                    if s == 6:
                        norm(2)
                        norm(3)
                    if s == 7:
                        dve.wait_ge(act_done, A1.after("lnx"))
                        V.scalar_tensor_tensor(out=av[:, 2], in0=av[:, 0], scalar=0.0, in1=av[:, 1], op0=ALU.max, op1=ALU.add).then_inc(dve_done, D1.one("sp"))
                        dve.wait_ge(dve_done, D1.after("sp"))
                        V.scalar_tensor_tensor(out=av[:, 3], in0=av[:, 2], scalar=-1.0, in1=alg[:, 0:1, :].to_broadcast([P, TB, H]),
                                               op0=ALU.mult, op1=ALU.mult).then_inc(dve_done, D1.one("g"))
                    if s == 10:
                        sums = side[:, 0, 0:4 * H].rearrange("p (a t h) -> p a t h", a=2, h=H)
                        dve.wait_ge(pe_done, P1.after("cum"))
                        V.tensor_copy(gc[:].rearrange("p h t -> p t h"), sums[:, 0]).then_inc(dve_done, D1.one("gc"))
                        V.tensor_copy(gth[:, 0], sums[:, 0]).then_inc(dve_done, D1.one("gth"))
                        V.tensor_copy(gth[:, 1], beta[:].rearrange("p h t -> p t h")).then_inc(dve_done, D1.one("gth2"))
                        dve.wait_ge(dve_done, D1.after("gc"))
                        V.tensor_tensor(ekd[:].rearrange("p h t -> p t h"), sums[:, 1], gc[:].rearrange("p h t -> p t h"),
                                        ALU.subtract).then_inc(dve_done, D1.one("kdx"))
                    if s == 13:
                        dve.wait_ge(pe_done, P1.after("gct"))
                        V.tensor_copy(gcT[:].rearrange("h a s -> h (a s)"), side[0:H, 1, :]).then_inc(dve_done, D1.one("gct"))
                    if 16 <= s < 16 + NC:
                        turn_lo(s - 16, cT, KD, A1, D1)

            def plain(t0, n, kn):
                per = 2 * kn // ROWS
                with dve.Fori(0, n // 2) as i:
                    for s in range(per):
                        lo(t0, i, per, s + DVE_LEAD)

            turn_Z(0, True)
            turn_Z(1, False)
            plain(T_Q, 6, KQ)
            plain(T_KV, 8, KKV)

            SCALE = float(QK) ** -0.5
            with dve.Fori(0, 4) as i:
                def after(name):
                    dve.wait_ge(dve_done, DB.after(name, turn))
                for slot in range(3 * KT):
                    lo(T_B, i, 3 * KT, slot + DVE_LEAD)
                    half, s = slot // 24, slot % 24
                    turn = i * 2 + half
                    flat = qk[:].rearrange("p a t h n -> p (a t h) n")
                    sqf = sq[:].rearrange("p a t h n -> p (a t h) n")
                    if s == 3:
                        dve.wait_ge(act_done, AB.after("sq", turn))
                        V.tensor_reduce(ss[:, 0:8], sqf, AX, ALU.add).then_inc(dve_done, DB.one("sum"))
                    if s == 4:
                        dve.wait_ge(act_done, AB.after("rstd", turn))
                        V.tensor_tensor(flat, flat, rs[:, 0:8].unsqueeze(2).to_broadcast([P, 8, QK]), ALU.mult).then_inc(dve_done, DB.one("unit"))
                        after("unit")
                        dve.wait_ge(s_bc, 48)
                        V.tensor_tensor(qk[:].rearrange("p a t h n -> p a (t h) n"), qk[:].rearrange("p a t h n -> p a (t h) n"),
                                        gqk[:].unsqueeze(2).to_broadcast([P, 2, 2 * TB, QK]), ALU.mult).then_inc(dve_done, DB.one("gain"))
                    if s == 5:
                        after("gain")
                        x1 = qk[:, :, :, :, NOPE:NOPE + HALF]
                        x2 = qk[:, :, :, :, NOPE + HALF:QK]
                        tg = lambda n, a: trig[:, n].unsqueeze(2).to_broadcast([P, TB, 2, HALF])
                        r = lambda n, a: rt[:, n, 4 * a:4 * a + 4, :].rearrange("p (t h) n -> p t h n", h=2)
                        for n, (xx, f, name) in enumerate(((x1, 0, "r1"), (x2, 1, "r2"), (x2, 0, "r3"), (x1, 1, "r4"))):
                            V.tensor_tensor(r(n, 0), xx[:, 0], tg(f, 0), ALU.mult)
                            V.tensor_tensor(r(n, 1), xx[:, 1], tg(f, 1), ALU.mult).then_inc(dve_done, DB.one(name))
                        after("r4")
                        rr = lambda n: rt[:, n].rearrange("p (a b) n -> p a b n", a=2)
                        v = lambda t: t.rearrange("p a t h n -> p a (t h) n")
                        V.tensor_tensor(v(x1), rr(0), rr(1), ALU.subtract).then_inc(dve_done, DB.one("r5"))
                        V.tensor_tensor(v(x2), rr(2), rr(3), ALU.add).then_inc(dve_done, DB.one("r6"))
                    if s == 9:
                        dve.wait_ge(pe_done, PB.after("heads", turn))
                        V.tensor_copy(qkTb[:].rearrange("p a h n -> p (a h n)"),
                                      side[0:ROPE, 2:4, :].rearrange("p a n -> p (a n)")).then_inc(dve_done, DB.one("ropeT"))
                    if s == 11:
                        dve.wait_ge(pe_done, PB.after("scores", turn))
                        V.scalar_tensor_tensor(out=sc[:], in0=side[:, 0:2, 0:3 * P], scalar=SCALE,
                                               in1=cst[:, C_MASK:C_MASK + 3 * P].unsqueeze(1).to_broadcast([P, 2, 3 * P]),
                                               op0=ALU.mult, op1=ALU.add).then_inc(dve_done, DB.one("mask"))
                        after("mask")
                        V.tensor_reduce(mx[:, 0, 0, :], sc[:, :, 0:P], AX, ALU.max).then_inc(dve_done, DB.one("max0"))
                        V.tensor_reduce(mx[:, 0, 1, :], sc[:, :, P:3 * P], AX, ALU.max).then_inc(dve_done, DB.one("max1"))
                        after("max1")
                        V.tensor_scalar(mx[:, 1], mx[:, 0], -1.0, None, ALU.mult).then_inc(dve_done, DB.one("neg"))
                    if s == 16:
                        dve.wait_ge(act_done, AB.after("expD", turn))
                        V.reciprocal(mx[:, 0], mx[:, 2]).then_inc(dve_done, DB.one("rden"))
                        after("rden")
                        dve.wait_ge(pe_done, PB.after("values", turn))
                        ogf = og[:].rearrange("p t h n -> p (t h) n")
                        V.tensor_tensor(ogf, side[:, 0, :].rearrange("p (b n) -> p b n", n=P),
                                        mx[:, 0].rearrange("p t h -> p (t h)").unsqueeze(2).to_broadcast([P, 2 * TB, DV]),
                                        ALU.mult).then_inc(dve_done, DB.one("div"))
                        after("div")
                        dve.wait_ge(s_zs, i * 32 + (16 * half + 16))
                        V.tensor_tensor(og[:], og[:], zs[:], ALU.mult).then_inc(dve_done, DB.one("gate"))
                    if s == 18:
                        dve.wait_ge(act_done, AB.after("hi", turn))
                        V.tensor_tensor(mT[1][:].rearrange("p h n -> p (h n)"), side[:, 1, :],
                                        mT[0][:].rearrange("p h n -> p (h n)").bitcast(F32), ALU.subtract).then_inc(dve_done, DB.one("lo"))

            plain(T_ZG, W // COLS, KD)

            for q in s_mix[0:2]:
                dve.wait_ge(q, 16 * (TURNS + 1))
            dve.wait_ge(s_conv, 16 * 2 * 12)
            V.memset(qeT[:], 0.0).then_inc(dve_done, DZ.one("zero"))
            bc = lambda a: a.unsqueeze(2).to_broadcast([P, 2 * TB, DV])
            with dve.Fori(0, TURNS) as i:
                def after(name):
                    dve.wait_ge(dve_done, DC.after(name, i))

                def of_pair(a):
                    return a[:, bass.ds(i * 2, 2), :].rearrange("p h t -> p (h t)")
                rk = rs[:, 0:8].rearrange("p (b j) -> p b j", j=2)
                for s in range(2 * KT):
                    lo(T_C, i, 2 * KT, s + DVE_LEAD)
                    if s == 0:
                        dve.wait_ge(act_done, AC.after("square", i))
                        V.tensor_reduce(ss[:, 0:8], tt[:].rearrange("p b j n -> p (b j) n"), AX, ALU.add).then_inc(dve_done, DC.one("sum"))
                    if s == 1:
                        dve.wait_ge(act_done, AC.after("rstd", i))
                        V.tensor_scalar(cf[:, 0], rk[:, :, 0], float(DV) ** -0.5, None, ALU.mult).then_inc(dve_done, DC.one("cq"))
                        V.tensor_tensor(sl[:, :, 1, :], sl[:, :, 1, :], bc(rk[:, :, 1]), ALU.mult).then_inc(dve_done, DC.one("kn"))
                        after("cq")
                        V.tensor_tensor(sl[:, :, 0, :], sl[:, :, 0, :], bc(cf[:, 0]), ALU.mult).then_inc(dve_done, DC.one("qn"))
                    if s == 2:
                        V.tensor_tensor(cf[:, 1], of_pair(beta), of_pair(egc), ALU.mult).then_inc(dve_done, DC.one("cke"))
                        after("cke")
                        V.tensor_tensor(kbe[:], sl[:, :, 1, :], bc(cf[:, 1]), ALU.mult).then_inc(dve_done, DC.one("kbe"))
                    if s == 4:
                        dve.wait_ge(pe_done, PC.after("turns", i))
                        dve.wait_ge(act_done, AC.after("erow", i))
                        dve.wait_ge(dve_done, DZ.after("zero"))
                        V.tensor_tensor(qeT[:].rearrange("p b a n -> p b (a n)").rearrange("p b (c n) -> p b c n", c=2)[:, :, :, 0:CHUNK],
                                        side[:, 3, :].rearrange("p (b c n) -> p b c n", c=2, n=CHUNK),
                                        erow[:].rearrange("p b (c n) -> p b c n", c=2), ALU.mult).then_inc(dve_done, DC.one("qeT"))
                        V.tensor_copy(pq[:, :, 1, :], side[:, 3, :].rearrange("p (b n) -> p b n", n=P)).then_inc(dve_done, DC.one("qT"))
                    if s == 6:
                        dve.wait_ge(pe_done, PC.after("products", i))
                        pr = side[:, 0:2, :].rearrange("p a (b j n) -> p (a b) j n", j=2, n=P)
                        dve.wait_ge(pool_done, GC.after("decb", i))
                        V.tensor_tensor(lt[:], pr[:, :, 0, :], lt[:], ALU.mult).then_inc(dve_done, DC.one("lt"))
                        V.tensor_tensor(dec[:], pr[:, :, 1, :], dec[:], ALU.mult).then_inc(dve_done, DC.one("attn"))
                        after("lt")
                        V.tensor_tensor(m1[:], lt[:], level(0).unsqueeze(1).to_broadcast([P, 2 * TB, P]), ALU.mult).then_inc(dve_done, DC.one("l1"))
                        after("l1")
                        V.tensor_tensor(tt[:, :, 1, :], ident.unsqueeze(1).to_broadcast([P, 2 * TB, P]), m1[:], ALU.subtract).then_inc(dve_done, DC.one("tt1"))
                    if s == 7:
                        dve.wait_ge(pe_done, PC.after("t1", i))
                        V.tensor_copy(tt[:, :, 0, :], side[:, 2, :].rearrange("p (b n) -> p b n", n=P)).then_inc(dve_done, DC.one("t1"))
                    if 8 <= s < 18:
                        n = 1 + (s - 8) // 2
                        if s % 2 == 0:
                            dve.wait_ge(pe_done, PC.after(f"ma{n}", i))
                            V.tensor_tensor(m1[:], side[:, 3, :].rearrange("p (b n) -> p b n", n=P),
                                            level(n).unsqueeze(1).to_broadcast([P, 2 * TB, P]), ALU.mult).then_inc(dve_done, DC.one(f"ma{n}"))
                        else:
                            dve.wait_ge(pe_done, PC.after(f"mb{n}", i))
                            j = 0 if n < len(LEVELS) - 1 else 1
                            V.tensor_tensor(tt[:, :, j, :], tt[:, :, j, :], side[:, 0, :].rearrange("p (b n) -> p b n", n=P),
                                            ALU.subtract).then_inc(dve_done, DC.one(f"mb{n}"))
                    if s == 18:
                        dve.wait_ge(pe_done, PC.after("solve", i))
                        V.tensor_copy(sl[:, :, 2, :], side[:, 2, :].rearrange("p (b n) -> p b n", n=P)).then_inc(dve_done, DC.one("u"))

                    def state(c, names):
                        for h in range(2):
                            V.scalar_tensor_tensor(out=st[:, c % 2, h, :], in0=st[:, (c - 1) % 2, h, :],
                                                   scalar=glast[:, bass.ds(i * 2 + h, 1), c - 1], in1=side[:, 1, h * P:(h + 1) * P],
                                                   op0=ALU.mult, op1=ALU.add).then_inc(dve_done, DC.one(names[h]))

                    def new_v(c, name):
                        r = slice((c % 2) * CHUNK, (c % 2 + 1) * CHUNK)
                        v = sl[:].rearrange("p (h t) j n -> p h t j n", t=TB)[r, :, c // 2, 2, :]
                        V.tensor_tensor(v, v, side[r, 0, 0:2 * P].rearrange("p (h n) -> p h n", n=P), ALU.subtract).then_inc(dve_done, DC.one(name))

                    if s == 19:
                        dve.wait_ge(pe_done, PC.after("kv0", i))
                        V.tensor_copy(st[:, 1].rearrange("p h n -> p (h n)"), side[:, 1, 0:2 * P]).then_inc(dve_done, DC.one("s1"))
                    if s == 20:
                        dve.wait_ge(pe_done, PC.after("ws1", i))
                        new_v(1, "v1")
                    if s == 21:
                        dve.wait_ge(pe_done, PC.after("kv1", i))
                        state(2, ("s2a", "s2b"))
                    if s == 22:
                        dve.wait_ge(pe_done, PC.after("ws2", i))
                        new_v(2, "v2")
                    if s == 23:
                        dve.wait_ge(pe_done, PC.after("kv2", i))
                        state(3, ("s3a", "s3b"))
                    if s == 24:
                        dve.wait_ge(pe_done, PC.after("ws3", i))
                        new_v(3, "v3")
                    if s == 26:
                        dve.wait_ge(act_done, AC.after("osq", i))
                        V.tensor_reduce(ss[:, 0:4], m1[:], AX, ALU.add).then_inc(dve_done, DC.one("osum"))
                    if s == 27:
                        dve.wait_ge(act_done, AC.after("orstd", i))
                        dve.wait_ge(pool_done, GC.after("gz", i))
                        V.tensor_tensor(m1[:], side[:, 2, :].rearrange("p (b n) -> p b n", n=P), bc(rs[:, 0:4]), ALU.mult).then_inc(dve_done, DC.one("on"))
                        after("on")
                        z = sl[:].rearrange("p (h t) j n -> p t h j n", t=TB)[:, :, :, 3, :]
                        V.tensor_tensor(z, z, m1[:].rearrange("p (t h) n -> p t h n", h=2), ALU.mult).then_inc(dve_done, DC.one("ogate"))
                    if s == 28:
                        dve.wait_ge(act_done, AC.after("hi", i))
                        V.tensor_tensor(gT[1][:].rearrange("p h n -> p (h n)"), side[:, 3, :],
                                        gT[0][:].rearrange("p h n -> p (h n)").bitcast(F32), ALU.subtract).then_inc(dve_done, DC.one("lo"))
                    if s == 15 or s == 31:
                        c = s // KT
                        dve.wait_ge(tile_used, i * (2 * KT) + (T_C + s + 2))
                        dve.wait_ge(s_bb, i * 16 + 16)
                        dve.wait_ge(stored[c], i * 16 + 16 * (20, 16)[c])
                        for tb in range(TB):
                            ins = V.scalar_tensor_tensor(out=stage[:, c, tb, :], in0=acc[c][:, tb, :], scalar=rx[:, tb:tb + 1], in1=bb[:, c, :],
                                                         op0=ALU.mult, op1=ALU.add)
                        ins.then_inc(gated[c], 1)

            KO = KW // ROWS

            def turn_D(i, previous):
                for s in range(2 * KO):
                    lo(T_D, i, 2 * KO, s + DVE_LEAD)
                    if s == 3 and previous:
                        dve.wait_ge(act_done, AD.after("hi", i - 1))
                        hT_lo(i - 1)
                    if s == KO - 1:
                        dve.wait_ge(tile_used, i * (2 * KO) + (T_D + KO + 1))
                        dve.wait_ge(s_gate[0], i * 16 + 16)
                        V.tensor_tensor(stage[:, 0], acc[0][:], stage[:, 0], ALU.mult).then_inc(gated[0], 1)
                    if s == 2 * KO - 1:
                        dve.wait_ge(tile_used, i * (2 * KO) + (T_D + 2 * KO + 1))
                        dve.wait_ge(s_gate[1], i * 16 + 16)
                        V.tensor_tensor(stage[:, 1], acc[1][:], stage[:, 1], ALU.mult).then_inc(gated[1], 1)
                        dve.wait_ge(gated[1], i + (TURNS + 2))
                        V.tensor_tensor(hb[:], stage[:, 0], stage[:, 1], ALU.add).then_inc(dve_done, DD.one("h3"))

            def hT_lo(i_prev):
                V.tensor_tensor(xT[1][:, bass.ds(i_prev * 4, 4), :].rearrange("p k n -> p (k n)"),
                                side[:, 0:2, :].rearrange("p a n -> p (a n)"),
                                xT[0][:, bass.ds(i_prev * 4, 4), :].rearrange("p k n -> p (k n)").bitcast(F32),
                                ALU.subtract).then_inc(dve_done, DD.one("lo"))

            turn_D(0, False)
            with dve.Fori(1, TURNS) as i:
                turn_D(i, True)
            dve.wait_ge(act_done, AD.after("hi", TURNS - 1))
            hT_lo(TURNS - 1)

            def residual(i, c, s):
                dve.wait_ge(tile_used, i * (2 * KT) + (T_E + s + 2))
                dve.wait_ge(s_xr[c], i * 16 + 16)
                dve.wait_ge(s_out[c], i * 16 + 16)
                V.tensor_tensor(stage[:, c], acc[c][:], xr[:, c], ALU.add).then_inc(summed[c], 1)

            with dve.Fori(0, 3) as i:
                for s in range(2 * KT):
                    lo(T_E, i, 2 * KT, s + DVE_LEAD)
                    if s == 15 or s == 31:
                        residual(i, s // KT, s)
            for s in range(2 * KT):
                if s + DVE_LEAD < 2 * KT:
                    lo(T_E, 3, 2 * KT, s + DVE_LEAD)
                if s == 15 or s == 31:
                    residual(3, s // KT, s)

        @block.gpsimd
        def _(pool):
            G = nc.gpsimd
            pool.wait_ge(dve_done, D0.after("sumx"))
            pool.dma_start(alg[:, 0, :], a_log.partition_broadcast(P)).then_inc(s_row, 16)
            pool.dma_start(alg[:, 1, :], dt_bias.partition_broadcast(P)).then_inc(s_row, 16)
            with nc.allow_non_contiguous_dma(reason="256 positions"):
                pool.dma_start(pos_i[:], positions.rearrange("a (t p) -> p (a t)", p=P)).then_inc(s_row, 16)
            G.memset(zrow[:], 0.0).then_inc(pool_done, G1.one("zero"))
            pool.wait_ge(pool_done, G1.after("zero"))
            pool.dma_start(g_d[0:TAPS - 1, :].rearrange("a (b n) -> (a b) n", n=256), zrow[:]).then_inc(s_zero, 16)
            for q in stored:
                pool.wait_ge(q, 16 * 10)
            pool.wait_ge(s_zero, 16)
            with pool.Fori(0, 4) as i:
                for n in range(3):
                    def done(name):
                        return GB.after(name, i * 3 + n)
                    pool.wait_ge(stored[n % 2], i * (16 * (2 - n % 2)) + 16 * (11 + n // 2))
                    if n:
                        pool.wait_ge(s_conv, i * 96 + 32 * n)
                    for j in range(TAPS):
                        pool.dma_start(xs[:, j], tok(g_d[j:j + S, :])[:, :, bass.ds(i * COLS + n * W, COLS)]).then_inc(s_tap, 16)
                    pool.dma_start(cw[:], conv_w[:, bass.ds(i * COLS + n * W, COLS)].partition_broadcast(P)).then_inc(s_tap, 16)
                    pool.wait_ge(s_tap, i * (3 * 16 * (TAPS + 1)) + (n + 1) * 16 * (TAPS + 1))
                    for j in range(TAPS):
                        G.tensor_tensor(xs[:, j], xs[:, j], cw[:, j:j + 1, :].to_broadcast([P, TB, COLS]),
                                        ALU.mult).then_inc(pool_done, GB.one(f"m{j}"))
                    for j in range(1, TAPS):
                        pool.wait_ge(pool_done, done("m3" if j == 1 else f"a{j - 1}"))
                        G.tensor_tensor(xs[:, 0], xs[:, 0], xs[:, j], ALU.add).then_inc(pool_done, GB.one(f"a{j}"))
                    pool.wait_ge(pool_done, done("a3"))
                    for tb in range(TB):
                        pool.dma_start(conv_d[tb * P:(tb + 1) * P, bass.ds(i * 4, 4), n, :],
                                       xs[:, 0, tb, :].rearrange("p (h n) -> p h n", n=DV)).then_inc(s_conv, 16)
                pool.wait_ge(s_conv, i * 96 + 96)
            for q in s_mix[0:2]:
                pool.wait_ge(q, 16 * (TURNS + 1))
            pool.dma_start(oT[0][:].bitcast(F32), mix_d[0][:]).then_inc(s_oT[0], 16)
            with pool.Fori(0, TURNS) as i:
                def of_pair(a):
                    return a[:, bass.ds(i * 2, 2), :].rearrange("p h t -> p (h t)").unsqueeze(2).to_broadcast([P, 2 * TB, DV])
                pool.wait_ge(s_gcb, i * 16 + 16)
                pool.wait_ge(pe_done, PC.after("out1", i - 1))
                G.tensor_tensor(dec[:], rowb[:, 0], of_pair(gc), ALU.subtract).then_inc(pool_done, GC.one("diff"))
                pool.wait_ge(pool_done, GC.after("diff", i))
                G.tensor_tensor(dec[:], dec[:], causal.unsqueeze(1).to_broadcast([P, 2 * TB, P]), ALU.mult).then_inc(pool_done, GC.one("below"))
                pool.wait_ge(act_done, AC.after("exp", i))
                G.tensor_tensor(dec[:], dec[:], causal.unsqueeze(1).to_broadcast([P, 2 * TB, P]), ALU.mult).then_inc(pool_done, GC.one("mask"))
                pool.wait_ge(pool_done, GC.after("mask", i))
                G.tensor_tensor(lt[:], dec[:], rowb[:, 1], ALU.mult).then_inc(pool_done, GC.one("decb"))
                pool.wait_ge(act_done, AC.after("silu", i))
                G.tensor_tensor(sl[:, :, 2, :], sl[:, :, 2, :], of_pair(beta), ALU.mult).then_inc(pool_done, GC.one("vb"))
                pool.wait_ge(dve_done, DC.after("kn", i))
                G.tensor_tensor(kd[:], sl[:, :, 1, :], of_pair(ekd), ALU.mult).then_inc(pool_done, GC.one("kd"))
                pool.wait_ge(s_zg, i * 32 + 32)
                pool.wait_ge(s_bc, 48)
                G.tensor_tensor(sl[:, :, 3, :], sl[:, :, 3, :], ggo[:].unsqueeze(1).to_broadcast([P, 2 * TB, DV]),
                                ALU.mult).then_inc(pool_done, GC.one("gz"))
            for q in s_mix:
                pool.wait_ge(q, 16 * (TURNS + 1))
            pool.wait_ge(pe_done, PC.after("turn", TURNS - 1))
            pool.wait_ge(gated[1], TURNS + 1)
            for n in range(1, 4):
                pool.dma_start(oT[n][:].bitcast(F32), mix_d[n][:]).then_inc(s_oT[n], 16)
            pool.wait_ge(stored[0], 16 * 28)
            pool.wait_ge(stored[1], 16 * 24)
            with pool.Fori(0, TURNS) as i:
                for c in range(2):
                    pool.wait_ge(gated[c], i + (TURNS + 1))
                    pool.wait_ge(dve_done, DD.after("h3", i - 1))
                    pool.dma_start(stage[:, c], tok(gate_d)[:, :, bass.ds(i * COLS + c * D, COLS)]).then_inc(s_gate[c], 16)
            pool.wait_ge(tile_used, T_E + 1)
            with pool.Fori(0, 4) as i:
                for c in range(2):
                    pool.wait_ge(summed[c], i + 1)
                    pool.dma_start(xr[:, c], tok(xf)[:, :, bass.ds(i * (2 * COLS) + c * COLS, COLS)]).then_inc(s_xr[c], 16)


_INS = ["x", "positions", "w_norm", "w_in", "b_gate", "w_q_up", "w_kv_up", "g_q_latent", "g_kv_latent", "g_q_head",
        "g_k_head", "w_o_mla", "conv_w", "a_log", "dt_bias", "g_gdn_out", "w_o_gdn", "w_out"]


def kernel(**inputs):
    import numpy as _np
    import concourse.bacc as _bacc
    from concourse import mybir as _mybir
    from concourse.bass_utils import run_bass_kernel_spmd as _run

    nc = _bacc.Bacc("TRN2", target_bir_lowering=False, num_devices=1)
    arrays, args = {}, []
    for name in _INS + ["consts"]:
        a = shape_constants() if name == "consts" else _np.ascontiguousarray(inputs[name])
        arrays[f"in_{name}_dram"] = a
        args.append(nc.dram_tensor(f"in_{name}_dram", a.shape, _mybir.dt.from_np(a.dtype), kind="ExternalInput").ap())
    args.append(nc.dram_tensor("out_dram", inputs["x"].shape, _mybir.dt.float32, kind="ExternalOutput").ap())
    hybrid_block(nc, *args)
    r = _run(nc, [arrays], core_ids=[0])
    return r.results[0]["out_dram"]
```

```python
from contextlib import ExitStack

import numpy as np

import concourse.bass as bass
from concourse import mybir

F32 = mybir.dt.float32
F32R = mybir.dt.float32r
I32 = mybir.dt.int32
ALU = mybir.AluOpType
ACT = mybir.ActivationFunctionType
AX = mybir.AxisListType.X

P = 128
RING = 4
ROWS = 2
COLS = 512
DVE_LEAD = 2
ACT_LEAD = 3
NEG = -1.0e30
CHUNK = 64
LEVELS = (1, 2, 4, 8, 16, 32)
LN_EXP = "natural_log_exp_and_others"

C_IDENT = 0
C_MASK = C_IDENT + P
C_CAUSAL = C_MASK + 3 * P
C_LEVEL = C_CAUSAL + P
C_SAME = C_LEVEL + P + (len(LEVELS) - 1) * P // 2
C_HALF = C_SAME + P
C_FREQ = C_HALF + 2 * P
C_EPS = C_FREQ + 32
C_ALL = C_EPS + 2


def shape_constants():
    c = np.zeros((P, C_ALL), np.float32)
    i = np.arange(P)
    c[:, C_IDENT:C_IDENT + P] = np.eye(P)
    for block, at in ((0, C_MASK), (1, C_MASK + P)):
        keys = np.arange((block + 1) * P)
        hidden = (keys[None, :] // CHUNK) > ((block * P + i)[:, None] // CHUNK)
        c[:, at:at + keys.size] = np.where(hidden, NEG, 0.0)
    same = (i[:, None] // CHUNK) == (i[None, :] // CHUNK)
    c[:, C_CAUSAL:C_CAUSAL + P] = same & (i[:, None] <= i[None, :])
    c[:, C_SAME:C_SAME + P] = same
    for n, s in enumerate(LEVELS):
        low = (i[:, None] // (2 * s) == i[None, :] // (2 * s)) & (i[:, None] % (2 * s) >= s) & (i[None, :] % (2 * s) < s)
        if n == 0:
            c[:, C_LEVEL:C_LEVEL + P] = low.T
        else:
            c[:, C_LEVEL + (n + 1) * P // 2:C_LEVEL + (n + 2) * P // 2] = low[:, i % (2 * s) < s]
    c[:CHUNK, C_HALF:C_HALF + P] = 1.0
    c[CHUNK:, C_HALF + P:C_HALF + 2 * P] = 1.0
    c[:, C_FREQ:C_FREQ + 32] = (10000.0 ** (-np.arange(0, 64, 2, dtype=np.float32) / np.float32(64))).astype(np.float32)
    c[:, C_EPS] = 1e-6
    c[:, C_EPS + 1] = 1.0
    return c


class Count:

    def __init__(self, sem):
        self.sem, self.base = sem, 0

    def phase(self, names, repeats=1):
        p = Phase(self, names.split(), self.base)
        self.base += len(p.names) * repeats
        return p


class Phase:

    def __init__(self, count, names, base):
        self.names, self.base, self.at = names, base, 0
        assert len(set(names)) == len(names)

    def after(self, name, turn=0):
        return turn * len(self.names) + (self.base + self.names.index(name) + 1)

    def one(self, name):
        assert self.names[self.at] == name, (self.names[self.at], name)
        self.at = (self.at + 1) % len(self.names)
        return 1


class Arena:

    def __init__(self, nc, base, end):
        self.nc, self.at, self.end = nc, base, end

    def take(self, name, shape, dtype=F32):
        n = int(np.prod(shape[1:])) * 4
        t = self.nc.alloc_sbuf_tensor_at(name, shape, dtype, offset=self.at)
        self.at += (n + 31) // 32 * 32
        assert self.at <= self.end, (name, self.at, self.end)
        return t


def hybrid_block(nc, x, positions, w_norm, w_in, b_gate, w_q_up, w_kv_up, g_q_latent, g_kv_latent, g_q_head,
                 g_k_head, w_o_mla, conv_w, a_log, dt_bias, g_gdn_out, w_o_gdn, w_out, consts, out):
    _, S, D = x.shape
    TB = S // P
    RQ, RKV = w_q_up.shape[0], w_kv_up.shape[0]
    H = a_log.shape[0]
    QK = g_q_head.shape[0]
    NOPE, ROPE, DV = P, QK - P, P
    HALF = ROPE // 2
    W = w_o_mla.shape[0]
    TAPS = conv_w.shape[0]
    assert TB == 2 and D == 4096 and H == 16 and QK == 192 and W == H * DV
    O_C = 0
    O_ROPE = RQ + RKV
    O_Z = O_ROPE + ROPE
    O_QKV = O_Z + W
    O_BA = O_QKV + 3 * W
    O_ZG = O_BA + 2 * H
    O_GATE = O_ZG + W
    KD, KQ, KKV, KW = D // P, RQ // P, RKV // P, W // P

    xf = x.rearrange("a s d -> (a s) d")
    outf = out.rearrange("a s d -> (a s) d")
    tok = lambda a: a.rearrange("(t p) n -> p t n", p=P)
    rows = lambda a: a.rearrange("(k p) n -> p k n", p=P)

    z_d = nc.dram_tensor("z_scratch", (S, W), F32).ap()
    q_d = nc.dram_tensor("q_scratch", (S, H * QK), F32).ap()
    kv_d = nc.dram_tensor("kv_scratch", (S, H * 2 * P), F32).ap()
    g_d = nc.dram_tensor("g_scratch", (S + TAPS - 1, 3 * W), F32).ap()
    conv_d = nc.dram_tensor("conv_scratch", (S, H, 3, DV), F32).ap()
    zg_d = nc.dram_tensor("zg_scratch", (S, W), F32).ap()
    gate_d = nc.dram_tensor("gate_scratch", (S, 2 * D), F32).ap()
    row_d = nc.dram_tensor("row_scratch", (2, H, S), F32).ap()
    mix_d = [nc.dram_tensor(f"mix_scratch{i}", (P, H, S), F32).ap() for i in range(4)]

    with ExitStack() as ctx:
        sb = lambda name, shape, dt=F32: ctx.enter_context(nc.sbuf_tensor(name, shape, dt))
        sem = lambda name: ctx.enter_context(nc.semaphore(name))

        xT = [sb("xT_hi", [P, KD, S], F32R), sb("xT_lo", [P, KD, S], F32R)]
        raw = sb("raw_ring", [P, RING, ROWS * COLS])
        whi = sb("hi_ring", [P, RING, ROWS * COLS], F32R)
        wlo = sb("lo_ring", [P, RING, ROWS * COLS], F32R)
        stage = sb("stage", [P, 2, TB, COLS])
        cst = sb("cst", [P, C_ALL])
        misc = sb("misc", [P, TB, ROPE + 2 * H])
        gcol = sb("gcol", [P, KD + KQ + KKV])
        gqk = sb("gqk", [P, 2, QK])
        ggo = sb("ggo", [P, DV])
        trig = sb("trig", [P, 2, TB, HALF])
        ss = sb("ss", [P, 16])
        rx = sb("rx", [P, TB])
        rs = sb("rs", [P, 16])
        beta = sb("beta", [P, H, TB])
        gc = sb("gc", [P, H, TB])
        egc = sb("egc", [P, H, TB])
        ekd = sb("ekd", [P, H, TB])
        glast = sb("glast", [P, H, 2 * TB])
        slab_base = nc.sbuf_base
        slab_end = nc.sbuf_usable_end
        area = lambda: Arena(nc, slab_base, slab_end)

        a0 = area()
        xin = a0.take("xin", [P, TB, D])
        junk = a0.take("junk", [P, COLS])
        graw = a0.take("graw", [KD + KQ + KKV, P])
        a1 = area()
        craw = a1.take("craw", [P, TB, RQ + RKV])
        cjunk = a1.take("cjunk", [P, RQ])
        cT = [a1.take("cT_hi", [P, KQ + KKV, S], F32R), a1.take("cT_lo", [P, KQ + KKV, S], F32R)]
        alg = a1.take("alg", [P, 2, H])
        pos_i = a1.take("pos_i", [P, TB], I32)
        pos_f = a1.take("pos_f", [P, TB])
        ang = a1.take("ang", [P, 2, TB, HALF])
        whole = a1.take("whole_turns", [P, 2, TB, HALF])
        av = a1.take("av", [P, 4, TB, H])
        gth = a1.take("gth", [P, 2, TB, H])
        gcT = a1.take("gcT", [H, 2, S])
        zrow = a1.take("zrow", [72, 256])
        miscT = a1.take("miscT", [ROPE + 2 * H, S])

        ab = area()
        qk = ab.take("qk", [P, 2, TB, 2, QK])
        vt = ab.take("vt", [P, TB, 2, DV])
        zs = ab.take("zs", [P, TB, 2, DV])
        sq = ab.take("sq", [P, 2, TB, 2, QK])
        qkTa = ab.take("qkTa", [P, 2, 2, TB * P])
        qkTb = ab.take("qkTb", [ROPE, 2, 2, TB * P])
        sc = ab.take("sc", [P, 2, 3 * P])
        pT = ab.take("pT", [P, 2, 3 * P])
        og = ab.take("og", [P, TB, 2, DV])
        rt = ab.take("rt", [P, 4, 4 * TB, HALF])
        mx = ab.take("mx", [P, 3, TB, 2])
        xs = ab.take("xs", [P, TAPS, TB, COLS])
        cw = ab.take("cw", [P, TAPS, COLS])
        mT = [ab.take("mT_hi", [P, 2, S], F32R), ab.take("mT_lo", [P, 2, S], F32R)]

        ac = area()
        cv = ac.take("cv", [P, TB, 2, 3, DV])
        rowb = ac.take("rowb", [P, 2, 2 * TB, P])
        erow = ac.take("erow", [P, 2 * TB, P])
        pq = ac.take("pq", [P, 2 * TB, 2, P])
        early = ac.at
        sl = ac.take("sl", [P, 2 * TB, 4, DV])
        tt = ac.take("tt", [P, 2 * TB, 2, P])
        wT = ac.take("wT", [P, 2 * TB, DV])
        kbe = ac.take("kbe", [P, 2 * TB, DV])
        kd = ac.take("kd", [P, 2 * TB, DV])
        qeT = ac.take("qeT", [P, 2 * TB, 3, P])
        dec = ac.take("dec", [P, 2 * TB, P])
        lt = ac.take("lt", [P, 2 * TB, P])
        m1 = ac.take("m1", [P, 2 * TB, P])
        m2 = ac.take("m2", [P, 2 * TB, P // 2])
        m3 = ac.take("m3", [P, 2 * TB, P])
        st = ac.take("st", [P, 2, 2, DV])
        bb = ac.take("bb", [P, 2, COLS])
        cf = ac.take("cf", [P, 2, 2 * TB])
        gT = [ac.take("gT_hi", [P, 2, S], F32R), ac.take("gT_lo", [P, 2, S], F32R)]

        ad = area()
        oT = [ad.take(name, [P, H, S], F32R) for name in ("oT_lo", "gT_all_hi", "gT_all_lo")]
        assert slab_base + H * S * 4 <= early
        hb = ad.take("hb", [P, TB, COLS])
        ad.at = max(ad.at, ac.at)
        oT.insert(0, ad.take("oT_hi", [P, H, S], F32R))
        ae = area()
        xr = ae.take("xr", [P, 2, TB, COLS])

        acc = [ctx.enter_context(nc.psum_tensor(f"acc{i}", [P, TB, COLS], F32)) for i in range(2)]
        side = ctx.enter_context(nc.psum_tensor("side", [P, 4, COLS], F32))

        ident = cst[:, C_IDENT:C_IDENT + P]
        causal = cst[:, C_CAUSAL:C_CAUSAL + P]
        level0 = cst[:, C_LEVEL:C_LEVEL + P]
        level = lambda n: cst[:, C_LEVEL + (n + 1) * P // 2:C_LEVEL + (n + 2) * P // 2]

        def level_cols(a, n, upper):
            s = LEVELS[n]
            if len(a.shape) == 2:
                return a.rearrange("p (g a s) -> p g a s", a=2, s=s)[:, :, upper, :]
            return a.rearrange("p b (g a s) -> p b g a s", a=2, s=s)[:, :, :, upper, :]

        def packed(a, n):
            s = LEVELS[n]
            if len(a.shape) == 2:
                return a.rearrange("p (g s) -> p g s", s=s)
            return a.rearrange("p b (g s) -> p b g s", s=s)
        eps = cst[:, C_EPS:C_EPS + 1]
        one = cst[:, C_EPS + 1:C_EPS + 2]

        landed = [sem(f"raw_landed{i}") for i in range(RING)]
        hi_done = sem("hi_done")
        lo_done = sem("lo_done")
        tile_used = sem("tile_used")
        emptied = [sem(f"acc_emptied{i}") for i in range(2)]
        gated = [sem(f"acc_gated{i}") for i in range(2)]
        summed = [sem(f"acc_summed{i}") for i in range(2)]
        stored = [sem(f"stage_stored{i}") for i in range(2)]
        s_ident = sem("ident_landed")
        s_const = sem("consts_landed")
        s_x = [sem(f"x_landed{i}") for i in range(D // COLS)]
        s_gain = sem("gains_landed")
        s_bc = sem("rows_landed")
        s_row = sem("scalar_rows_landed")
        s_zero = sem("zero_rows_stored")
        s_gc = sem("gc_stored")
        s_mix = [sem(f"mix_stored{i}") for i in range(4)]
        s_qk = sem("qk_loaded")
        s_v = sem("v_loaded")
        s_zs = sem("zs_loaded")
        s_tap = sem("taps_loaded")
        s_conv = sem("conv_stored")
        s_cv = sem("conv_loaded")
        s_zg = sem("zg_loaded")
        s_gcb = sem("gc_rows_loaded")
        s_bb = sem("gate_bias_loaded")
        PIECES = 4
        s_mla = [sem(f"mla_loaded{i}") for i in range(2)]
        s_gdn = [sem(f"gdn_loaded{i}") for i in range(PIECES)]
        s_gate = [sem(f"gate_loaded{i}") for i in range(2)]
        s_xr = [sem(f"residual_loaded{i}") for i in range(2)]
        s_out = [sem(f"out_stored{i}") for i in range(2)]
        pe_done, act_done, dve_done, pool_done = sem("pe_done"), sem("act_done"), sem("dve_done"), sem("pool_done")
        cp, ca, cd, cg = Count(pe_done), Count(act_done), Count(dve_done), Count(pool_done)

        NG = KD // 2
        NC = (KQ + KKV) // 2
        seq = lambda name, n: " ".join(f"{name}{i}" for i in range(n))
        P0 = cp.phase("x0 gains " + " ".join(f"x{g}" for g in range(1, NG)))
        SQ_AT = 4
        X_LEAD = 3
        A0 = ca.phase(seq("hi", X_LEAD) + " " +
                      " ".join((f"hi{i + X_LEAD} " if i + X_LEAD < NG else "") + (f"sq{i - SQ_AT}" if i >= SQ_AT else "")
                               for i in range(SQ_AT + D // COLS * TB)) + " ln rstd")
        D0 = cd.phase("gcol " + seq("lo", NG) + " sumx")
        P1 = cp.phase("misc cum gct " + seq("c", NC))
        A1 = ca.phase("sumsq0 sumsq1 sumsq2 sumsq3 misc lnq lnkv rstd beta expa expx lnx sin egc ekd glast " + seq("hi", NC))
        D1 = cd.phase("pos ang0 ang1 u0 u1 r0 r1 s1 s2 s3 s4 s5 adt nabs norm0 norm1 norm2 norm3 sp g "
                      "gc gth gth2 kdx gct " + seq("lo", NC))
        G1 = cg.phase("zero")
        TURNS = H // 2
        PAIR = 24
        PB = cp.phase("heads scores probs values turn", TURNS)
        AB = ca.phase("rope sq ln rstd headsT expA expB expC expD probsT hi", TURNS)
        DB = cd.phase("sum unit gain r1 r2 r3 r4 r5 r6 ropeT mask max0 max1 neg rden div gate lo", TURNS)
        lv = range(1, len(LEVELS))
        PC = cp.phase("turns products t1 " + " ".join(f"ma{n} mb{n}" for n in lv) +
                      " solve kv0 ws1 kv1 ws2 kv2 ws3 out1 turn", TURNS)
        AC = ca.phase("silu ln rstd exp erow kT " + " ".join(f"tT{n}" for n in lv if n > 1) +
                      " wT osq oln orstd hi", TURNS)
        DZ = cd.phase("zero zero3")
        DC = cd.phase("sum cq kn qn cke kbe qeT qT lt attn l1 tt1 t1 " +
                      " ".join(f"ma{n} mb{n}" for n in lv) +
                      " u s1 v1 s2a s2b v2 s3a s3b v3 osum on ogate lo", TURNS)
        GB = cg.phase("m0 m1 m2 m3 a1 a2 a3", 12)
        GC = cg.phase("diff below square mask decb vb kd gz", TURNS)
        H_AT = 3
        PD = cp.phase("turn", TURNS)
        AD = ca.phase("hi", TURNS)
        DD = cd.phase("h3 lo", TURNS)

        T_MISC = 3 * KD // ROWS
        T_Z = T_MISC + RING
        T_Q = T_Z + (W // COLS) * KD // ROWS
        T_KV = T_Q + (H * QK // COLS) * KQ // ROWS
        T_B = T_KV + (H * 2 * P // COLS) * KKV // ROWS
        T_ZG = T_B + 12 * KD // ROWS
        T_C = T_ZG + (W // COLS) * KD // ROWS
        T_D = T_C + 16 * KD // ROWS
        T_E = T_D + 8 * 2 * KW // ROWS
        MK = KD // RING
        MN = ROPE + 2 * H
        BEFORE = dict(Z=(2, 2), Q=(4, 4), KV=(7, 7), B=(11, 11), ZG=(17, 17), C=(19, 19))

        def landed_value(turn, t0, s):
            return turn * 16 + (16 * ((t0 + s) // RING + 1) + (16 if t0 >= T_MISC else 0))

        def width(t):
            return MK * MN if T_MISC <= t < T_Z else ROWS * COLS

        block = ctx.enter_context(nc.Block())

        @block.sync
        def _(sp):
            sp.dma_start(cst[:, 0:P], consts[:, 0:P]).then_inc(s_ident, 16)

            def load(t0, turn, per, s, src):
                if not (isinstance(turn, int) and t0 + turn * per + s < RING):
                    sp.wait_ge(lo_done, turn * per + (t0 + s - RING + 1))
                for dst, a in src:
                    sp.dma_start(dst, a).then_inc(landed[s % RING], 16)

            def tile(w, k0, col, s):
                return [(raw[:, s % RING, :].rearrange("p (k n) -> p k n", k=ROWS),
                         rows(w)[:, k0:k0 + ROWS, bass.ds(col, COLS)])]

            def chunks(t0, n, w, col0, kn, per_turn=2):
                per = per_turn * kn // ROWS
                with sp.Fori(0, n // per_turn) as i:
                    for c in range(per_turn):
                        for k in range(kn // ROWS):
                            s = c * (kn // ROWS) + k
                            load(t0, i, per, s, tile(w, k * ROWS, i * (per_turn * COLS) + (col0 + c * COLS), s))

            KT = KD // ROWS
            for s in range(KT):
                load(0, 0, KT, s, tile(w_in, s * ROWS, O_C, s))
                if s == RING - 1:
                    sp.dma_start(cst[:, P:C_ALL], consts[:, P:C_ALL]).then_inc(s_const, 16)
            with sp.Fori(1, 3) as i:
                for s in range(KT):
                    load(0, i, KT, s, tile(w_in, s * ROWS, i * COLS + O_C, s))
            for s in range(RING):
                dst = raw[:, s, 0:MK * MN].rearrange("p (k n) -> p k n", k=MK)
                src = rows(w_in)[:, s * MK:(s + 1) * MK, :]
                load(T_MISC, 0, RING, s, [(dst[:, :, 0:ROPE], src[:, :, O_ROPE:O_ROPE + ROPE]),
                                          (dst[:, :, ROPE:MN], src[:, :, O_BA:O_BA + 2 * H])])
            chunks(T_Z, W // COLS, w_in, O_Z, KD)
            chunks(T_Q, H * QK // COLS, w_q_up, 0, KQ)
            chunks(T_KV, H * 2 * P // COLS, w_kv_up, 0, KKV)
            with sp.Fori(0, 2) as i:
                for s in range(6 * KT):
                    group, kind = s // (3 * KT), s // KT % 3
                    load(T_B, i, 6 * KT, s, tile(w_in, (s % KT) * ROWS, i * (2 * COLS) + (group * COLS + O_QKV + kind * W), s))
                    if s % PAIR == 6:
                        pair = s // PAIR
                        for q in stored:
                            sp.wait_ge(q, 16 * 10)
                        sp.wait_ge(pe_done, PB.after("heads", i * 4 + (pair - 1)))
                        sp.dma_start(qk[:, 0].rearrange("p t h n -> p t (h n)"),
                                     tok(q_d)[:, :, bass.ds(i * (8 * QK) + pair * 2 * QK, 2 * QK)]).then_inc(s_qk, 16)
                        for h in range(2):
                            sp.dma_start(qk[:, 1, :, h, 0:NOPE],
                                         tok(kv_d)[:, :, bass.ds(i * (16 * P) + (pair * 4 + h * 2) * P, P)]).then_inc(s_qk, 16)
                        sp.wait_ge(dve_done, DB.after("gate", i * 4 + (pair - 1)))
                        for h in range(2):
                            sp.dma_start(vt[:, :, h, :],
                                         tok(kv_d)[:, :, bass.ds(i * (16 * P) + (pair * 4 + h * 2 + 1) * P, P)]).then_inc(s_v, 16)
                        sp.dma_start(zs[:].rearrange("p t h n -> p t (h n)"),
                                     tok(z_d)[:, :, bass.ds(i * (8 * DV) + pair * 2 * DV, 2 * DV)]).then_inc(s_zs, 16)
            chunks(T_ZG, W // COLS, w_in, O_ZG, KD)
            with sp.Fori(0, TURNS) as i:
                for s in range(2 * KT):
                    load(T_C, i, 2 * KT, s, tile(w_in, (s % KT) * ROWS, i * (2 * COLS) + (O_GATE + (s // KT) * COLS), s))
                    if s == 0:
                        sp.wait_ge(s_conv, 16 * 2 * 12)
                        for q in s_mix[0:2]:
                            sp.wait_ge(q, 16 * (TURNS + 1))
                        sp.wait_ge(act_done, AC.after("silu", i - 1))
                        sp.dma_start(cv[:].rearrange("p t h j n -> p t (h j n)"),
                                     conv_d.rearrange("(t p) h j n -> p t (h j n)", p=P)
                                     [:, :, bass.ds(i * (6 * DV), 6 * DV)]).then_inc(s_cv, 16)
                        sp.wait_ge(act_done, AC.after("erow", i - 1))
                        sp.wait_ge(pool_done, GC.after("decb", i - 1))
                        sp.dma_start(rowb[:].rearrange("p a b n -> p a (b n)"),
                                     row_d[:, bass.ds(i * 2, 2), :].rearrange("a h s -> a (h s)").partition_broadcast(P)).then_inc(s_gcb, 16)
                    if s == 8:
                        sp.wait_ge(stored[0], 16 * 18)
                        sp.wait_ge(stored[1], 16 * 18)
                        sp.wait_ge(pe_done, PC.after("turn", i - 1))
                        for h in range(2):
                            sp.dma_start(sl[:, h * TB:(h + 1) * TB, 3, :],
                                         tok(zg_d)[:, :, bass.ds(i * (2 * DV) + h * DV, DV)]).then_inc(s_zg, 16)
                        sp.dma_start(bb[:].rearrange("p a n -> p (a n)"),
                                     b_gate.rearrange("a n -> (a n)")[bass.ds(i * (2 * COLS), 2 * COLS)]
                                     .partition_broadcast(P)).then_inc(s_bb, 16)
            with sp.Fori(0, TURNS) as i:
                for s in range(2 * KW // ROWS):
                    w, k = (w_o_mla, s) if s < KW // ROWS else (w_o_gdn, s - KW // ROWS)
                    load(T_D, i, 2 * KW // ROWS, s, tile(w, k * ROWS, i * COLS, s))
            chunks(T_E, 8, w_out, 0, KD)

        @block.tensor
        def _(pe):
            def tiles(t0, turn, per, s0, s1, c, left, kn, k_at=0):
                for s in range(s0, s1):
                    pe.wait_ge(lo_done, turn * per + (t0 + s + 1))
                    for kk in range(ROWS):
                        k = (s * ROWS + kk) % kn
                        for tb in range(TB):
                            o = acc[c][:, tb, :]
                            lh = left[0][:, k_at + k, tb * P:(tb + 1) * P]
                            ll = left[1][:, k_at + k, tb * P:(tb + 1) * P]
                            rh = whi[:, s % RING, kk * COLS:(kk + 1) * COLS]
                            rl = wlo[:, s % RING, kk * COLS:(kk + 1) * COLS]
                            nc.tensor.matmul(o, lh, rh, start=(k == 0), stop=False)
                            nc.tensor.matmul(o, lh, rl, start=False, stop=False)
                            last = nc.tensor.matmul(o, ll, rh, start=False, stop=(k == kn - 1))
                    last.then_inc(tile_used, 1)

            def turn_group(src, g, name, phase, lo_phase):
                if g >= 4:
                    pe.wait_ge(dve_done, lo_phase.after(f"lo{g - 4}"))
                for kk in range(2):
                    for tb in range(TB):
                        k = 2 * g + kk
                        mm = nc.tensor.transpose(side[:, g % 4, kk * S + tb * P:kk * S + (tb + 1) * P],
                                                 src[:, tb, k * P:(k + 1) * P], ident)
                mm.then_inc(pe_done, phase.one(f"{name}{g}"))

            pe.sem_inc(tile_used, 1)
            pe.wait_ge(s_ident, 16)
            NR = KD + KQ + KKV
            KT = KD // ROWS

            def turn_x(g):
                pe.wait_ge(s_x[g // 2], 16)
                turn_group(xin, g, "x", P0, D0)

            turn_x(0)
            pe.wait_ge(s_gain, 48)
            nc.tensor.transpose(acc[0][:, 0, 0:NR], graw[:, :], cst[0:NR, C_IDENT:C_IDENT + NR]).then_inc(pe_done, P0.one("gains"))
            for g in range(1, 4):
                turn_x(g)
            for s in range(KT):
                pe.wait_ge(dve_done, D0.after(f"lo{s}"))
                tiles(0, 0, KT, s, s + 1, 0, xT, KD)
                if s + 4 < NG:
                    turn_x(s + 4)
            tiles(KT, 0, KT, 0, KT, 1, xT, KD)
            pe.wait_ge(emptied[0], 2)
            tiles(2 * KT, 0, KT, 0, KT, 0, xT, KD)
            pe.wait_ge(emptied[1], 2)
            for s in range(RING):
                pe.wait_ge(lo_done, T_MISC + s + 1)
                for kk in range(MK):
                    k = s * MK + kk
                    o = acc[1][0:MN, 0, 0:S]
                    wh, wl = (w[:, s % RING, kk * MN:(kk + 1) * MN] for w in (whi, wlo))
                    nc.tensor.matmul(o, wh, xT[0][:, k, :], start=(k == 0), stop=False)
                    nc.tensor.matmul(o, wh, xT[1][:, k, :], start=False, stop=False)
                    last = nc.tensor.matmul(o, wl, xT[0][:, k, :], start=False, stop=(k == KD - 1))
                last.then_inc(tile_used, 1)

            def plain(t0, n, left, kn, before, k_at=0):
                per = 2 * kn // ROWS
                with pe.Fori(0, n // 2) as i:
                    for c in range(2):
                        pe.wait_ge(emptied[c], i + (before[c] + 1))
                        tiles(t0, i, per, c * per // 2, (c + 1) * per // 2, c, left, kn, k_at=k_at)

            def turn_Z(i, first):
                for s in range(2 * KT):
                    if s % KT == 0:
                        pe.wait_ge(emptied[s // KT], i + (BEFORE["Z"][s // KT] + 1))
                    tiles(T_Z, i, 2 * KT, s, s + 1, s // KT, xT, KD)
                    if not first:
                        continue
                    if s == 1:
                        pe.wait_ge(emptied[1], 3)
                        for tb in range(TB):
                            mm = nc.tensor.transpose(side[:, 0, tb * MN:(tb + 1) * MN], miscT[:, tb * P:(tb + 1) * P], cst[0:MN, C_IDENT:C_IDENT + MN])
                        mm.then_inc(pe_done, P1.one("misc"))
                    if s == 9:
                        pe.wait_ge(dve_done, D1.after("g"))
                        pe.wait_ge(act_done, A1.after("misc"))
                        pe.wait_ge(s_const, 16)
                        for tb in range(TB):
                            g = av[:, 3, tb, :]
                            nc.tensor.matmul(side[:, 0, tb * H:(tb + 1) * H], causal, g, start=True, stop=True)
                            nc.tensor.matmul(side[:, 0, (2 + tb) * H:(3 + tb) * H], cst[:, C_SAME:C_SAME + P], g, start=True, stop=True)
                            for c in range(2):
                                mm = nc.tensor.matmul(side[:, 0, (4 + 2 * tb + c) * H:(5 + 2 * tb + c) * H],
                                                      cst[:, C_HALF + c * P:C_HALF + (c + 1) * P], g, start=True, stop=True)
                        mm.then_inc(pe_done, P1.one("cum"))
                    if s == 12:
                        pe.wait_ge(dve_done, D1.after("gth2"))
                        for a in range(2):
                            for tb in range(TB):
                                mm = nc.tensor.transpose(side[0:H, 1, a * S + tb * P:a * S + (tb + 1) * P], gth[:, a, tb, :], ident)
                        mm.then_inc(pe_done, P1.one("gct"))
                    if 15 <= s < 15 + NC:
                        pe.wait_ge(dve_done, D1.after("gct"))
                        pe.wait_ge(act_done, A1.after("glast"))
                        turn_group(craw, s - 15, "c", P1, D1)

            turn_Z(0, True)
            turn_Z(1, False)
            pe.wait_ge(dve_done, D1.after(f"lo{NC - 1}"))
            plain(T_Q, 6, cT, KQ, BEFORE["Q"])
            plain(T_KV, 8, cT, KKV, BEFORE["KV"], k_at=KQ)

            def attend(i, pair, B):
                turn = i * 4 + pair
                B(0, 12)
                pe.wait_ge(dve_done, DB.after("r6", turn))
                for s in range(2):
                    for h in range(2):
                        for tb in range(TB):
                            n = ((s * 2 + h) * TB + tb) * P
                            nc.tensor.transpose(side[:, n // COLS, n % COLS:n % COLS + P], qk[:, s, tb, h, 0:NOPE], ident)
                            mm = nc.tensor.transpose(side[0:ROPE, 2 + n // COLS, n % COLS:n % COLS + P],
                                                     qk[:, s, tb, h, NOPE:QK], ident)
                mm.then_inc(pe_done, PB.one("heads"))
                B(12, 14)
                pe.wait_ge(act_done, AB.after("headsT", turn))
                pe.wait_ge(dve_done, DB.after("ropeT", turn))
                for h in range(2):
                    for tb in range(TB):
                        o = side[:, h, tb * P:tb * P + (tb + 1) * P]
                        nc.tensor.matmul(o, qkTa[:, 0, h, tb * P:(tb + 1) * P], qkTa[:, 1, h, 0:(tb + 1) * P], start=True, stop=False)
                        mm = nc.tensor.matmul(o, qkTb[:, 0, h, tb * P:(tb + 1) * P], qkTb[:, 1, h, 0:(tb + 1) * P], start=False, stop=True)
                mm.then_inc(pe_done, PB.one("scores"))
                B(14, 17)
                pe.wait_ge(act_done, AB.after("expD", turn))
                for h in range(2):
                    for b in range(3):
                        mm = nc.tensor.transpose(side[:, 2 + h, b * P:(b + 1) * P], sc[:, h, b * P:(b + 1) * P], ident)
                mm.then_inc(pe_done, PB.one("probs"))
                B(17, 19)
                pe.wait_ge(act_done, AB.after("probsT", turn))
                pe.wait_ge(s_v, i * 128 + (pair * 32 + 32))
                for tb in range(TB):
                    for h in range(2):
                        for kb_ in range(tb + 1):
                            mm = nc.tensor.matmul(side[:, 0, (tb * 2 + h) * P:(tb * 2 + h + 1) * P],
                                                  pT[:, h, (tb + kb_) * P:(tb + kb_ + 1) * P], vt[:, kb_, h, :],
                                                  start=(kb_ == 0), stop=(kb_ == tb))
                mm.then_inc(pe_done, PB.one("values"))
                B(19, 21)
                pe.wait_ge(dve_done, DB.after("gate", turn))
                for h in range(2):
                    for tb in range(TB):
                        mm = nc.tensor.transpose(side[:, 1, h * S + tb * P:h * S + (tb + 1) * P], og[:, tb, h, :], ident)
                mm.then_inc(pe_done, PB.one("turn"))
                B(21, PAIR)

            with pe.Fori(0, 2) as i:
                def B(s0, s1):
                    for s in range(s0, s1):
                        chunk = s // KT
                        if s % KT == 0:
                            pe.wait_ge(emptied[chunk % 2], i * 3 + (BEFORE["B"][chunk % 2] + chunk // 2 + 1))
                        tiles(T_B, i, 6 * KT, s, s + 1, chunk % 2, xT, KD)

                for pair in range(4):
                    attend(i, pair, lambda a, b: B(pair * PAIR + a, pair * PAIR + b))
            plain(T_ZG, W // COLS, xT, KD, BEFORE["ZG"])

            pe.wait_ge(dve_done, DB.after("lo", TURNS - 1))
            with pe.Fori(0, TURNS) as i:
                def C(s):
                    if s % KT == 0:
                        pe.wait_ge(emptied[s // KT], BEFORE["C"][s // KT] + 1)
                        pe.wait_ge(gated[s // KT], i + 1)
                    tiles(T_C, i, 2 * KT, s, s + 1, s // KT, xT, KD)

                col = lambda n: side[:, n // COLS, n % COLS:n % COLS + P]
                hb4 = range(2 * TB)
                for s in range(6):
                    C(s)
                pe.wait_ge(dve_done, DC.after("qn", i))
                for n in range(2):
                    for b in hb4:
                        mm = nc.tensor.transpose(side[:, 2 + n, b * P:(b + 1) * P], sl[:, b, 1 - n, :], ident)
                mm.then_inc(pe_done, PC.one("turns"))
                C(6)
                C(7)
                pe.wait_ge(act_done, AC.after("kT", i))
                pe.wait_ge(dve_done, DC.after("qT", i))
                for b in hb4:
                    mm = nc.tensor.matmul(side[:, b // 2, (b % 2) * 2 * P:(b % 2 + 1) * 2 * P], pq[:, b, 0, :],
                                          pq[:, b].rearrange("p a n -> p (a n)"), start=True, stop=True)
                mm.then_inc(pe_done, PC.one("products"))
                C(8)
                C(9)
                pe.wait_ge(dve_done, DC.after("tt1", i))
                for b in hb4:
                    mm = nc.tensor.transpose(side[:, 2, b * P:(b + 1) * P], tt[:, b, 1, :], ident)
                mm.then_inc(pe_done, PC.one("t1"))
                s = 10
                before = "t1"
                for n in lv:
                    C(s)
                    pe.wait_ge(dve_done, DC.after(before, i))
                    for b in hb4:
                        mm = nc.tensor.matmul(packed(side[:, 3, b * P // 2:(b + 1) * P // 2], n), lt[:, b, :],
                                              level_cols(tt[:, b, 0, :], n, 0), start=True, stop=True)
                    if n > 1:
                        for b in hb4:
                            mm = nc.tensor.transpose(side[:, 2, b * P:(b + 1) * P], tt[:, b, 0, :], ident)
                    mm.then_inc(pe_done, PC.one(f"ma{n}"))
                    C(s + 1)
                    pe.wait_ge(dve_done, DC.after(f"ma{n}", i))
                    if n > 1:
                        pe.wait_ge(act_done, AC.after(f"tT{n}", i))
                    for b in hb4:
                        o = packed(side[:, 0, b * P // 2:(b + 1) * P // 2], n)
                        if n < len(LEVELS) - 1:
                            mm = nc.tensor.matmul(o, tt[:, b, 1, :], packed(m2[:, b, :], n), start=True, stop=True)
                        else:
                            mm = nc.tensor.matmul(o, m3[:, b, :], level_cols(tt[:, b, 1, :], n, 1), start=True, stop=True)
                    mm.then_inc(pe_done, PC.one(f"mb{n}"))
                    s += 2
                    before = f"mb{n}"
                C(20)
                pe.wait_ge(dve_done, DC.after(before, i))
                pe.wait_ge(pool_done, GC.after("vb", i))
                for b in hb4:
                    nc.tensor.matmul(side[:, 2, b * P:(b + 1) * P], tt[:, b, 1, :], sl[:, b, 2, :], start=True, stop=True)
                    mm = nc.tensor.matmul(side[:, 3, b * P:(b + 1) * P], kbe[:, b, :], tt[:, b, 1, :], start=True, stop=True)
                mm.then_inc(pe_done, PC.one("solve"))

                def state_add(c):
                    r = slice((c % 2) * CHUNK, (c % 2 + 1) * CHUNK)
                    for h in range(2):
                        b = h * TB + c // 2
                        mm = nc.tensor.matmul(side[:, 1, h * P:(h + 1) * P], kd[r, b, :], sl[r, b, 2, :], start=True, stop=True)
                    return mm

                def from_state(c, name):
                    for h in range(2):
                        b = h * TB + c // 2
                        mm = nc.tensor.matmul(side[:, 0, h * P:(h + 1) * P], wT[:, b, :], st[:, c % 2, h, :], start=True, stop=True)
                    mm.then_inc(pe_done, PC.one(name))

                def block_out(tb):
                    for h in range(2):
                        b = h * TB + tb
                        o = side[:, 2, (tb * 2 + h) * P:(tb * 2 + h + 1) * P]
                        cs = [c for c in (2 * tb, 2 * tb + 1) if c > 0]
                        flat = qeT[:, b].rearrange("p a n -> p (a n)")
                        for c in cs:
                            nc.tensor.matmul(o, flat[:, (c % 2) * P:(c % 2) * P + P], st[:, c % 2, h, :], start=(c == cs[0]), stop=False)
                        mm = nc.tensor.matmul(o, dec[:, b, :], sl[:, b, 2, :], start=False, stop=True)
                    return mm

                C(21)
                pe.wait_ge(dve_done, DC.after("u", i))
                pe.wait_ge(pool_done, GC.after("kd", i))
                state_add(0).then_inc(pe_done, PC.one("kv0"))
                C(22)
                pe.wait_ge(act_done, AC.after("wT", i))
                pe.wait_ge(dve_done, DC.after("s1", i))
                from_state(1, "ws1")
                C(23)
                pe.wait_ge(dve_done, DC.after("v1", i))
                block_out(0)
                state_add(1).then_inc(pe_done, PC.one("kv1"))
                C(24)
                pe.wait_ge(dve_done, DC.after("s2b", i))
                from_state(2, "ws2")
                C(25)
                pe.wait_ge(dve_done, DC.after("v2", i))
                state_add(2).then_inc(pe_done, PC.one("kv2"))
                C(26)
                pe.wait_ge(dve_done, DC.after("s3b", i))
                from_state(3, "ws3")
                C(27)
                pe.wait_ge(dve_done, DC.after("v3", i))
                block_out(1).then_inc(pe_done, PC.one("out1"))
                for s in range(28, 31):
                    C(s)
                pe.wait_ge(dve_done, DC.after("ogate", i))
                for h in range(2):
                    for tb in range(TB):
                        mm = nc.tensor.transpose(side[:, 3, h * S + tb * P:h * S + (tb + 1) * P], sl[:, h * TB + tb, 3, :], ident)
                mm.then_inc(pe_done, PC.one("turn"))
                C(31)

            KO = KW // ROWS

            def turn_h(i_prev):
                pe.wait_ge(dve_done, DD.after("h3", i_prev))
                for k in range(4):
                    for tb in range(TB):
                        mm = nc.tensor.transpose(side[:, k // 2, (k % 2) * S + tb * P:(k % 2) * S + (tb + 1) * P],
                                                 hb[:, tb, k * P:(k + 1) * P], ident)
                mm.then_inc(pe_done, PD.one("turn"))

            for q in s_mla:
                pe.wait_ge(q, 16)
            pe.wait_ge(gated[0], TURNS + 1)
            tiles(T_D, 0, 2 * KO, 0, KO, 0, oT[0:2], KW)
            pe.wait_ge(gated[1], TURNS + 1)
            for n in range(PIECES):
                pe.wait_ge(s_gdn[n], 32)
                tiles(T_D, 0, 2 * KO, KO + n * KO // PIECES, KO + (n + 1) * KO // PIECES, 1, oT[2:4], KW)
            with pe.Fori(1, TURNS) as i:
                pe.wait_ge(gated[0], i + (TURNS + 1))
                tiles(T_D, i, 2 * KO, 0, 3, 0, oT[0:2], KW)
                turn_h(i - 1)
                tiles(T_D, i, 2 * KO, 3, KO, 0, oT[0:2], KW)
                pe.wait_ge(gated[1], i + (TURNS + 1))
                tiles(T_D, i, 2 * KO, KO, 2 * KO, 1, oT[2:4], KW)
            def turn_E(i, first):
                pe.wait_ge(summed[0], i + 1)
                if first:
                    pe.wait_ge(gated[0], 2 * TURNS + 1)
                    pe.wait_ge(dve_done, DD.after("lo", TURNS - 2))
                    tiles(T_E, i, 2 * KT, 0, H_AT, 0, xT, KD)
                    turn_h(TURNS - 1)
                    tiles(T_E, i, 2 * KT, H_AT, KT - 2, 0, xT, KD)
                    pe.wait_ge(dve_done, DD.after("lo", TURNS - 1))
                    tiles(T_E, i, 2 * KT, KT - 2, KT, 0, xT, KD)
                else:
                    tiles(T_E, i, 2 * KT, 0, KT, 0, xT, KD)
                pe.wait_ge(summed[1], i + 1)
                if first:
                    pe.wait_ge(gated[1], 2 * TURNS + 1)
                tiles(T_E, i, 2 * KT, KT, 2 * KT, 1, xT, KD)

            turn_E(0, True)
            with pe.Fori(1, 4) as i:
                turn_E(i, False)

        @block.scalar
        def _(act):
            def hi(t0, turn, per, s):
                act.wait_ge(landed[s % RING], landed_value(turn * (per // RING), t0, s))
                if not (isinstance(turn, int) and t0 + turn * per + s < RING):
                    act.wait_ge(tile_used, turn * per + (t0 + s - RING + 2))
                w = width(t0 + s)
                nc.scalar.copy(whi[:, s % RING, 0:w], raw[:, s % RING, 0:w]).then_inc(hi_done, 1)

            def rsqrt(dst, src, n, phase, ln, rstd, i=0):
                nc.scalar.activation(dst, src, ACT.Ln, bias=eps, scale=1.0 / n).then_inc(act_done, phase.one(ln))
                act.wait_ge(act_done, phase.after(ln, i))
                nc.scalar.activation(dst, dst, ACT.Exp, scale=-0.5).then_inc(act_done, phase.one(rstd))

            for q in emptied:
                act.sem_inc(q, 1)
            for q in (*stored, *s_mix, *s_out):
                act.sem_inc(q, 16)
            NR = KD + KQ + KKV
            nc.scalar.preload_act_table_set(LN_EXP)

            def load_x(n):
                act.dma_start(xin[:, :, n * COLS:(n + 1) * COLS], tok(xf)[:, :, n * COLS:(n + 1) * COLS]).then_inc(s_x[n], 16)

            load_x(0)
            for n in range(1, D // COLS):
                load_x(n)
            act.dma_start(gqk[:, 0, :], g_q_head.partition_broadcast(P)).then_inc(s_bc, 16)
            act.dma_start(gqk[:, 1, :], g_k_head.partition_broadcast(P)).then_inc(s_bc, 16)
            act.dma_start(ggo[:], g_gdn_out.partition_broadcast(P)).then_inc(s_bc, 16)

            def turn_hi(g, src_phase, name, dst, g0, phase):
                act.wait_ge(pe_done, src_phase.after(f"{name}{g}"))
                for kk in range(2):
                    k = 2 * g + kk
                    ins = nc.scalar.activation(dst[:, k, :], side[:, g % 4, kk * S:(kk + 1) * S], ACT.Copy,
                                               scale=gcol[:, g0 + k:g0 + k + 1])
                ins.then_inc(act_done, phase.one(f"hi{g}"))

            def scaled(dst, src, func=ACT.Copy):
                for tb in range(TB):
                    ins = nc.scalar.activation(dst[:, tb, :], src[:, tb, :], func, scale=rx[:, tb:tb + 1])
                return ins

            KT = KD // ROWS
            act.wait_ge(dve_done, D0.after("gcol"))
            for s in range(ACT_LEAD):
                turn_hi(s, P0, "x", xT[0], 0, A0)
                hi(0, 0, RING, s)
            for s in range(2 * KT):
                hi(0, 0, RING, s + ACT_LEAD)
                if s + X_LEAD < NG:
                    turn_hi(s + X_LEAD, P0, "x", xT[0], 0, A0)
                q = s - SQ_AT
                if 0 <= q < D // COLS * TB:
                    n, tb = q // TB, q % TB
                    act.wait_ge(s_x[n], 16)
                    if q:
                        act.wait_ge(act_done, A0.after(f"sq{q - 1}"))
                    nc.scalar.activation(junk[:], xin[:, tb, n * COLS:(n + 1) * COLS], ACT.Square,
                                         accum_out=ss[:, tb * (D // COLS) + n:tb * (D // COLS) + n + 1]).then_inc(act_done, A0.one(f"sq{q}"))
                if s == SQ_AT + D // COLS * TB:
                    act.wait_ge(dve_done, D0.after("sumx"))
                    act.wait_ge(s_const, 16)
                    rsqrt(rx[:], rx[:], D, A0, "ln", "rstd")
                    act.wait_ge(tile_used, KT + 1)
                    act.wait_ge(dve_done, D0.after(f"lo{NG - 1}"))
                    act.wait_ge(act_done, A0.after("rstd"))
                    scaled(craw[:, :, 0:COLS], acc[0]).then_inc(emptied[0], 1)
            act.wait_ge(tile_used, 2 * KT + 1)
            scaled(craw[:, :, COLS:2 * COLS], acc[1]).then_inc(emptied[1], 1)
            for s in range(2 * KT, 3 * KT):
                hi(0, 0, RING, s + ACT_LEAD) if s + ACT_LEAD < T_MISC else hi(T_MISC, 0, RING, s + ACT_LEAD - T_MISC)
            act.wait_ge(tile_used, T_MISC + 1)
            scaled(craw[:, :, 2 * COLS:3 * COLS], acc[0]).then_inc(emptied[0], 1)
            hi(T_MISC, 0, RING, ACT_LEAD)
            for s in range(3):
                hi(T_Z, 0, RING, s)
            act.wait_ge(tile_used, T_Z + 1)
            nc.scalar.copy(miscT[:], acc[1][0:MN, 0, 0:S]).then_inc(emptied[1], 1)

            def plain(t0, n, kn, dst, n_emptied, n_stored, func):
                per = 2 * kn // ROWS
                with act.Fori(0, n // 2) as i:
                    for s in range(per):
                        hi(t0, i, per, s + ACT_LEAD)
                        if (s + 1) % (per // 2) == 0:
                            c = s // (per // 2)
                            store(i * per + (t0 + s + 1), c, i + n_emptied[c], i * 16 + 16 * n_stored[c], dst,
                                  i * (2 * COLS) + c * COLS, func)

            def store(used, c, n_emptied, n_stored, dst, col, func):
                act.wait_ge(tile_used, used + 1)
                act.wait_ge(stored[c], n_stored + 16)
                if func is None:
                    nc.scalar.copy(stage[:, c], acc[c][:]).then_inc(emptied[c], 1)
                else:
                    scaled(stage[:, c], acc[c], func).then_inc(emptied[c], 1)
                act.wait_ge(emptied[c], n_emptied + 2)
                act.dma_start(tok(dst)[:, :, bass.ds(col, COLS)], stage[:, c]).then_inc(stored[c], 16)

            def turn_Z(i, first):
                for s in range(2 * KT):
                    hi(T_Z, i, 2 * KT, s + ACT_LEAD)
                    if (s + 1) % KT == 0:
                        c = s // KT
                        store(i * (2 * KT) + (T_Z + s + 1), c, i + BEFORE["Z"][c], i * 16, z_d, i * (2 * COLS) + c * COLS, ACT.Silu)
                    if not first:
                        continue
                    if s < 2:
                        act.wait_ge(emptied[0], 3)
                        act.wait_ge(emptied[1], 3)
                        for tb in range(TB):
                            n = 2 * s + tb
                            a, b = ((0, RQ), (RQ, RQ + RKV))[s]
                            if n:
                                act.wait_ge(act_done, A1.after(f"sumsq{n - 1}"))
                            nc.scalar.activation(cjunk[:, 0:b - a], craw[:, tb, a:b], ACT.Square,
                                                 accum_out=ss[:, n:n + 1]).then_inc(act_done, A1.one(f"sumsq{n}"))
                    if s == 2:
                        act.wait_ge(pe_done, P1.after("misc"))
                        scaled(misc, side[:, 0, 0:TB * MN].rearrange("p (t n) -> p t n", n=MN)).then_inc(act_done, A1.one("misc"))
                    if s == 3:
                        act.wait_ge(act_done, A1.after("sumsq3"))
                        nc.scalar.activation(rs[:, 0:2], ss[:, 0:2], ACT.Ln, bias=eps, scale=1.0 / RQ).then_inc(act_done, A1.one("lnq"))
                        nc.scalar.activation(rs[:, 2:4], ss[:, 2:4], ACT.Ln, bias=eps, scale=1.0 / RKV).then_inc(act_done, A1.one("lnkv"))
                        act.wait_ge(act_done, A1.after("lnkv"))
                        nc.scalar.activation(rs[:, 0:4], rs[:, 0:4], ACT.Exp, scale=-0.5).then_inc(act_done, A1.one("rstd"))
                    if s == 4:
                        act.wait_ge(act_done, A1.after("misc"))
                        nc.scalar.activation(beta[:].rearrange("p h t -> p t h"), misc[:, :, ROPE:ROPE + H], ACT.Sigmoid).then_inc(act_done, A1.one("beta"))
                        act.wait_ge(s_row, 48)
                        nc.scalar.activation(alg[:, 0, :], alg[:, 0, :], ACT.Exp).then_inc(act_done, A1.one("expa"))
                    if s == 6:
                        act.wait_ge(dve_done, D1.after("nabs"))
                        nc.scalar.activation(av[:, 1], av[:, 1], ACT.Exp).then_inc(act_done, A1.one("expx"))
                        act.wait_ge(act_done, A1.after("expx"))
                        nc.scalar.activation(av[:, 1], av[:, 1], ACT.Ln, bias=one).then_inc(act_done, A1.one("lnx"))
                    if s == 8:
                        nc.scalar.activation(trig[:], ang[:], ACT.Sin).then_inc(act_done, A1.one("sin"))
                    if s == 11:
                        act.wait_ge(pe_done, P1.after("cum"))
                        act.wait_ge(dve_done, D1.after("kdx"))
                        nc.scalar.activation(egc[:], gc[:], ACT.Exp).then_inc(act_done, A1.one("egc"))
                        nc.scalar.activation(ekd[:], ekd[:], ACT.Exp).then_inc(act_done, A1.one("ekd"))
                        nc.scalar.activation(glast[:].rearrange("p h c -> p c h"),
                                             side[:, 0, 4 * H:8 * H].rearrange("p (c h) -> p c h", h=H), ACT.Exp).then_inc(act_done, A1.one("glast"))
                    if s == 14:
                        act.wait_ge(dve_done, D1.after("gct"))
                        act.dma_start(row_d.rearrange("a h s -> h a s"), gcT[:]).then_inc(s_gc, 16)
                    if 16 <= s < 16 + NC:
                        turn_hi(s - 16, P1, "c", cT[0], KD, A1)

            turn_Z(0, True)
            turn_Z(1, False)
            plain(T_Q, 6, KQ, q_d, BEFORE["Q"], (2, 2), None)
            plain(T_KV, 8, KKV, kv_d, BEFORE["KV"], (5, 5), None)
            act.wait_ge(s_gc, 16)

            nc.scalar.preload_act_table_set(LN_EXP)
            with act.Fori(0, 2) as i:
                for slot in range(6 * KT):
                    hi(T_B, i, 6 * KT, slot + ACT_LEAD)
                    pair, s = slot // PAIR, slot % PAIR
                    turn = i * 4 + pair
                    if s == 0:
                        act.wait_ge(pe_done, PB.after("heads", i * 4 + (pair - 1)))
                        nc.scalar.copy(qk[:, 1, :, :, NOPE:QK],
                                       misc[:, :, 0:ROPE].unsqueeze(2).to_broadcast([P, TB, 2, ROPE])).then_inc(act_done, AB.one("rope"))
                    if s == 5:
                        act.wait_ge(s_qk, i * 192 + (48 * pair + 48))
                        act.wait_ge(act_done, AB.after("rope", turn))
                        nc.scalar.activation(sq[:].rearrange("p a t h n -> p (a t h n)"), qk[:].rearrange("p a t h n -> p (a t h n)"),
                                             ACT.Square).then_inc(act_done, AB.one("sq"))
                    if s == 6:
                        act.wait_ge(dve_done, DB.after("sum", turn))
                        rsqrt(rs[:, 0:8], ss[:, 0:8], QK, AB, "ln", "rstd", turn)
                    if s == 11:
                        act.wait_ge(pe_done, PB.after("heads", turn))
                        nc.scalar.copy(qkTa[:].rearrange("p a h n -> p (a h n)"),
                                       side[:, 0:2, :].rearrange("p a n -> p (a n)")).then_inc(act_done, AB.one("headsT"))
                    if s == 14:
                        act.wait_ge(dve_done, DB.after("neg", turn))
                        for n, name in enumerate(("expA", "expB", "expC", "expD")):
                            tb, h = n // 2, n % 2
                            r = sc[:, h, tb * P:tb * P + (tb + 1) * P]
                            nc.scalar.activation(r, r, ACT.Exp, bias=mx[:, 1, tb, h:h + 1],
                                                 accum_out=mx[:, 2, tb, h:h + 1]).then_inc(act_done, AB.one(name))
                    if s == 16:
                        act.wait_ge(pe_done, PB.after("probs", turn))
                        nc.scalar.copy(pT[:], side[:, 2:4, 0:3 * P]).then_inc(act_done, AB.one("probsT"))
                    if (slot + 1) % KT == 0:
                        n = slot // KT
                        c = n % 2
                        store(i * (6 * KT) + (T_B + slot + 1), c, i * 3 + (BEFORE["B"][c] + n // 2), i * 48 + 16 * (9 + n // 2),
                              g_d[TAPS - 1:TAPS - 1 + S, :], i * (2 * COLS) + (n // 3 * COLS + n % 3 * W), ACT.Copy)
                    if s == 20:
                        act.wait_ge(pe_done, PB.after("turn", turn))
                        for q in s_mix[0:2]:
                            act.wait_ge(q, i * 64 + (16 * pair + 16))
                        nc.scalar.copy(mT[0][:].rearrange("p h n -> p (h n)"), side[:, 1, :]).then_inc(act_done, AB.one("hi"))
                    if s == 22:
                        act.wait_ge(dve_done, DB.after("lo", turn))
                        for n in range(2):
                            act.dma_start(mix_d[n][:, bass.ds(i * 8 + pair * 2, 2), :], mT[n][:].bitcast(F32)).then_inc(s_mix[n], 16)

            plain(T_ZG, 4, KD, zg_d, BEFORE["ZG"], (15, 15), ACT.Silu)

            nc.scalar.preload_act_table(ACT.Sigmoid)
            with act.Fori(0, TURNS) as i:
                for s in range(2 * KT):
                    hi(T_C, i, 2 * KT, s + ACT_LEAD)
                    if s == 1:
                        act.wait_ge(s_cv, i * 16 + 16)
                        act.wait_ge(pe_done, PC.after("turn", i - 1))
                        nc.scalar.activation(sl[:, :, 0:3, :].rearrange("p (h t) j n -> p t h (j n)", h=2),
                                             cv[:].rearrange("p t h j n -> p t h (j n)"), ACT.Silu).then_inc(act_done, AC.one("silu"))
                    if s == 3:
                        nc.scalar.preload_act_table_set(LN_EXP)
                        act.wait_ge(dve_done, DC.after("sum", i))
                        nc.scalar.activation(rs[:, 0:8], ss[:, 0:8], ACT.Ln, bias=eps).then_inc(act_done, AC.one("ln"))
                        act.wait_ge(act_done, AC.after("ln", i))
                        nc.scalar.activation(rs[:, 0:8], rs[:, 0:8], ACT.Exp, scale=-0.5).then_inc(act_done, AC.one("rstd"))
                    if s == 4:
                        act.wait_ge(pool_done, GC.after("below", i))
                        nc.scalar.activation(dec[:], dec[:], ACT.Exp).then_inc(act_done, AC.one("exp"))
                        act.wait_ge(s_gcb, i * 16 + 16)
                        nc.scalar.activation(erow[:], rowb[:, 0], ACT.Exp).then_inc(act_done, AC.one("erow"))
                    if s == 6:
                        act.wait_ge(pe_done, PC.after("turns", i))
                        nc.scalar.copy(pq[:, :, 0, :], side[:, 2, :].rearrange("p (b n) -> p b n", n=P)).then_inc(act_done, AC.one("kT"))
                    if 12 <= s < 20 and s % 2 == 0:
                        n = 1 + (s - 10) // 2
                        act.wait_ge(pe_done, PC.after(f"ma{n}", i))
                        nc.scalar.copy(tt[:, :, 1, :], side[:, 2, :].rearrange("p (b n) -> p b n", n=P)).then_inc(act_done, AC.one(f"tT{n}"))
                    if s == 21:
                        act.wait_ge(pe_done, PC.after("solve", i))
                        nc.scalar.copy(wT[:].rearrange("p b n -> p (b n)"), side[:, 3, :]).then_inc(act_done, AC.one("wT"))
                    if s == 15 or s == 31:
                        c = s // KT
                        act.wait_ge(gated[c], i + 2)
                        nc.scalar.activation(stage[:, c], stage[:, c], ACT.Sigmoid).then_inc(emptied[c], 1)
                        act.wait_ge(emptied[c], i + (BEFORE["C"][c] + 2))
                        act.dma_start(tok(gate_d)[:, :, bass.ds(i * (2 * COLS) + c * COLS, COLS)], stage[:, c]).then_inc(stored[c], 16)
                    if s == 28:
                        act.wait_ge(pe_done, PC.after("out1", i))
                        nc.scalar.activation(m1[:].rearrange("p b n -> p (b n)"), side[:, 2, :], ACT.Square).then_inc(act_done, AC.one("osq"))
                        nc.scalar.preload_act_table_set(LN_EXP)
                        act.wait_ge(dve_done, DC.after("osum", i))
                        rsqrt(rs[:, 0:4], ss[:, 0:4], DV, AC, "oln", "orstd", i)
                    if s == 30:
                        act.wait_ge(pe_done, PC.after("turn", i))
                        for q in s_mix[2:4]:
                            act.wait_ge(q, i * 16 + 16)
                        nc.scalar.copy(gT[0][:].rearrange("p h n -> p (h n)"), side[:, 3, :]).then_inc(act_done, AC.one("hi"))
                    if s == 31:
                        act.wait_ge(dve_done, DC.after("lo", i))
                        for n in range(2):
                            act.dma_start(mix_d[2 + n][:, bass.ds(i * 2, 2), :], gT[n][:].bitcast(F32)).then_inc(s_mix[2 + n], 16)

            def hT_hi(i_prev):
                act.wait_ge(pe_done, PD.after("turn", i_prev))
                nc.scalar.copy(xT[0][:, bass.ds(i_prev * 4, 4), :].rearrange("p k n -> p (k n)"),
                               side[:, 0:2, :].rearrange("p a n -> p (a n)")).then_inc(act_done, AD.one("hi"))

            KO = KW // ROWS
            for s in range(2 * KO):
                hi(T_D, 0, 2 * KO, s + ACT_LEAD)
            with act.Fori(1, TURNS) as i:
                for s in range(2 * KO):
                    hi(T_D, i, 2 * KO, s + ACT_LEAD)
                    if s == H_AT:
                        hT_hi(i - 1)

            def turn_E(i, first, last):
                for s in range(2 * KT):
                    if not last or s + ACT_LEAD < 2 * KT:
                        hi(T_E, i, 2 * KT, s + ACT_LEAD)
                    if first and s == H_AT:
                        hT_hi(TURNS - 1)
                    if (s + 1) % KT == 0:
                        c = s // KT
                        act.wait_ge(summed[c], i + 2)
                        act.dma_start(tok(outf)[:, :, bass.ds(i * (2 * COLS) + c * COLS, COLS)], stage[:, c]).then_inc(s_out[c], 16)

            turn_E(0, True, False)
            with act.Fori(1, 3) as i:
                turn_E(i, False, False)
            turn_E(3, False, True)
            for q in s_out:
                act.wait_ge(q, 64 + 16)
            for q in s_mix:
                act.wait_ge(q, 16 * (TURNS + 1))
            for q in stored:
                act.wait_ge(q, 16 * 26)

        @block.vector
        def _(dve):
            V = nc.vector

            def lo(t0, turn, per, s):
                dve.wait_ge(hi_done, turn * per + (t0 + s + 1))
                w = width(t0 + s)
                V.tensor_tensor(wlo[:, s % RING, 0:w], raw[:, s % RING, 0:w], whi[:, s % RING, 0:w].bitcast(F32),
                                ALU.subtract).then_inc(lo_done, 1)

            for q in (*gated, *summed):
                dve.sem_inc(q, 1)
            dve.wait_ge(pe_done, P0.after("gains"))
            NR = KD + KQ + KKV
            V.tensor_copy(gcol[:], acc[0][:, 0, 0:NR]).then_inc(dve_done, D0.one("gcol"))
            dve.wait_ge(dve_done, D0.after("gcol"))

            def turn_lo(g, dst, g0, a_phase, phase):
                dve.wait_ge(act_done, a_phase.after(f"hi{g}"))
                for kk in range(2):
                    k = 2 * g + kk
                    ins = V.scalar_tensor_tensor(out=dst[1][:, k, :], in0=side[:, g % 4, kk * S:(kk + 1) * S],
                                                 scalar=gcol[:, g0 + k:g0 + k + 1], in1=dst[0][:, k, :].bitcast(F32),
                                                 op0=ALU.mult, op1=ALU.subtract)
                ins.then_inc(dve_done, phase.one(f"lo{g}"))

            KT = KD // ROWS
            for s in range(DVE_LEAD):
                turn_lo(s, xT, 0, A0, D0)
                lo(0, 0, RING, s)
            for s in range(3 * KT + RING):
                t = s + DVE_LEAD
                if t < NG:
                    turn_lo(t, xT, 0, A0, D0)
                lo(0, 0, RING, t) if t < T_MISC else lo(T_MISC, 0, RING, t - T_MISC) if t < T_Z else lo(T_Z, 0, RING, t - T_Z)
                if s == SQ_AT + D // COLS * TB - 1:
                    dve.wait_ge(act_done, A0.after(f"sq{D // COLS * TB - 1}"))
                    V.tensor_reduce(rx[:], ss[:].rearrange("p (t n) -> p t n", t=TB), AX, ALU.add).then_inc(dve_done, D0.one("sumx"))

            TWO_PI = 2.0 * np.pi
            MAGIC = 1.5 * 2.0 ** 23
            PART1 = 6.28125
            PART2 = float(np.float32(np.round((TWO_PI - PART1) * 2.0 ** 21) / 2.0 ** 21))
            PART3 = float(np.float32(TWO_PI - PART1 - PART2))

            def norm(n):
                a, b = ((0, RQ), (RQ, RQ + RKV))[n // TB]
                V.tensor_scalar(craw[:, n % TB, a:b], craw[:, n % TB, a:b], rs[:, n:n + 1], None, ALU.mult).then_inc(dve_done, D1.one(f"norm{n}"))

            def turn_Z(i, first):
                for s in range(2 * KT):
                    lo(T_Z, i, 2 * KT, s + DVE_LEAD)
                    if not first:
                        continue
                    if s == 1:
                        dve.wait_ge(s_row, 48)
                        dve.wait_ge(s_const, 16)
                        V.tensor_copy(pos_f[:], pos_i[:]).then_inc(dve_done, D1.one("pos"))
                        dve.wait_ge(dve_done, D1.after("pos"))
                        for tb in range(TB):
                            V.tensor_scalar(ang[:, :, tb, :], cst[:, C_FREQ:C_FREQ + HALF].unsqueeze(1).to_broadcast([P, 2, HALF]),
                                            pos_f[:, tb:tb + 1], None, ALU.mult).then_inc(dve_done, D1.one(f"ang{tb}"))
                    if s == 2:
                        dve.wait_ge(dve_done, D1.after("ang1"))
                        V.tensor_scalar(whole[:, 0], ang[:, 0], 1.0 / TWO_PI, 0.25, ALU.mult, ALU.add).then_inc(dve_done, D1.one("u0"))
                        V.tensor_scalar(whole[:, 1], ang[:, 1], 1.0 / TWO_PI, None, ALU.mult).then_inc(dve_done, D1.one("u1"))
                        dve.wait_ge(dve_done, D1.after("u1"))
                        V.tensor_scalar(whole[:], whole[:], MAGIC, None, ALU.add).then_inc(dve_done, D1.one("r0"))
                        dve.wait_ge(dve_done, D1.after("r0"))
                        V.tensor_scalar(whole[:], whole[:], MAGIC, None, ALU.subtract).then_inc(dve_done, D1.one("r1"))
                    if s == 3:
                        for part, name, before in ((PART1, "s1", "r1"), (PART2, "s2", "s1"), (PART3, "s3", "s2")):
                            dve.wait_ge(dve_done, D1.after(before))
                            V.scalar_tensor_tensor(out=ang[:], in0=whole[:], scalar=-part, in1=ang[:], op0=ALU.mult, op1=ALU.add).then_inc(dve_done, D1.one(name))
                        dve.wait_ge(dve_done, D1.after("s3"))
                        V.tensor_scalar(ang[:, 0], ang[:, 0], np.pi / 2, None, ALU.add).then_inc(dve_done, D1.one("s4"))
                        dve.wait_ge(dve_done, D1.after("s4"))
                        V.tensor_scalar(ang[:], ang[:], 3.1415925, -3.1415925, ALU.min, ALU.max).then_inc(dve_done, D1.one("s5"))
                    if s == 4:
                        dve.wait_ge(act_done, A1.after("misc"))
                        V.tensor_tensor(av[:, 0], misc[:, :, ROPE + H:MN], alg[:, 1:2, :].to_broadcast([P, TB, H]), ALU.add).then_inc(dve_done, D1.one("adt"))
                        dve.wait_ge(dve_done, D1.after("adt"))
                        V.scalar_tensor_tensor(out=av[:, 1], in0=av[:, 0], scalar=-1.0, in1=av[:, 0], op0=ALU.mult, op1=ALU.min).then_inc(dve_done, D1.one("nabs"))
                        dve.wait_ge(act_done, A1.after("rstd"))
                        norm(0)
                    if s == 5:
                        norm(1)
                    if s == 6:
                        norm(2)
                        norm(3)
                    if s == 7:
                        dve.wait_ge(act_done, A1.after("lnx"))
                        V.scalar_tensor_tensor(out=av[:, 2], in0=av[:, 0], scalar=0.0, in1=av[:, 1], op0=ALU.max, op1=ALU.add).then_inc(dve_done, D1.one("sp"))
                        dve.wait_ge(dve_done, D1.after("sp"))
                        V.scalar_tensor_tensor(out=av[:, 3], in0=av[:, 2], scalar=-1.0, in1=alg[:, 0:1, :].to_broadcast([P, TB, H]),
                                               op0=ALU.mult, op1=ALU.mult).then_inc(dve_done, D1.one("g"))
                    if s == 10:
                        sums = side[:, 0, 0:4 * H].rearrange("p (a t h) -> p a t h", a=2, h=H)
                        dve.wait_ge(pe_done, P1.after("cum"))
                        V.tensor_copy(gc[:].rearrange("p h t -> p t h"), sums[:, 0]).then_inc(dve_done, D1.one("gc"))
                        V.tensor_copy(gth[:, 0], sums[:, 0]).then_inc(dve_done, D1.one("gth"))
                        V.tensor_copy(gth[:, 1], beta[:].rearrange("p h t -> p t h")).then_inc(dve_done, D1.one("gth2"))
                        dve.wait_ge(dve_done, D1.after("gc"))
                        V.tensor_tensor(ekd[:].rearrange("p h t -> p t h"), sums[:, 1], gc[:].rearrange("p h t -> p t h"),
                                        ALU.subtract).then_inc(dve_done, D1.one("kdx"))
                    if s == 13:
                        dve.wait_ge(pe_done, P1.after("gct"))
                        V.tensor_copy(gcT[:].rearrange("h a s -> h (a s)"), side[0:H, 1, :]).then_inc(dve_done, D1.one("gct"))
                    if 16 <= s < 16 + NC:
                        turn_lo(s - 16, cT, KD, A1, D1)

            def plain(t0, n, kn):
                per = 2 * kn // ROWS
                with dve.Fori(0, n // 2) as i:
                    for s in range(per):
                        lo(t0, i, per, s + DVE_LEAD)

            turn_Z(0, True)
            turn_Z(1, False)
            plain(T_Q, 6, KQ)
            plain(T_KV, 8, KKV)

            SCALE = float(QK) ** -0.5
            with dve.Fori(0, 2) as i:
                def after(name):
                    dve.wait_ge(dve_done, DB.after(name, turn))
                for slot in range(6 * KT):
                    lo(T_B, i, 6 * KT, slot + DVE_LEAD)
                    pair, s = slot // PAIR, slot % PAIR
                    turn = i * 4 + pair
                    flat = qk[:].rearrange("p a t h n -> p (a t h) n")
                    sqf = sq[:].rearrange("p a t h n -> p (a t h) n")
                    if s == 5:
                        dve.wait_ge(act_done, AB.after("sq", turn))
                        V.tensor_reduce(ss[:, 0:8], sqf, AX, ALU.add).then_inc(dve_done, DB.one("sum"))
                    if s == 6:
                        dve.wait_ge(act_done, AB.after("rstd", turn))
                        V.tensor_tensor(flat, flat, rs[:, 0:8].unsqueeze(2).to_broadcast([P, 8, QK]), ALU.mult).then_inc(dve_done, DB.one("unit"))
                    if s == 7:
                        after("unit")
                        dve.wait_ge(s_bc, 48)
                        V.tensor_tensor(qk[:].rearrange("p a t h n -> p a (t h) n"), qk[:].rearrange("p a t h n -> p a (t h) n"),
                                        gqk[:].unsqueeze(2).to_broadcast([P, 2, 2 * TB, QK]), ALU.mult).then_inc(dve_done, DB.one("gain"))
                    if s == 8:
                        after("gain")
                        x1 = qk[:, :, :, :, NOPE:NOPE + HALF]
                        x2 = qk[:, :, :, :, NOPE + HALF:QK]
                        tg = lambda n, a: trig[:, n].unsqueeze(2).to_broadcast([P, TB, 2, HALF])
                        r = lambda n, a: rt[:, n, 4 * a:4 * a + 4, :].rearrange("p (t h) n -> p t h n", h=2)
                        for n, (xx, f, name) in enumerate(((x1, 0, "r1"), (x2, 1, "r2"), (x2, 0, "r3"), (x1, 1, "r4"))):
                            V.tensor_tensor(r(n, 0), xx[:, 0], tg(f, 0), ALU.mult)
                            V.tensor_tensor(r(n, 1), xx[:, 1], tg(f, 1), ALU.mult).then_inc(dve_done, DB.one(name))
                    if s == 9:
                        after("r4")
                        rr = lambda n: rt[:, n].rearrange("p (a b) n -> p a b n", a=2)
                        v = lambda t: t.rearrange("p a t h n -> p a (t h) n")
                        V.tensor_tensor(v(x1), rr(0), rr(1), ALU.subtract).then_inc(dve_done, DB.one("r5"))
                        V.tensor_tensor(v(x2), rr(2), rr(3), ALU.add).then_inc(dve_done, DB.one("r6"))
                    if s == 11:
                        dve.wait_ge(pe_done, PB.after("heads", turn))
                        V.tensor_copy(qkTb[:].rearrange("p a h n -> p (a h n)"),
                                      side[0:ROPE, 2:4, :].rearrange("p a n -> p (a n)")).then_inc(dve_done, DB.one("ropeT"))
                    if s == 13:
                        dve.wait_ge(pe_done, PB.after("scores", turn))
                        V.scalar_tensor_tensor(out=sc[:], in0=side[:, 0:2, 0:3 * P], scalar=SCALE,
                                               in1=cst[:, C_MASK:C_MASK + 3 * P].unsqueeze(1).to_broadcast([P, 2, 3 * P]),
                                               op0=ALU.mult, op1=ALU.add).then_inc(dve_done, DB.one("mask"))
                        after("mask")
                        V.tensor_reduce(mx[:, 0, 0, :], sc[:, :, 0:P], AX, ALU.max).then_inc(dve_done, DB.one("max0"))
                        V.tensor_reduce(mx[:, 0, 1, :], sc[:, :, P:3 * P], AX, ALU.max).then_inc(dve_done, DB.one("max1"))
                        after("max1")
                        V.tensor_scalar(mx[:, 1], mx[:, 0], -1.0, None, ALU.mult).then_inc(dve_done, DB.one("neg"))
                    if s == 18:
                        dve.wait_ge(act_done, AB.after("expD", turn))
                        V.reciprocal(mx[:, 0], mx[:, 2]).then_inc(dve_done, DB.one("rden"))
                        after("rden")
                        dve.wait_ge(pe_done, PB.after("values", turn))
                        ogf = og[:].rearrange("p t h n -> p (t h) n")
                        V.tensor_tensor(ogf, side[:, 0, :].rearrange("p (b n) -> p b n", n=P),
                                        mx[:, 0].rearrange("p t h -> p (t h)").unsqueeze(2).to_broadcast([P, 2 * TB, DV]),
                                        ALU.mult).then_inc(dve_done, DB.one("div"))
                        after("div")
                        dve.wait_ge(s_zs, i * 64 + (16 * pair + 16))
                        V.tensor_tensor(og[:], og[:], zs[:], ALU.mult).then_inc(dve_done, DB.one("gate"))
                    if s == 20:
                        dve.wait_ge(act_done, AB.after("hi", turn))
                        V.tensor_tensor(mT[1][:].rearrange("p h n -> p (h n)"), side[:, 1, :],
                                        mT[0][:].rearrange("p h n -> p (h n)").bitcast(F32), ALU.subtract).then_inc(dve_done, DB.one("lo"))

            plain(T_ZG, W // COLS, KD)

            for q in s_mix[0:2]:
                dve.wait_ge(q, 16 * (TURNS + 1))
            dve.wait_ge(s_conv, 16 * 2 * 12)
            V.memset(qeT[:], 0.0).then_inc(dve_done, DZ.one("zero"))
            V.memset(m3[:], 0.0).then_inc(dve_done, DZ.one("zero3"))
            bc = lambda a: a.unsqueeze(2).to_broadcast([P, 2 * TB, DV])
            with dve.Fori(0, TURNS) as i:
                def after(name):
                    dve.wait_ge(dve_done, DC.after(name, i))

                def of_pair(a):
                    return a[:, bass.ds(i * 2, 2), :].rearrange("p h t -> p (h t)")
                rk = rs[:, 0:8].rearrange("p (b j) -> p b j", j=2)
                for s in range(2 * KT):
                    lo(T_C, i, 2 * KT, s + DVE_LEAD)
                    if s == 3:
                        dve.wait_ge(pool_done, GC.after("square", i))
                        V.tensor_reduce(ss[:, 0:8], tt[:].rearrange("p b j n -> p (b j) n"), AX, ALU.add).then_inc(dve_done, DC.one("sum"))
                    if s == 4:
                        dve.wait_ge(act_done, AC.after("rstd", i))
                        V.tensor_scalar(cf[:, 0], rk[:, :, 0], float(DV) ** -0.5, None, ALU.mult).then_inc(dve_done, DC.one("cq"))
                        V.tensor_tensor(sl[:, :, 1, :], sl[:, :, 1, :], bc(rk[:, :, 1]), ALU.mult).then_inc(dve_done, DC.one("kn"))
                        after("cq")
                        V.tensor_tensor(sl[:, :, 0, :], sl[:, :, 0, :], bc(cf[:, 0]), ALU.mult).then_inc(dve_done, DC.one("qn"))
                    if s == 5:
                        V.tensor_tensor(cf[:, 1], of_pair(beta), of_pair(egc), ALU.mult).then_inc(dve_done, DC.one("cke"))
                        after("cke")
                        V.tensor_tensor(kbe[:], sl[:, :, 1, :], bc(cf[:, 1]), ALU.mult).then_inc(dve_done, DC.one("kbe"))
                    if s == 6:
                        dve.wait_ge(pe_done, PC.after("turns", i))
                        dve.wait_ge(act_done, AC.after("erow", i))
                        dve.wait_ge(dve_done, DZ.after("zero3"))
                        V.tensor_tensor(qeT[:].rearrange("p b a n -> p b (a n)").rearrange("p b (c n) -> p b c n", c=2)[:, :, :, 0:CHUNK],
                                        side[:, 3, :].rearrange("p (b c n) -> p b c n", c=2, n=CHUNK),
                                        erow[:].rearrange("p b (c n) -> p b c n", c=2), ALU.mult).then_inc(dve_done, DC.one("qeT"))
                        V.tensor_copy(pq[:, :, 1, :], side[:, 3, :].rearrange("p (b n) -> p b n", n=P)).then_inc(dve_done, DC.one("qT"))
                    if s == 8:
                        dve.wait_ge(pe_done, PC.after("products", i))
                        pr = side[:, 0:2, :].rearrange("p a (b j n) -> p (a b) j n", j=2, n=P)
                        dve.wait_ge(pool_done, GC.after("decb", i))
                        V.tensor_tensor(lt[:], pr[:, :, 0, :], lt[:], ALU.mult).then_inc(dve_done, DC.one("lt"))
                        V.tensor_tensor(dec[:], pr[:, :, 1, :], dec[:], ALU.mult).then_inc(dve_done, DC.one("attn"))
                        after("lt")
                        V.tensor_tensor(m1[:], lt[:], level0.unsqueeze(1).to_broadcast([P, 2 * TB, P]), ALU.mult).then_inc(dve_done, DC.one("l1"))
                        after("l1")
                        V.tensor_tensor(tt[:, :, 1, :], ident.unsqueeze(1).to_broadcast([P, 2 * TB, P]), m1[:], ALU.subtract).then_inc(dve_done, DC.one("tt1"))
                    if s == 9:
                        dve.wait_ge(pe_done, PC.after("t1", i))
                        V.tensor_copy(tt[:, :, 0, :], side[:, 2, :].rearrange("p (b n) -> p b n", n=P)).then_inc(dve_done, DC.one("t1"))
                    if 10 <= s < 20:
                        n = 1 + (s - 10) // 2
                        if s % 2 == 0:
                            dve.wait_ge(pe_done, PC.after(f"ma{n}", i))
                            o = m2[:] if n < len(LEVELS) - 1 else level_cols(m3[:], n, 0)
                            f = lambda a: a if n < len(LEVELS) - 1 else packed(a, n)
                            V.tensor_tensor(o, f(side[:, 3, 0:2 * TB * P // 2].rearrange("p (b n) -> p b n", n=P // 2)),
                                            f(level(n).unsqueeze(1).to_broadcast([P, 2 * TB, P // 2])), ALU.mult).then_inc(dve_done, DC.one(f"ma{n}"))
                        else:
                            dve.wait_ge(pe_done, PC.after(f"mb{n}", i))
                            t = level_cols(tt[:, :, 0, :], n, 0) if n < len(LEVELS) - 1 else level_cols(tt[:, :, 1, :], n, 1)
                            V.tensor_tensor(t, t, packed(side[:, 0, 0:2 * TB * P // 2].rearrange("p (b n) -> p b n", n=P // 2), n),
                                            ALU.subtract).then_inc(dve_done, DC.one(f"mb{n}"))
                    if s == 20:
                        dve.wait_ge(pe_done, PC.after("solve", i))
                        V.tensor_copy(sl[:, :, 2, :], side[:, 2, :].rearrange("p (b n) -> p b n", n=P)).then_inc(dve_done, DC.one("u"))

                    def state(c, names):
                        for h in range(2):
                            V.scalar_tensor_tensor(out=st[:, c % 2, h, :], in0=st[:, (c - 1) % 2, h, :],
                                                   scalar=glast[:, bass.ds(i * 2 + h, 1), c - 1], in1=side[:, 1, h * P:(h + 1) * P],
                                                   op0=ALU.mult, op1=ALU.add).then_inc(dve_done, DC.one(names[h]))

                    def new_v(c, name):
                        r = slice((c % 2) * CHUNK, (c % 2 + 1) * CHUNK)
                        v = sl[:].rearrange("p (h t) j n -> p h t j n", t=TB)[r, :, c // 2, 2, :]
                        V.tensor_tensor(v, v, side[r, 0, 0:2 * P].rearrange("p (h n) -> p h n", n=P), ALU.subtract).then_inc(dve_done, DC.one(name))

                    if s == 21:
                        dve.wait_ge(pe_done, PC.after("kv0", i))
                        V.tensor_copy(st[:, 1].rearrange("p h n -> p (h n)"), side[:, 1, 0:2 * P]).then_inc(dve_done, DC.one("s1"))
                    if s == 22:
                        dve.wait_ge(pe_done, PC.after("ws1", i))
                        new_v(1, "v1")
                    if s == 23:
                        dve.wait_ge(pe_done, PC.after("kv1", i))
                        state(2, ("s2a", "s2b"))
                    if s == 24:
                        dve.wait_ge(pe_done, PC.after("ws2", i))
                        new_v(2, "v2")
                    if s == 25:
                        dve.wait_ge(pe_done, PC.after("kv2", i))
                        state(3, ("s3a", "s3b"))
                    if s == 26:
                        dve.wait_ge(pe_done, PC.after("ws3", i))
                        new_v(3, "v3")
                    if s == 28:
                        dve.wait_ge(act_done, AC.after("osq", i))
                        V.tensor_reduce(ss[:, 0:4], m1[:], AX, ALU.add).then_inc(dve_done, DC.one("osum"))
                    if s == 29:
                        dve.wait_ge(act_done, AC.after("orstd", i))
                        dve.wait_ge(pool_done, GC.after("gz", i))
                        V.tensor_tensor(m1[:], side[:, 2, :].rearrange("p (b n) -> p b n", n=P), bc(rs[:, 0:4]), ALU.mult).then_inc(dve_done, DC.one("on"))
                        after("on")
                        z = sl[:].rearrange("p (h t) j n -> p t h j n", t=TB)[:, :, :, 3, :]
                        V.tensor_tensor(z, z, m1[:].rearrange("p (t h) n -> p t h n", h=2), ALU.mult).then_inc(dve_done, DC.one("ogate"))
                    if s == 30:
                        dve.wait_ge(act_done, AC.after("hi", i))
                        V.tensor_tensor(gT[1][:].rearrange("p h n -> p (h n)"), side[:, 3, :],
                                        gT[0][:].rearrange("p h n -> p (h n)").bitcast(F32), ALU.subtract).then_inc(dve_done, DC.one("lo"))
                    if s == 15 or s == 31:
                        c = s // KT
                        dve.wait_ge(tile_used, i * (2 * KT) + (T_C + s + 2))
                        dve.wait_ge(s_bb, i * 16 + 16)
                        dve.wait_ge(stored[c], i * 16 + 16 * 18)
                        for tb in range(TB):
                            ins = V.scalar_tensor_tensor(out=stage[:, c, tb, :], in0=acc[c][:, tb, :], scalar=rx[:, tb:tb + 1], in1=bb[:, c, :],
                                                         op0=ALU.mult, op1=ALU.add)
                        ins.then_inc(gated[c], 1)

            KO = KW // ROWS

            def turn_D(i, previous):
                for s in range(2 * KO):
                    lo(T_D, i, 2 * KO, s + DVE_LEAD)
                    if s == 3 and previous:
                        dve.wait_ge(act_done, AD.after("hi", i - 1))
                        hT_lo(i - 1)
                    if s == KO - 1:
                        dve.wait_ge(tile_used, i * (2 * KO) + (T_D + KO + 1))
                        dve.wait_ge(s_gate[0], i * 16 + 16)
                        V.tensor_tensor(stage[:, 0], acc[0][:], stage[:, 0], ALU.mult).then_inc(gated[0], 1)
                    if s == 2 * KO - 1:
                        dve.wait_ge(tile_used, i * (2 * KO) + (T_D + 2 * KO + 1))
                        dve.wait_ge(s_gate[1], i * 16 + 16)
                        V.tensor_tensor(stage[:, 1], acc[1][:], stage[:, 1], ALU.mult).then_inc(gated[1], 1)
                        dve.wait_ge(gated[1], i + (TURNS + 2))
                        V.tensor_tensor(hb[:], stage[:, 0], stage[:, 1], ALU.add).then_inc(dve_done, DD.one("h3"))

            def hT_lo(i_prev):
                V.tensor_tensor(xT[1][:, bass.ds(i_prev * 4, 4), :].rearrange("p k n -> p (k n)"),
                                side[:, 0:2, :].rearrange("p a n -> p (a n)"),
                                xT[0][:, bass.ds(i_prev * 4, 4), :].rearrange("p k n -> p (k n)").bitcast(F32),
                                ALU.subtract).then_inc(dve_done, DD.one("lo"))

            turn_D(0, False)
            with dve.Fori(1, TURNS) as i:
                turn_D(i, True)

            def turn_E(i, first, last):
                for s in range(2 * KT):
                    if not last or s + DVE_LEAD < 2 * KT:
                        lo(T_E, i, 2 * KT, s + DVE_LEAD)
                    if first and s == H_AT:
                        dve.wait_ge(act_done, AD.after("hi", TURNS - 1))
                        hT_lo(TURNS - 1)
                    if (s + 1) % KT == 0:
                        c = s // KT
                        dve.wait_ge(tile_used, i * (2 * KT) + (T_E + s + 2))
                        dve.wait_ge(s_xr[c], i * 16 + 16)
                        dve.wait_ge(s_out[c], i * 16 + 16)
                        V.tensor_tensor(stage[:, c], acc[c][:], xr[:, c], ALU.add).then_inc(summed[c], 1)

            turn_E(0, True, False)
            with dve.Fori(1, 3) as i:
                turn_E(i, False, False)
            turn_E(3, False, True)

        @block.gpsimd
        def _(pool):
            G = nc.gpsimd
            for at, n, g in ((0, KD, w_norm), (KD, KQ, g_q_latent), (KD + KQ, KKV, g_kv_latent)):
                pool.dma_start(graw[at:at + n, :], g.rearrange("(k p) -> k p", p=P)).then_inc(s_gain, 16)
            pool.wait_ge(dve_done, D0.after("sumx"))
            pool.dma_start(alg[:, 0, :], a_log.partition_broadcast(P)).then_inc(s_row, 16)
            pool.dma_start(alg[:, 1, :], dt_bias.partition_broadcast(P)).then_inc(s_row, 16)
            with nc.allow_non_contiguous_dma(reason="256 positions"):
                pool.dma_start(pos_i[:], positions.rearrange("a (t p) -> p (a t)", p=P)).then_inc(s_row, 16)
            G.memset(zrow[:], 0.0).then_inc(pool_done, G1.one("zero"))
            pool.wait_ge(pool_done, G1.after("zero"))
            pool.dma_start(g_d[0:TAPS - 1, :].rearrange("a (b n) -> (a b) n", n=256), zrow[:]).then_inc(s_zero, 16)
            for q in stored:
                pool.wait_ge(q, 16 * 10)
            pool.wait_ge(s_zero, 16)
            with pool.Fori(0, 2) as i:
                for chunk in range(6):
                    group, n = chunk // 3, chunk % 3
                    col = i * (2 * COLS) + (group * COLS + n * W)

                    def done(name):
                        return GB.after(name, i * 6 + chunk)
                    pool.wait_ge(stored[chunk % 2], i * 48 + 16 * (11 + chunk // 2))
                    if chunk:
                        pool.wait_ge(s_conv, i * 192 + 32 * chunk)
                    for j in range(TAPS):
                        pool.dma_start(xs[:, j], tok(g_d[j:j + S, :])[:, :, bass.ds(col, COLS)]).then_inc(s_tap, 16)
                    pool.dma_start(cw[:], conv_w[:, bass.ds(col, COLS)].partition_broadcast(P)).then_inc(s_tap, 16)
                    pool.wait_ge(s_tap, i * (6 * 16 * (TAPS + 1)) + (chunk + 1) * 16 * (TAPS + 1))
                    for j in range(TAPS):
                        G.tensor_tensor(xs[:, j], xs[:, j], cw[:, j:j + 1, :].to_broadcast([P, TB, COLS]),
                                        ALU.mult).then_inc(pool_done, GB.one(f"m{j}"))
                    for j in range(1, TAPS):
                        pool.wait_ge(pool_done, done("m3" if j == 1 else f"a{j - 1}"))
                        G.tensor_tensor(xs[:, 0], xs[:, 0], xs[:, j], ALU.add).then_inc(pool_done, GB.one(f"a{j}"))
                    pool.wait_ge(pool_done, done("a3"))
                    for tb in range(TB):
                        pool.dma_start(conv_d[tb * P:(tb + 1) * P, bass.ds(i * 8 + group * 4, 4), n, :],
                                       xs[:, 0, tb, :].rearrange("p (h n) -> p h n", n=DV)).then_inc(s_conv, 16)
                pool.wait_ge(s_conv, i * 192 + 192)
            for q in s_mix[0:2]:
                pool.wait_ge(q, 16 * (TURNS + 1))
            pool.dma_start(oT[0][:].bitcast(F32), mix_d[0][:]).then_inc(s_mla[0], 16)
            with pool.Fori(0, TURNS) as i:
                def of_pair(a):
                    return a[:, bass.ds(i * 2, 2), :].rearrange("p h t -> p (h t)").unsqueeze(2).to_broadcast([P, 2 * TB, DV])
                pool.wait_ge(s_gcb, i * 16 + 16)
                pool.wait_ge(pe_done, PC.after("out1", i - 1))
                G.tensor_tensor(dec[:], rowb[:, 0], of_pair(gc), ALU.subtract).then_inc(pool_done, GC.one("diff"))
                pool.wait_ge(pool_done, GC.after("diff", i))
                G.tensor_tensor(dec[:], dec[:], causal.unsqueeze(1).to_broadcast([P, 2 * TB, P]), ALU.mult).then_inc(pool_done, GC.one("below"))
                pool.wait_ge(act_done, AC.after("silu", i))
                G.tensor_tensor(tt[:], sl[:, :, 0:2, :], sl[:, :, 0:2, :], ALU.mult).then_inc(pool_done, GC.one("square"))
                pool.wait_ge(act_done, AC.after("exp", i))
                G.tensor_tensor(dec[:], dec[:], causal.unsqueeze(1).to_broadcast([P, 2 * TB, P]), ALU.mult).then_inc(pool_done, GC.one("mask"))
                pool.wait_ge(pool_done, GC.after("mask", i))
                G.tensor_tensor(lt[:], dec[:], rowb[:, 1], ALU.mult).then_inc(pool_done, GC.one("decb"))
                G.tensor_tensor(sl[:, :, 2, :], sl[:, :, 2, :], of_pair(beta), ALU.mult).then_inc(pool_done, GC.one("vb"))
                pool.wait_ge(dve_done, DC.after("kn", i))
                G.tensor_tensor(kd[:], sl[:, :, 1, :], of_pair(ekd), ALU.mult).then_inc(pool_done, GC.one("kd"))
                pool.wait_ge(s_zg, i * 32 + 32)
                pool.wait_ge(s_bc, 48)
                G.tensor_tensor(sl[:, :, 3, :], sl[:, :, 3, :], ggo[:].unsqueeze(1).to_broadcast([P, 2 * TB, DV]),
                                ALU.mult).then_inc(pool_done, GC.one("gz"))
            pool.wait_ge(pe_done, PC.after("products", TURNS - 1))
            pool.wait_ge(dve_done, DC.after("qT", TURNS - 1))
            pool.wait_ge(pool_done, GC.after("decb", TURNS - 1))
            pool.dma_start(oT[1][:].bitcast(F32), mix_d[1][:]).then_inc(s_mla[1], 16)
            for q in s_mix:
                pool.wait_ge(q, 16 * (TURNS + 1))
            pool.wait_ge(pe_done, PC.after("turn", TURNS - 1))
            pool.wait_ge(gated[1], TURNS + 1)

            def load_gdn(n):
                heads = slice(n * H // PIECES, (n + 1) * H // PIECES)
                for j in range(2):
                    pool.dma_start(oT[2 + j][:, heads, :].bitcast(F32), mix_d[2 + j][:, heads, :]).then_inc(s_gdn[n], 16)

            def load_gate(i, c):
                pool.dma_start(stage[:, c], tok(gate_d)[:, :, bass.ds(i * COLS + c * D, COLS)]).then_inc(s_gate[c], 16)

            load_gdn(0)
            for q in stored:
                pool.wait_ge(q, 16 * 26)
            load_gate(0, 0)
            for n in range(1, PIECES):
                pool.wait_ge(tile_used, T_D + 3 * n)
                load_gdn(n)
            load_gate(0, 1)
            with pool.Fori(1, TURNS) as i:
                for c in range(2):
                    pool.wait_ge(gated[c], i + (TURNS + 1))
                    pool.wait_ge(dve_done, DD.after("h3", i - 1))
                    load_gate(i, c)
            pool.wait_ge(tile_used, T_E + 1)
            with pool.Fori(0, 4) as i:
                for c in range(2):
                    pool.wait_ge(summed[c], i + 1)
                    pool.dma_start(xr[:, c], tok(xf)[:, :, bass.ds(i * (2 * COLS) + c * COLS, COLS)]).then_inc(s_xr[c], 16)


_INS = ["x", "positions", "w_norm", "w_in", "b_gate", "w_q_up", "w_kv_up", "g_q_latent", "g_kv_latent", "g_q_head",
        "g_k_head", "w_o_mla", "conv_w", "a_log", "dt_bias", "g_gdn_out", "w_o_gdn", "w_out"]


def kernel(**inputs):
    import numpy as _np
    import concourse.bacc as _bacc
    from concourse import mybir as _mybir
    from concourse.bass_utils import run_bass_kernel_spmd as _run

    nc = _bacc.Bacc("TRN2", target_bir_lowering=False, num_devices=1)
    arrays, args = {}, []
    for name in _INS + ["consts"]:
        a = shape_constants() if name == "consts" else _np.ascontiguousarray(inputs[name])
        arrays[f"in_{name}_dram"] = a
        args.append(nc.dram_tensor(f"in_{name}_dram", a.shape, _mybir.dt.from_np(a.dtype), kind="ExternalInput").ap())
    args.append(nc.dram_tensor("out_dram", inputs["x"].shape, _mybir.dt.float32, kind="ExternalOutput").ap())
    hybrid_block(nc, *args)
    r = _run(nc, [arrays], core_ids=[0])
    return r.results[0]["out_dram"]
```
